# Optimizing a Trainium2 kernel written in Bass

```python
import math
import jax
import jax.numpy as jnp
from jax import lax
import numpy as np
import jax, jax.numpy as jnp

D_MODEL = 1024
BATCH = 1
SEQ = 256
DEPTH = 1

CHUNK = 64
EPS = 1e-6

A_HEADS = 8
A_DK = 128
A_DV = 128
A_QK = A_HEADS * A_DK
A_V = A_HEADS * A_DV
CONV_W = 4
CONV_CH = 2 * A_QK + A_V

B_HEADS = 8
B_DK = 128
B_DV = 128
B_K = B_HEADS * B_DK
B_V = B_HEADS * B_DV

IN_SPLITS = (A_QK, A_QK, A_V, A_HEADS, A_HEADS, A_V, B_K, B_V, B_K, B_V, D_MODEL, D_MODEL)
IN_WIDTH = 3 * A_QK + 2 * A_V + 2 * A_HEADS + 2 * B_K + 2 * B_V + 2 * D_MODEL

N_KEYS = 128
N_EXPERTS = N_KEYS * N_KEYS
P_HEADS = 8
P_DKEY = 256
P_DHALF = P_DKEY // 2
P_TOPK = 16
P_TOKEN_BLOCK = 128


def _rmsnorm(x, g):
    xf = x.astype(jnp.float32)
    y = xf * lax.rsqrt(jnp.mean(xf * xf, axis=-1, keepdims=True) + EPS) * g.astype(jnp.float32)
    return y.astype(x.dtype)

def _l2norm(x):
    return x * lax.rsqrt(jnp.sum(x * x, axis=-1, keepdims=True) + EPS)

def _split_cols(p):
    outs = []
    off = 0
    for w in IN_SPLITS:
        outs.append(p[..., off:off + w])
        off += w
    return outs

def _causal_conv_silu(x, w):
    k_w = w.shape[0]
    t = x.shape[1]
    xp = jnp.pad(x, ((0, 0), (k_w - 1, 0), (0, 0)))
    y = sum(xp[:, j:j + t] * w[j] for j in range(k_w))
    return jax.nn.silu(y)

def _to_chunks(x):
    b, t, h, d = x.shape
    return x.reshape(b, t // CHUNK, CHUNK, h, d).transpose(1, 0, 3, 2, 4)

def _to_chunks_s(x):
    b, t, h = x.shape
    return x.reshape(b, t // CHUNK, CHUNK, h).transpose(1, 0, 3, 2)

def _from_chunks(o):
    n, b, h, c, d = o.shape
    return o.transpose(1, 0, 3, 2, 4).reshape(b, n * c, h, d)

def _gated_delta_rule(q, k, v, beta, g):
    dk = q.shape[-1]
    dv = v.shape[-1]
    q = _l2norm(q) * (dk ** -0.5)
    k = _l2norm(k)
    qc, kc, vc = _to_chunks(q), _to_chunks(k), _to_chunks(v)
    bc = _to_chunks_s(beta)
    G = jnp.cumsum(_to_chunks_s(g), axis=-1)
    causal = jnp.tril(jnp.ones((CHUNK, CHUNK), dtype=bool))
    diff = G[..., :, None] - G[..., None, :]
    decay = jnp.where(causal, jnp.exp(jnp.where(causal, diff, 0.0)), 0.0)
    kb = kc * bc[..., None]
    a_kk = jnp.einsum('nbhid,nbhjd->nbhij', kb, kc) * decay
    lhs = jnp.eye(CHUNK, dtype=jnp.float32) + jnp.tril(a_kk, -1)
    rhs = jnp.concatenate([vc * bc[..., None], kb * jnp.exp(G)[..., None]], axis=-1)
    sol = lax.linalg.triangular_solve(lhs, rhs, left_side=True, lower=True, unit_diagonal=True)
    u, w = sol[..., :dv], sol[..., dv:]
    a_qk = jnp.einsum('nbhid,nbhjd->nbhij', qc, kc) * decay
    q_dec = qc * jnp.exp(G)[..., None]
    k_dec = kc * jnp.exp(G[..., -1:] - G)[..., None]
    g_last = jnp.exp(G[..., -1])

    def step(S, inp):
        u_n, w_n, aqk_n, qd_n, kd_n, gl_n = inp
        v_new = u_n - jnp.einsum('bhcd,bhde->bhce', w_n, S)
        o = jnp.einsum('bhcd,bhde->bhce', qd_n, S) + jnp.einsum('bhij,bhje->bhie', aqk_n, v_new)
        S = S * gl_n[..., None, None] + jnp.einsum('bhcd,bhce->bhde', kd_n, v_new)
        return S, o

    s0 = jnp.zeros((q.shape[0], q.shape[2], dk, dv), jnp.float32)
    _, o = lax.scan(step, s0, (u, w, a_qk, q_dec, k_dec, g_last))
    return _from_chunks(o)

def _hgrn2_recurrence(q, k, v, log_f):
    dk = q.shape[-1]
    dv = v.shape[-1]
    qc, kc, vc = _to_chunks(q), _to_chunks(k), _to_chunks(v)
    bc = jnp.cumsum(_to_chunks(log_f), axis=-2)
    causal3 = jnp.tril(jnp.ones((CHUNK, CHUNK), dtype=bool))[:, :, None]

    def step(S, inp):
        q_n, k_n, v_n, b_n = inp
        diff = b_n[..., :, None, :] - b_n[..., None, :, :]
        dec = jnp.where(causal3, jnp.exp(jnp.where(causal3, diff, 0.0)), 0.0)
        a = jnp.einsum('bhid,bhjd,bhijd->bhij', q_n, k_n, dec)
        o = jnp.einsum('bhid,bhde->bhie', q_n * jnp.exp(b_n), S) + jnp.einsum('bhij,bhje->bhie', a, v_n)
        b_last = b_n[..., -1:, :]
        S = S * jnp.exp(b_last)[..., 0, :, None] + jnp.einsum('bhjd,bhje->bhde', k_n * jnp.exp(b_last - b_n), v_n)
        return S, o

    s0 = jnp.zeros((q.shape[0], q.shape[2], dk, dv), jnp.float32)
    _, o = lax.scan(step, s0, (qc, kc, vc, bc))
    return _from_chunks(o)

def _peer(x, w_pq, sub_keys, expert_u, expert_v):
    b, t, d = x.shape
    n_tok = b * t
    xf = x.reshape(n_tok, d)
    q = (xf @ w_pq).reshape(n_tok, P_HEADS, 2, P_DHALF)
    s = jnp.einsum('thpd,phkd->thpk', q, sub_keys)
    top_s, top_i = lax.top_k(s, P_TOPK)
    cand_s = (top_s[:, :, 0, :, None] + top_s[:, :, 1, None, :]).reshape(n_tok, P_HEADS, P_TOPK * P_TOPK)
    cand_i = (top_i[:, :, 0, :, None] * N_KEYS + top_i[:, :, 1, None, :]).reshape(n_tok, P_HEADS, P_TOPK * P_TOPK)
    best_s, pos = lax.top_k(cand_s, P_TOPK)
    idx = jnp.take_along_axis(cand_i, pos, axis=-1)
    gate = jax.nn.softmax(best_s.astype(jnp.float32), axis=-1).astype(x.dtype)
    n_blk = n_tok // P_TOKEN_BLOCK
    xb = xf.reshape(n_blk, P_TOKEN_BLOCK, d)
    ib = idx.reshape(n_blk, P_TOKEN_BLOCK, P_HEADS * P_TOPK)
    gb = gate.reshape(n_blk, P_TOKEN_BLOCK, P_HEADS * P_TOPK)

    def block(args):
        xt, it, gt = args
        u = expert_u[it]
        h = jax.nn.gelu(jnp.einsum('td,tkd->tk', xt, u), approximate=False)
        v = expert_v[it]
        return jnp.einsum('tk,tkd->td', gt * h, v)

    y = lax.map(block, (xb, ib, gb))
    return y.reshape(b, t, d)

def first_inputs(seed: int = 0) -> dict:
    key = jax.random.key(seed)
    ks = jax.random.split(key, 20)

    def nrm(k, shape, scale):
        return jax.random.normal(k, shape, jnp.float32) * scale

    x = nrm(ks[0], (BATCH, SEQ, D_MODEL), 1.0)
    norm1 = 1.0 + nrm(ks[1], (DEPTH, D_MODEL), 0.02)
    w_in = nrm(ks[2], (DEPTH, D_MODEL, IN_WIDTH), D_MODEL ** -0.5)
    conv_a = nrm(ks[3], (DEPTH, CONV_W, CONV_CH), CONV_W ** -0.5)
    a_log = jnp.log(jax.random.uniform(ks[4], (DEPTH, A_HEADS), jnp.float32, 1.0, 16.0))
    dt = jnp.exp(jax.random.uniform(ks[5], (DEPTH, A_HEADS), jnp.float32, math.log(1e-3), math.log(1e-1)))
    dt_bias = dt + jnp.log(-jnp.expm1(-dt))
    a_onorm = 1.0 + nrm(ks[6], (DEPTH, A_DV), 0.02)
    b_lower_bound = 1.0 + nrm(ks[7], (DEPTH + 1, B_K), 0.1)
    b_onorm = 1.0 + nrm(ks[8], (DEPTH, B_DV), 0.02)
    w_branch_a = nrm(ks[9], (DEPTH, A_V, D_MODEL), A_V ** -0.5)
    w_branch_b = nrm(ks[10], (DEPTH, B_V, D_MODEL), B_V ** -0.5)
    w_out = nrm(ks[11], (DEPTH, D_MODEL, D_MODEL), D_MODEL ** -0.5)
    norm2 = 1.0 + nrm(ks[12], (DEPTH, D_MODEL), 0.02)
    w_pq = nrm(ks[13], (DEPTH, D_MODEL, P_HEADS * P_DKEY), D_MODEL ** -0.5)
    sub_keys = nrm(ks[14], (DEPTH, 2, P_HEADS, N_KEYS, P_DHALF), P_DHALF ** -0.5)
    expert_u = nrm(ks[15], (DEPTH, N_EXPERTS, D_MODEL), D_MODEL ** -0.5)
    expert_v = nrm(ks[16], (DEPTH, N_EXPERTS, D_MODEL), P_HEADS ** -0.5)
    final_norm = 1.0 + nrm(ks[17], (D_MODEL,), 0.02)
    return {'x': x, 'norm1': norm1, 'w_in': w_in, 'conv_a': conv_a, 'a_log': a_log,
            'dt_bias': dt_bias, 'a_onorm': a_onorm, 'b_lower_bound': b_lower_bound,
            'b_onorm': b_onorm, 'w_branch_a': w_branch_a, 'w_branch_b': w_branch_b,
            'w_out': w_out, 'norm2': norm2, 'w_pq': w_pq, 'sub_keys': sub_keys,
            'expert_u': expert_u, 'expert_v': expert_v, 'final_norm': final_norm}

def first_block(x, norm1, w_in, conv_a, a_log, dt_bias, a_onorm, b_lower_bound, b_onorm,
              w_branch_a, w_branch_b, w_out, norm2, w_pq, sub_keys, expert_u, expert_v,
              final_norm):
    dt = x.dtype
    bsz, t, _ = x.shape
    f32 = jnp.float32
    lower_bounds = jnp.cumsum(jax.nn.softmax(b_lower_bound.astype(f32), axis=0), axis=0)
    for l in range(DEPTH):
        h = _rmsnorm(x, norm1[l])
        proj = h @ w_in[l]
        a_q, a_k, a_v, a_beta, a_alpha, a_gate, b_f, b_i, b_q, b_gate, g_a, g_b = _split_cols(proj)

        qkv = _causal_conv_silu(jnp.concatenate([a_q, a_k, a_v], axis=-1), conv_a[l]).astype(f32)
        qa = qkv[..., :A_QK].reshape(bsz, t, A_HEADS, A_DK)
        ka = qkv[..., A_QK:2 * A_QK].reshape(bsz, t, A_HEADS, A_DK)
        va = qkv[..., 2 * A_QK:].reshape(bsz, t, A_HEADS, A_DV)
        beta = jax.nn.sigmoid(a_beta.astype(f32))
        log_alpha = -jnp.exp(a_log[l].astype(f32)) * jax.nn.softplus(a_alpha.astype(f32) + dt_bias[l].astype(f32))
        o_a = _gated_delta_rule(qa, ka, va, beta, log_alpha)
        o_a = _rmsnorm(o_a, a_onorm[l]) * jax.nn.silu(a_gate.astype(f32)).reshape(bsz, t, A_HEADS, A_DV)
        y_a = o_a.reshape(bsz, t, A_V).astype(dt) @ w_branch_a[l]

        lb = lower_bounds[l].reshape(B_HEADS, B_DK)
        f_gate = lb + (1.0 - lb) * jax.nn.sigmoid(b_f.astype(f32).reshape(bsz, t, B_HEADS, B_DK))
        qb = jax.nn.silu(b_q.astype(f32)).reshape(bsz, t, B_HEADS, B_DK)
        ib = b_i.astype(f32).reshape(bsz, t, B_HEADS, B_DV)
        o_b = _hgrn2_recurrence(qb, 1.0 - f_gate, ib, jnp.log(f_gate))
        o_b = _rmsnorm(o_b, b_onorm[l]) * jax.nn.sigmoid(b_gate.astype(f32)).reshape(bsz, t, B_HEADS, B_DV)
        y_b = o_b.reshape(bsz, t, B_V).astype(dt) @ w_branch_b[l]

        mix = jax.nn.sigmoid(g_a) * y_a + jax.nn.sigmoid(g_b) * y_b
        x = x + mix @ w_out[l]

        h2 = _rmsnorm(x, norm2[l])
        x = x + _peer(h2, w_pq[l], sub_keys[l], expert_u[l], expert_v[l])
    return _rmsnorm(x, final_norm)


DEPTH_2 = 2

N_MIXERS = 2
N_POOL_LAYERS = (DEPTH_2 + 1) // 2
N_ATTN_LAYERS = DEPTH_2 // 2
ALPHA = (2.0 * DEPTH_2) ** 0.25
BETA = (8.0 * DEPTH_2) ** -0.25
LN_EPS = 1e-5
POOL_WINDOWS = (2, 4, 8, 16)
N_GROUPS = len(POOL_WINDOWS)
GROUP_W = D_MODEL // N_GROUPS
HEAD_DIM = 64
N_HEADS = D_MODEL // (2 * HEAD_DIM)
V_DIM = 2 * HEAD_DIM
D_ATTN = N_HEADS * V_DIM
Q_BLOCK = 128
NUM_BUCKETS = 32
MAX_EXACT = NUM_BUCKETS // 2
MAX_DISTANCE = 128
D_FF = ((int(math.ceil(8 * D_MODEL / 3)) + 255) // 256) * 256


def _layernorm(x, g, b):
    xf = x.astype(jnp.float32)
    mu = jnp.mean(xf, axis=-1, keepdims=True)
    var = jnp.mean(jnp.square(xf - mu), axis=-1, keepdims=True)
    y = (xf - mu) * lax.rsqrt(var + LN_EPS)
    return (y * g.astype(jnp.float32) + b.astype(jnp.float32)).astype(x.dtype)

def _multiscale_pool(x, w, scale):
    B, S, D = x.shape
    xg = x.astype(jnp.float32).reshape(B, S, N_GROUPS, GROUP_W)
    cs = jnp.pad(jnp.cumsum(xg, axis=1), ((0, 0), (1, 0), (0, 0), (0, 0)))
    t = jnp.arange(S)
    pooled = []
    for g, win in enumerate(POOL_WINDOWS):
        hi = cs[:, 1:, g]
        lo = jnp.pad(cs[:, :S + 1 - win, g], ((0, 0), (win - 1, 0), (0, 0)))
        cnt = jnp.minimum(t + 1, win).astype(jnp.float32)[None, :, None]
        pooled.append((hi - lo) / cnt)
    pooled = jnp.stack(pooled, axis=2)
    mixed = jnp.einsum('bsgc,gcd->bsgd', pooled - xg, w.astype(jnp.float32))
    return (mixed.reshape(B, S, D) * scale.astype(jnp.float32)).astype(x.dtype)

def _rel_bucket(rel):
    n = jnp.maximum(rel, 0)
    is_small = n < MAX_EXACT
    nf = jnp.maximum(n, 1).astype(jnp.float32)
    large = MAX_EXACT + (jnp.log(nf / MAX_EXACT) / math.log(MAX_DISTANCE / MAX_EXACT)
                         * (NUM_BUCKETS - MAX_EXACT)).astype(jnp.int32)
    large = jnp.minimum(large, NUM_BUCKETS - 1)
    return jnp.where(is_small, n, large)

def _diff_attention(x, w_qkv, w_o, lam_p, subln_g, rel_table, lambda_init):
    B, S, D = x.shape
    qkv = x @ w_qkv
    q, k, v = jnp.split(qkv, 3, axis=-1)
    q = q.reshape(B, S, N_HEADS, 2, HEAD_DIM).transpose(0, 2, 3, 1, 4)
    k = k.reshape(B, S, N_HEADS, 2, HEAD_DIM).transpose(0, 2, 3, 1, 4)
    v = v.reshape(B, S, N_HEADS, V_DIM).transpose(0, 2, 1, 3)
    lp = lam_p.astype(jnp.float32)
    lam = (jnp.exp(jnp.sum(lp[0] * lp[1])) - jnp.exp(jnp.sum(lp[2] * lp[3])) + lambda_init)
    sm_scale = HEAD_DIM ** -0.5
    outs = []
    for qb in range(S // Q_BLOCK):
        q0 = qb * Q_BLOCK
        kend = q0 + Q_BLOCK
        s = jnp.einsum('bhcqd,bhckd->bhcqk', q[:, :, :, q0:kend], k[:, :, :, :kend]).astype(jnp.float32) * sm_scale
        rel = (q0 + jnp.arange(Q_BLOCK))[:, None] - jnp.arange(kend)[None, :]
        bias = rel_table[_rel_bucket(rel)].astype(jnp.float32).transpose(2, 0, 1)
        s = jnp.where(rel >= 0, s + bias[None, :, None], -jnp.inf)
        p = jax.nn.softmax(s, axis=-1)
        a = p[:, :, 0] - lam * p[:, :, 1]
        outs.append(jnp.einsum('bhqk,bhkv->bhqv', a.astype(v.dtype), v[:, :, :kend]))
    o = jnp.concatenate(outs, axis=2).astype(jnp.float32)
    o = o * lax.rsqrt(jnp.mean(jnp.square(o), axis=-1, keepdims=True) + LN_EPS)
    o = o * subln_g.astype(jnp.float32) * (1.0 - lambda_init)
    o = o.transpose(0, 2, 1, 3).reshape(B, S, D_ATTN).astype(x.dtype)
    return o @ w_o

def _swiglu(x, w_gate, w_up, w_down):
    return (jax.nn.silu(x @ w_gate) * (x @ w_up)) @ w_down

def second_inputs(seed: int = 0) -> dict:
    key = jax.random.key(seed)
    ks = jax.random.split(key, 20)
    f32 = jnp.float32
    nrm = lambda k, s: jax.random.normal(k, s, f32)
    x = nrm(ks[0], (BATCH, SEQ, D_MODEL))
    pool_w = nrm(ks[1], (N_POOL_LAYERS, N_GROUPS, GROUP_W, GROUP_W)) * (GROUP_W ** -0.5) * BETA
    pool_scale = 1.0 + 0.02 * nrm(ks[2], (N_POOL_LAYERS, D_MODEL))
    w_qk = nrm(ks[3], (N_ATTN_LAYERS, D_MODEL, 2 * D_ATTN)) * (D_MODEL ** -0.5)
    w_v = nrm(ks[4], (N_ATTN_LAYERS, D_MODEL, D_ATTN)) * (D_MODEL ** -0.5) * BETA
    w_qkv = jnp.concatenate([w_qk, w_v], axis=-1)
    w_o = nrm(ks[5], (N_ATTN_LAYERS, D_ATTN, D_MODEL)) * (D_ATTN ** -0.5) * BETA
    lam_p = 0.1 * nrm(ks[6], (N_ATTN_LAYERS, 4, HEAD_DIM))
    subln_g = 1.0 + 0.02 * nrm(ks[7], (N_ATTN_LAYERS, V_DIM))
    rel_table = 0.5 * nrm(ks[8], (NUM_BUCKETS, N_HEADS))
    w_gate = nrm(ks[9], (DEPTH_2, D_MODEL, D_FF)) * (D_MODEL ** -0.5) * BETA
    w_up = nrm(ks[10], (DEPTH_2, D_MODEL, D_FF)) * (D_MODEL ** -0.5) * BETA
    w_down = nrm(ks[11], (DEPTH_2, D_FF, D_MODEL)) * (D_FF ** -0.5) * BETA
    ln_mix_g = 1.0 + 0.02 * nrm(ks[12], (DEPTH_2, D_MODEL))
    ln_mix_b = 0.02 * nrm(ks[13], (DEPTH_2, D_MODEL))
    ln_ffn_g = 1.0 + 0.02 * nrm(ks[14], (DEPTH_2, D_MODEL))
    ln_ffn_b = 0.02 * nrm(ks[15], (DEPTH_2, D_MODEL))
    return {"x": x, "pool_w": pool_w, "pool_scale": pool_scale, "w_qkv": w_qkv, "w_o": w_o,
            "lam_p": lam_p, "subln_g": subln_g, "rel_table": rel_table, "w_gate": w_gate,
            "w_up": w_up, "w_down": w_down, "ln_mix_g": ln_mix_g, "ln_mix_b": ln_mix_b,
            "ln_ffn_g": ln_ffn_g, "ln_ffn_b": ln_ffn_b}

def second_block(x, pool_w, pool_scale, w_qkv, w_o, lam_p, subln_g, rel_table, w_gate,
              w_up, w_down, ln_mix_g, ln_mix_b, ln_ffn_g, ln_ffn_b):
    for i in range(DEPTH_2):
        j = i // N_MIXERS
        if i % N_MIXERS == 0:
            h = _multiscale_pool(x, pool_w[j], pool_scale[j])
        else:
            lambda_init = 0.8 - 0.6 * math.exp(-0.3 * i)
            h = _diff_attention(x, w_qkv[j], w_o[j], lam_p[j], subln_g[j], rel_table, lambda_init)
        x = _layernorm(ALPHA * x + h, ln_mix_g[i], ln_mix_b[i])
        x = _layernorm(ALPHA * x + _swiglu(x, w_gate[i], w_up[i], w_down[i]), ln_ffn_g[i], ln_ffn_b[i])
    return x


def setup_inputs(seed=0):
    out = dict(first_inputs(seed))
    for name, value in second_inputs(seed + 1).items():
        if name != "x":
            out[name + "_2"] = value
    return out


def reference(
    x, norm1, w_in, conv_a, a_log, dt_bias, a_onorm, b_lower_bound, b_onorm, w_branch_a,
    w_branch_b, w_out, norm2, w_pq, sub_keys, expert_u, expert_v, final_norm, pool_w_2,
    pool_scale_2, w_qkv_2, w_o_2, lam_p_2, subln_g_2, rel_table_2, w_gate_2, w_up_2, w_down_2,
    ln_mix_g_2, ln_mix_b_2, ln_ffn_g_2, ln_ffn_b_2,
):
    x = first_block(
        x, norm1, w_in, conv_a, a_log, dt_bias, a_onorm, b_lower_bound, b_onorm, w_branch_a,
        w_branch_b, w_out, norm2, w_pq, sub_keys, expert_u, expert_v, final_norm,
    )
    return second_block(
        x, pool_w_2, pool_scale_2, w_qkv_2, w_o_2, lam_p_2, subln_g_2, rel_table_2, w_gate_2,
        w_up_2, w_down_2, ln_mix_g_2, ln_mix_b_2, ln_ffn_g_2, ln_ffn_b_2,
    )


_drawn_inputs = setup_inputs


def setup_inputs(seed=0):
    import zlib

    import numpy as np

    out = dict(_drawn_inputs(seed))
    spreads = {}
    factors = {'a_onorm': 3.794,
     'b_lower_bound': 4.545,
     'b_onorm': 3.921,
     'final_norm': 2.739,
     'pool_scale_2': 8.0,
     'subln_g_2': 8.0}
    for name, (base, spread) in spreads.items():
        noise = np.random.default_rng([zlib.crc32(name.encode()), seed]).standard_normal(out[name].shape)
        drawn = base * np.exp(spread * noise) if base else spread * noise
        out[name] = jnp.asarray(drawn.astype(out[name].dtype))
    for name, factor in factors.items():
        out[name] = (out[name] * factor).astype(out[name].dtype)
    return out
```

```python
from contextlib import ExitStack

import numpy as np

import concourse.bass as bass
from concourse import mybir

F32 = mybir.dt.float32
I32 = mybir.dt.int32
U32 = mybir.dt.uint32
ALU = mybir.AluOpType
ACT = mybir.ActivationFunctionType
AX_X = mybir.AxisListType.X

P = 128
D = 1024
T = 256
TILES = T // P
KC = D // P
CHUNK = 64
HEADS = 8
DH = 128
EPS = 1e-6
CONV_W = 4
N_KEYS = 128
TOPK = 16
P_HEADS = 8
SLOTS = P_HEADS * TOPK
D_FF = 2816
FF_T = D_FF // P
LN_EPS = 1e-5
ALPHA = 4.0 ** 0.25
WINDOWS = (2, 4, 8, 16)
HEAD_DIM = 64
LAMBDA_INIT = 0.8 - 0.6 * float(np.exp(-0.3))
MASKED = -1e30
LOWEST = -3.0e38
MAIN = 35 * D
LEVELS = 6

PANEL = 4096
HALF = 512
FF_PANELS = FF_T // 2
DOWN_PANELS = -(-FF_T // 4)

WEIGHTS = [("conv", 6), ("a_gate", 2), ("b_f", 2), ("b_i", 2), ("b_q", 2), ("b_gate", 2), ("g_a", 2),
           ("g_b", 2), ("branch_a", 2), ("branch_b", 2), ("w_out", 2), ("w_pq", 4),
           ("ff0", FF_PANELS), ("down0", DOWN_PANELS), ("qk", 4), ("v", 2), ("w_o", 2),
           ("ff1", FF_PANELS), ("down1", DOWN_PANELS)]
BY_TILE = ("branch_a", "branch_b", "w_out", "w_pq")
_at = [x for x, _ in WEIGHTS].index(BY_TILE[0])
_one = WEIGHTS[_at:_at + len(BY_TILE)]
PLAN = (WEIGHTS[:_at] + [(f"{x}.{m}", n) for m in range(TILES) for x, n in _one]
        + WEIGHTS[_at + len(BY_TILE):])


def first_of(plan):
    first, total = {}, 0
    for name, n in plan:
        first[name] = total
        total += n
    return first, total


FIRST, N_PANELS = first_of(PLAN)
IN_WALL, WALL_PANELS = first_of(WEIGHTS)
COUNT = dict(PLAN)
WALL_AT = [IN_WALL[x.split(".")[0]] + q for x, n in PLAN for q in range(n)]
HALF_AT = {}
for _name, _n in PLAN:
    HALF_AT[_name] = sum(n for x, n in PLAN if FIRST[x] < FIRST[_name]
                         and not x.startswith("down") and "." not in x)
BESIDE = [(x, q, j) for x in ("b_f", "b_i", "b_q", "b_gate", "g_a", "g_b") for q in range(2) for j in range(2)]
BESIDE_DELTA = 16

MATS = (["ident", "upto", "after", "ones", "chunk0", "chunk1"]
        + [f"span{l}" for l in range(LEVELS)] + [f"level{l}" for l in range(LEVELS)])
MAT = {n: i for i, n in enumerate(MATS)}
ROWS = ["b_low0", "b_low1", "norm2", "final_norm", "pool_scale", "ln_mix_g0", "ln_mix_b0",
        "ln_ffn_g0", "ln_ffn_b0", "ln_mix_g1", "ln_mix_b1", "ln_ffn_g1", "ln_ffn_b1"]
ROW = {n: i for i, n in enumerate(ROWS)}


def constant_matrices():
    p, i = np.meshgrid(np.arange(P), np.arange(P), indexing="ij")
    same = p // CHUNK == i // CHUNK
    out = [p == i, same & (p <= i), same & (p > i), np.ones((P, P)), p < CHUNK, p >= CHUNK]
    spans, levels = [], []
    for l in range(LEVELS):
        s = 1 << l
        mid = i // (2 * s) * 2 * s + s
        right = i >= mid
        spans.append(np.where(right, (p >= mid) & (p <= i), (p > i) & (p < mid)))
        levels.append((p // (2 * s) == i // (2 * s)) & right & (p < mid))
    return np.stack([np.asarray(m, np.float32) for m in out + spans + levels], 1)


def pool_matrices():
    s, t = np.meshgrid(np.arange(T), np.arange(T), indexing="ij")
    groups = [((s <= t) & (s > t - w)) / np.minimum(t + 1, w) - (s == t) for w in WINDOWS]
    m = np.stack(groups, 1).astype(np.float32)
    return np.ascontiguousarray(m.reshape(TILES, P, len(WINDOWS), T).transpose(1, 0, 2, 3))


def rel_bucket(n):
    large = 16 + (np.log(np.maximum(n, 1) / 16) / np.log(8.0) * 16).astype(np.int64)
    return np.where(n < 16, n, np.minimum(large, 31))


PARTS = 10
GATE_A, Q_A, K_A, V_A, F_B, I_B, Q_B, GATE_B, MIX_A, MIX_B = range(PARTS)
SCRATCH = TILES * PARTS * D
STATE_A, STATE_B, KEPT_IN = 12, 13, 14
KEPT = SCRATCH + D * KEPT_IN
RING = 8
H2, DIAGS = MIX_A, MIX_B


class Signal:

    def __init__(self, ctx, nc, name):
        self.sem = ctx.enter_context(nc.semaphore(name))
        self.base = 0

    def count(self, n):
        return self.sem, self.base + n


class Chain:

    def __init__(self, ctx, nc, name):
        self.sem = ctx.enter_context(nc.semaphore(name))
        self.n, self.turn = 0, 0

    def next(self):
        self.n += 1
        return self.sem

    def made(self, behind=0):
        return self.sem, self.turn + (self.n - behind)

    def begin(self, i, per_turn):
        self.start, self.per = self.n, per_turn
        self.turn = i * per_turn

    def end(self, turns):
        assert self.n - self.start == self.per, (self.n - self.start, self.per)
        self.turn = 0
        self.n = self.start + self.per * turns


def pairs(eng, n, body):
    if n // 2 > 1:
        with eng.Fori(0, n // 2) as i:
            body(i, 0)
            body(i, 1)
    else:
        for i in range(n // 2):
            body(i, 0)
            body(i, 1)
    if n % 2:
        body(n // 2, 0)


def spread(ap, n):
    return ap.unsqueeze(1).broadcast_to([ap.shape[0], n, ap.shape[1]])


def along(ap, n):
    return ap.unsqueeze(2).broadcast_to([ap.shape[0], ap.shape[1], n])


class Core:

    def __init__(self, nc, ctx, dram):
        self.nc, self.dram = nc, dram
        self.sb = lambda name, shape, dt=F32: ctx.enter_context(nc.sbuf_tensor(name, shape, dt))
        self.panels = self.sb("panels", [P, 2, PANEL])
        self.mats = self.sb("mats", [P, len(MATS), P])
        self.masks = self.sb("masks", [P, LEVELS, P], I32)
        self.x = self.sb("x", [P, TILES, D])
        self.xT = self.sb("xT", [P, KC, T])
        self.main = self.sb("main", [P, MAIN])
        self.small = self.sb("small", [P, 768])
        self.onorm = self.sb("onorm", [P, 3, DH])
        self.ps = ctx.enter_context(nc.psum_tensor("ps", [P, 8, HALF], F32))
        sig = lambda name: Signal(ctx, nc, name)
        self.panel_loaded = [sig("panel_loaded0"), sig("panel_loaded1")]
        self.half_done = sig("half_done")
        self.panel_done = sig("panel_done")
        self.bank_read = [sig(f"bank_read{b}") for b in range(4)]
        self.bank_uses = [1] * 4
        self.pair_full = [sig("pair_full0"), sig("pair_full1")]
        self.pair_read = [sig("pair_read0"), sig("pair_read1")]
        for p in self.pair_read:
            p.base = 1
        self.turned = sig("turned")
        self.loaded = sig("loaded")
        self.stored = sig("stored")
        self.named, self.raised = {}, {}
        self.act_chain = Chain(ctx, nc, "act_chain")
        self.dve_chain = Chain(ctx, nc, "dve_chain")
        self.w_bt = self.sb("w_bt", [P, KC, 16])
        self.w_conv = self.sb("w_conv", [P, 3 * HEADS, CONV_W])
        self.bt = self.sb("bt", [P, 32])
        self.ctx = ctx

    def next(self, name):
        if name not in self.named:
            self.named[name] = Signal(self.ctx, self.nc, name)
        self.raised[name] = self.raised.get(name, 0) + 1
        return self.named[name].sem

    def count(self, name, n=1):
        if name not in self.named:
            self.named[name] = Signal(self.ctx, self.nc, name)
        return self.named[name].count(n)

    def end_stage(self):
        for name, n in self.raised.items():
            self.named[name].base += n
        self.raised = {}

    def mat(self, name):
        return self.mats[:, MAT[name], :]

    def area(self, at, *shape):
        n = int(np.prod(shape))
        v = self.main[:, at:at + n]
        if len(shape) == 2:
            return v.rearrange("p (a b) -> p a b", a=shape[0])
        if len(shape) == 3:
            return v.rearrange("p (a b c) -> p a b c", a=shape[0], b=shape[1])
        return v

    def part(self, m, n):
        return self.area(PARTS * D * m + D * n, HEADS, P)

    def row(self, m, n):
        return self.area(PARTS * D * m + D * n, D)

    def stream(self, sp, name):
        first, n = FIRST[name] + 2, min(COUNT[name], N_PANELS - FIRST[name] - 2)
        wall = self.dram["wall"]
        at = WALL_AT[first:first + max(n, 0)]
        if n // 2 > 1 and at == list(range(at[0], at[0] + n)):
            pair = wall[at[0]:at[0] + n // 2 * 2].rearrange("(g s) p n -> g s p n", s=2)
            with sp.Fori(0, n // 2) as i:
                for par in range(2):
                    slot = (first + par) % 2
                    sp.wait_ge(self.panel_done.sem, 2 * i + (first + par - 1))
                    sp.dma_start(self.panels[:, slot, :], pair[i, par])\
                      .then_inc(self.panel_loaded[slot].sem, 16)
            loaded = n // 2 * 2
        else:
            loaded = 0
        for q in range(loaded, n):
            slot = (first + q) % 2
            sp.wait_ge(self.panel_done.sem, first + q - 1)
            sp.dma_start(self.panels[:, slot, :], wall[at[q]]).then_inc(self.panel_loaded[slot].sem, 16)

    def wait_panel(self, pe, name, i, par):
        first = FIRST[name]
        slot = (first + par) % 2
        pe.wait_ge(self.panel_loaded[slot].sem, 16 * i + 16 * ((first + par) // 2 + 1))
        return slot

    def products(self, pe, name, actT, channel_major):
        first = FIRST[name]
        base = list(self.bank_uses)

        def body(i, par):
            slot = self.wait_panel(pe, name, i, par)
            w = self.panels[:, slot, :].rearrange("p (k n) -> p k n", k=KC)
            for j in range(2):
                bank = 2 * slot + j
                pe.wait_ge(self.bank_read[bank].sem, i + base[bank])
                if channel_major:
                    for t in range(2):
                        for k in range(KC):
                            c = (2 * j + t) * P
                            mm = pe.matmul(self.ps[:, bank, t * T:(t + 1) * T], w[:, k, c:c + P],
                                           actT[:, k, :], start=(k == 0), stop=(k == KC - 1))
                else:
                    for k in range(KC):
                        mm = pe.matmul(self.ps[:, bank, :], actT[:, k, j * P:(j + 1) * P],
                                       w[:, k, :], start=(k == 0), stop=(k == KC - 1))
                mm.then_inc((self.half_done if j == 0 else self.panel_done).sem, 1)

        pairs(pe, COUNT[name], body)
        self._used(name)

    def _used(self, name):
        first = FIRST[name]
        for q in range(COUNT[name]):
            for j in range(2):
                self.bank_uses[2 * ((first + q) % 2) + j] += 1

    def product_beside(self, pe, n):
        name, q, j = BESIDE[n]
        slot = self.wait_panel(pe, name, q // 2, q % 2)
        w = self.panels[:, slot, :].rearrange("p (k n) -> p k n", k=KC)
        bank = 2 * slot + j
        pe.wait_ge(self.bank_read[bank].sem, self.bank_uses[bank])
        self.bank_uses[bank] += 1
        if name == "b_q":
            for t in range(2):
                for k in range(KC):
                    at = (2 * j + t) * P
                    mm = pe.matmul(self.ps[:, bank, t * T:(t + 1) * T], w[:, k, at:at + P],
                                   self.xT[:, k, :], start=(k == 0), stop=(k == KC - 1))
        else:
            for k in range(KC):
                mm = pe.matmul(self.ps[:, bank, :], self.xT[:, k, j * P:(j + 1) * P],
                               w[:, k, :], start=(k == 0), stop=(k == KC - 1))
        mm.then_inc((self.half_done if j == 0 else self.panel_done).sem, 1)

    def read_beside(self, act, n):
        name, q, j = BESIDE[n]
        bank = 2 * ((FIRST[name] + q) % 2) + j
        done = self.half_done if j == 0 else self.panel_done
        act.wait_ge(done.sem, (HALF_AT[name] if j == 0 else FIRST[name]) + q + 1)
        if name == "b_q":
            for m in range(TILES):
                src = self.ps[:, bank, :].rearrange("p (k m t) -> p k m t", k=2, m=TILES)[:, :, m, :]
                ins = act.activation(self.part(m, Q_B)[:, 4 * q + 2 * j:4 * q + 2 * j + 2, :], src, ACT.Silu)
        else:
            at, func = {"b_f": (F_B, ACT.Sigmoid), "b_i": (I_B, ACT.Copy), "b_gate": (GATE_B, ACT.Sigmoid),
                        "g_a": (MIX_A, ACT.Sigmoid), "g_b": (MIX_B, ACT.Sigmoid)}[name]
            ins = act.activation(self.row(j, at)[:, q * HALF:(q + 1) * HALF], self.ps[:, bank, :], func)
        ins.then_inc(self.bank_read[bank].sem, 1)

    def products_of_tile(self, pe, name, actT, channel_major):
        for q in range(COUNT[name]):
            slot = self.wait_panel(pe, name, q // 2, q % 2)
            w = self.panels[:, slot, :].rearrange("p (k n) -> p k n", k=KC)
            bank = 2 * slot
            pe.wait_ge(self.bank_read[bank].sem, self.bank_uses[bank])
            self.bank_uses[bank] += 1
            if channel_major:
                for t in range(4):
                    for k in range(KC):
                        mm = pe.matmul(self.ps[:, bank, t * P:(t + 1) * P], w[:, k, t * P:(t + 1) * P],
                                       actT[:, k, :], start=(k == 0), stop=(k == KC - 1))
            else:
                for k in range(KC):
                    mm = pe.matmul(self.ps[:, bank, :], actT[:, k, :], w[:, k, :],
                                   start=(k == 0), stop=(k == KC - 1))
            mm.then_inc(self.panel_done.sem, 1)

    def evacuate(self, eng, name, read, halves=(0, 1)):
        first = FIRST[name]

        def body(i, par):
            slot = (first + par) % 2
            for j in halves:
                done = self.half_done if j == 0 else self.panel_done
                base = HALF_AT[name] if j == 0 else first
                eng.wait_ge(done.sem, 2 * i + (base + par + 1))
                read(i, par, j, 2 * slot + j).then_inc(self.bank_read[2 * slot + j].sem, 1)

        pairs(eng, COUNT[name], body)



def turn(c, pe, src, waits_for_bank=True):
    for n in range(4):
        if waits_for_bank:
            pe.wait_ge(c.bank_read[n].sem, c.bank_uses[n])
        c.bank_uses[n] += 1
        for k in range(2):
            for m in range(TILES):
                at = (2 * n + k) * P
                mm = pe.transpose(c.ps[:, n, k * T + m * P:k * T + (m + 1) * P],
                                  src[:, m, at:at + P], c.mat("ident"))
        mm.then_inc(c.turned.sem, 1)


def turn_tile(c, pe, src):
    for n in (0, 2):
        pe.wait_ge(c.bank_read[n].sem, c.bank_uses[n])
        c.bank_uses[n] += 1
        for k in range(4):
            at = (2 * n + k) * P
            mm = pe.transpose(c.ps[:, n, k * P:(k + 1) * P], src[:, at:at + P], c.mat("ident"))
        mm.then_inc(c.turned.sem, 1)


def read_turned_tile(c, act, dst, nth):
    for n in (0, 2):
        act.wait_ge(*c.turned.count(2 * nth + n // 2 + 1))
        act.activation(dst[:, 2 * n:2 * n + 4, :], c.ps[:, n, :].rearrange("p (k t) -> p k t", k=4),
                       ACT.Copy).then_inc(c.bank_read[n].sem, 1)


def wait_turned_tile_read(c, pe):
    for n in (0, 2):
        pe.wait_ge(c.bank_read[n].sem, c.bank_uses[n])


def read_turned(c, eng, dst, nth):
    for n in range(4):
        eng.wait_ge(*c.turned.count(4 * nth + n + 1))
        out = dst[:, 2 * n:2 * n + 2, :].rearrange("p k t -> p (k t)")
        eng.activation(out, c.ps[:, n, :], ACT.Copy).then_inc(c.bank_read[n].sem, 1)


def wait_turned_read(c, pe):
    for n in range(4):
        pe.wait_ge(c.bank_read[n].sem, c.bank_uses[n])


def load_row(c, eng, dst, name):
    eng.dma_start(dst, c.dram["rows"][ROW[name]]).then_inc(c.loaded.sem, 16)


def norm(c, kind, row_g, row_b=None, eps=EPS, store=None, turned=True, first=False, at=6 * D):
    nc = c.nc
    centred = c.area(8 * D, TILES, D)
    junk = c.area(10 * D, TILES, D)
    g, b = c.area(12 * D, D), c.area(13 * D, D)
    out = c.x if kind != "rms_beside" else c.area(at, TILES, D)
    stat = c.small[:, 0:16]
    layer = kind == "layer"
    src = centred if layer else c.x
    n_loads = 1 + layer + (6 if first else 0)
    with nc.Block() as block:
        @block.sync
        def _(sp):
            if first:
                for m in range(TILES):
                    sp.dma_start(c.x[:, m, :], c.dram["x"][m]).then_inc(c.loaded.sem, 16)
                sp.dma_start(c.mats[:, :, :], c.dram["mats"]).then_inc(c.loaded.sem, 16)
                sp.dma_start(c.masks[:, :, :], c.dram["masks"]).then_inc(c.loaded.sem, 16)
                sp.dma_start(c.onorm[:, :, :], c.dram["onorms"]).then_inc(c.loaded.sem, 16)
                sp.dma_start(g, c.dram["norm1"]).then_inc(c.loaded.sem, 16)
                sp.dma_start(c.w_bt[:, :, :], c.dram["w_bt"]).then_inc(c.loaded.sem, 16)
                for n in range(2):
                    sp.dma_start(c.panels[:, n, :], c.dram["wall"][n]).then_inc(c.panel_loaded[n].sem, 16)
            else:
                load_row(c, sp, g, row_g)
                if layer:
                    load_row(c, sp, b, row_b)
            if store is not None:
                for m in range(TILES):
                    sp.wait_ge(*c.count("normed", m + 1))
                    sp.dma_start(store[m], c.x[:, m, :]).then_inc(c.stored.sem, 16)
                sp.wait_ge(*c.stored.count(16 * TILES))

        @block.scalar
        def _(act):
            if first:
                for n in range(4):
                    act.sem_inc(c.bank_read[n].sem, 1)
                for n in range(2):
                    act.sem_inc(c.pair_read[n].sem, 1)
                act.wait_ge(*c.loaded.count(16 * n_loads))
            for m in range(TILES):
                if layer:
                    act.wait_ge(*c.count("centred", m + 1))
                act.activation(junk[:, m, :], src[:, m, :], ACT.Square,
                                               accum_out=stat[:, 4 + m:5 + m]).then_inc(c.next("square"), 1)
            act.wait_ge(*c.count("mean"))
            act.activation(stat[:, 8:10], stat[:, 6:8], ACT.Sqrt).then_inc(c.next("root"), 1)
            if turned:
                read_turned(c, act, c.xT, 0)

        @block.vector
        def _(dve):
            def step(ins):
                ins.then_inc(c.dve_chain.next(), 1)
                dve.wait_ge(*c.dve_chain.made())

            if layer:
                for m in range(TILES):
                    step(dve.reduce_sum(stat[:, m:m + 1], c.x[:, m, :], AX_X))
                    step(dve.tensor_scalar(stat[:, 2 + m:3 + m], stat[:, m:m + 1], -1.0 / D, None, ALU.mult))
                    dve.tensor_scalar(centred[:, m, :], c.x[:, m, :],
                                                      stat[:, 2 + m:3 + m], None, ALU.add).then_inc(c.next("centred"), 1)
            for m in range(TILES):
                dve.wait_ge(*c.count("square", m + 1))
            dve.tensor_scalar(stat[:, 6:8], stat[:, 4:6], 1.0 / D, eps,
                                              ALU.mult, ALU.add).then_inc(c.next("mean"), 1)
            dve.wait_ge(*c.count("root"))
            step(dve.reciprocal(stat[:, 10:12], stat[:, 8:10]))
            dve.wait_ge(*c.loaded.count(16 * n_loads))
            for m in range(TILES):
                if layer:
                    step(dve.scalar_tensor_tensor(out=centred[:, m, :], in0=centred[:, m, :],
                                                  scalar=stat[:, 10 + m:11 + m], in1=g,
                                                  op0=ALU.mult, op1=ALU.mult))
                    last = dve.tensor_tensor(out[:, m, :], centred[:, m, :], b, ALU.add)
                else:
                    last = dve.scalar_tensor_tensor(out=out[:, m, :], in0=c.x[:, m, :],
                                                    scalar=stat[:, 10 + m:11 + m], in1=g,
                                                    op0=ALU.mult, op1=ALU.mult)
                last.then_inc(c.next("normed"), 1)

        @block.tensor
        def _(pe):
            if turned:
                if first:
                    pe.wait_ge(*c.loaded.count(16 * n_loads))
                for m in range(TILES):
                    pe.wait_ge(*c.count("normed", m + 1))
                turn(c, pe, out)
    c.loaded.base += 16 * n_loads
    if store is not None:
        c.stored.base += 16 * TILES
    if turned:
        c.turned.base += 4
    c.end_stage()



def project(c):
    nc = c.nc
    raw = c.area(SCRATCH, 3 * HEADS, T + 4)
    main = c.main[:, 0:SCRATCH].rearrange("p (m n t) -> p m n t", m=TILES, t=P)
    pair = c.ps[:, 4, 0:32]
    read_base = list(c.bank_uses)
    with nc.Block() as block:
        @block.sync
        def _(sp):
            sp.dma_start(c.w_conv[:, :, :], c.dram["w_conv"]).then_inc(c.loaded.sem, 16)
            c.stream(sp, "conv")
            c.stream(sp, "a_gate")

        @block.tensor
        def _(pe):
            c.products(pe, "conv", c.xT, channel_major=True)
            for m in range(TILES):
                for k in range(KC):
                    mm = pe.matmul(pair[:, 16 * m:16 * m + 16], c.xT[:, k, m * P:(m + 1) * P],
                                   c.w_bt[:, k, :], start=(k == 0), stop=(k == KC - 1))
            mm.then_inc(c.next("bt_done"), 1)
            c.products(pe, "a_gate", c.xT, channel_major=False)

        @block.scalar
        def _(act):
            act.wait_ge(*c.count("zeros"))

            def read_conv(i, par, j, bank):
                return act.activation(raw[:, bass.ds(8 * i + 4 * par + 2 * j, 2), 3:3 + T],
                                      c.ps[:, bank, :].rearrange("p (k t) -> p k t", k=2), ACT.Copy)
            c.evacuate(act, "conv", read_conv)
            act.wait_ge(*c.count("bt_done"))
            act.activation(c.bt[:, :], pair, ACT.Copy).then_inc(c.next("bt"), 1)

            def read_gate(i, par, j, bank):
                q = 2 * i + par
                return act.activation(c.row(j, GATE_A)[:, q * HALF:(q + 1) * HALF], c.ps[:, bank, :], ACT.Silu)
            c.evacuate(act, "a_gate", read_gate)
            act.wait_ge(*c.count("conv"))
            for m in range(TILES):
                v = c.area(PARTS * D * m + D * Q_A, 3 * D)
                act.activation(v, v, ACT.Silu).then_inc(c.act_chain.next(), 1)

        @block.vector
        def _(dve):
            dve.memset(raw[:, :, 0:3], 0.0).then_inc(c.next("zeros"), 1)
            dve.wait_ge(*c.loaded.count(16))

            def conv(i, par):
                slot = (FIRST["conv"] + par) % 2
                for j in range(2):
                    bank = 2 * slot + j
                    dve.wait_ge(c.bank_read[bank].sem, i + (read_base[bank] + 1))
                    at = 8 * i + 4 * par + 2 * j
                    for tap in range(CONV_W):
                        for t in range(2):
                            w = c.w_conv[:, bass.ds(at + t, 1), tap:tap + 1].rearrange("p a b -> p (a b)")
                            out = main[:, :, bass.ds(at + (HEADS * Q_A + t), 1), :].rearrange("p m a t -> p m (a t)")
                            src = raw[:, bass.ds(at + t, 1), tap:tap + T].rearrange("p a (m t) -> p (a m) t", m=TILES)
                            if tap == 0:
                                ins = dve.tensor_scalar(out, src, w, None, ALU.mult)
                            else:
                                dve.wait_ge(*c.dve_chain.made(behind=1))
                                ins = dve.scalar_tensor_tensor(out=out, in0=src, scalar=w, in1=out,
                                                               op0=ALU.mult, op1=ALU.add)
                            ins.then_inc(c.dve_chain.next(), 1)

            with dve.Fori(0, COUNT["conv"] // 2) as i:
                c.dve_chain.begin(i, 4 * 2 * CONV_W)
                for par in range(2):
                    conv(i, par)
            c.dve_chain.end(COUNT["conv"] // 2)
            dve.wait_ge(*c.dve_chain.made())
            dve.memset(c.small[:, 700:701], 0.0).then_inc(c.next("conv"), 1)
    c.loaded.base += 16
    c.end_stage()


class Units:

    def __init__(self, c, names):
        self.c, self.names = c, list(names)
        self.at = {x: i for i, x in enumerate(self.names)}
        assert len(self.at) == len(self.names)
        self.n = 0

    def bank(self, name):
        return 4 + 2 * (self.at[name] % 2)

    def view(self, name, groups=HEADS):
        b = self.bank(name)
        return self.c.ps[:, b:b + 2, :].rearrange("p b (g n) -> p (b g) n", g=groups // 2)

    def emptied(self, name):
        assert self.names[self.n] == name, (name, self.names[self.n])
        u = self.at[name]
        return self.c.pair_read[u % 2].count(u // 2)

    def filled(self):
        u, self.n = self.n, self.n + 1
        return self.c.pair_full[u % 2].sem

    def full(self, name):
        u = self.at[name]
        return self.c.pair_full[u % 2].count(u // 2 + 1)

    def freed(self, name):
        return self.c.pair_read[self.at[name] % 2].sem

    def read_out(self, name):
        u = self.at[name]
        return self.c.pair_read[u % 2].count(u // 2 + 1)

    def close(self):
        n = len(self.names)
        assert self.n == n, (self.n, n)
        for p in range(2):
            self.c.pair_full[p].base += (n + 1 - p) // 2
            self.c.pair_read[p].base += (n + 1 - p) // 2




def norm_gate_act(c, act, o, stat, junk, turn_no):
    act.activation(junk, o, ACT.Square).then_inc(c.next("o_squares"), 1)
    act.wait_ge(*c.count("o_mean", turn_no))
    act.activation(stat[:, 16:24], stat[:, 8:16], ACT.Sqrt).then_inc(c.next("o_root"), 1)


def norm_gate_dve(c, dve, o, gate, which, stat, junk, turn_no, eps=EPS):
    def step(ins):
        ins.then_inc(c.dve_chain.next(), 1)
        dve.wait_ge(*c.dve_chain.made())

    dve.wait_ge(*c.count("o_squares", turn_no))
    step(dve.tensor_reduce(stat[:, 0:8], junk, AX_X, ALU.add))
    dve.tensor_scalar(stat[:, 8:16], stat[:, 0:8], 1.0 / DH, eps, ALU.mult, ALU.add).then_inc(c.next("o_mean"), 1)
    step(dve.tensor_tensor(o, o, spread(c.onorm[:, which, :], HEADS), ALU.mult))
    dve.wait_ge(*c.count("o_root", turn_no))
    step(dve.reciprocal(stat[:, 24:32], stat[:, 16:24]))
    step(dve.tensor_tensor(o, o, along(stat[:, 24:32], DH), ALU.mult))
    if gate is not None:
        step(dve.tensor_tensor(gate, gate, o, ALU.mult))


DOTS_BESIDE_DELTA = 80
DOTS_BESIDE_HGRN = 48
ROWS_BESIDE_BRANCHES = 32
ROWS_BESIDE_CHOICE = 48
assert DOTS_BESIDE_DELTA + DOTS_BESIDE_HGRN == SLOTS
PART_OF_DVE = 4


class Experts:

    def __init__(self, c, ctx):
        nc = c.nc
        self.c = c
        self.ring = [c.row(0, n) for n in range(RING)]
        self.diags = [c.row(0, DIAGS)[:, P * n:P * (n + 1)] for n in range(RING)]
        self.experts, self.gates, self.dots_at, self.weights = (
            c.area(KEPT + 256 * n, TILES, SLOTS) for n in range(4))
        self.now = [c.sb(f"numbers_now{n}", [P, 4], U32) for n in range(2)]
        sem = lambda name: ctx.enter_context(nc.semaphore(name))
        self.row_used, self.row_summed, self.diag_made = sem("row_used"), sem("row_summed"), sem("diag_made")
        self.numbers, self.groups_begun = sem("numbers"), sem("groups_begun")
        self.row_in = [sem(f"row_in{n}") for n in range(RING)]
        self.end = 0
        self.row = {"pool": 0, "dve": 0, "pe": 0, "act": 0}

    def of_dve(self, r):
        phase, q = divmod(r, SLOTS)
        whole = (phase + 1) // 2 * SLOTS + phase // 2 * (SLOTS // PART_OF_DVE)
        return whole + (q if phase % 2 == 0 else -(-q // PART_OF_DVE))

    def of_pe(self, r):
        return r - self.of_dve(r)

    def steps(self, r):
        return (RING, 0) if r // SLOTS % 2 == 0 else (RING // PART_OF_DVE, RING - RING // PART_OF_DVE)

    def fetch(self, pool, turns):
        r = self.row["pool"]
        if r % SLOTS == 0:
            self.fetch_turn(pool, 0)
            turns -= 1
        if turns:
            with pool.Fori(0, turns) as i:
                self.fetch_turn(pool, i)
            self.row["pool"] += RING * (turns - 1)

    def fetch_turn(self, pool, i):
        for half in range(2):
            r = self.row["pool"]
            phase, q = divmod(r, SLOTS)
            dve_rows, pe_rows = self.steps(r)
            if r >= RING:
                pool.wait_ge(self.row_used, dve_rows * i + self.of_dve(r - 4))
                if self.of_pe(r - 4):
                    pool.wait_ge(self.row_summed, pe_rows * i + self.of_pe(r - 4))
            ins = pool.tensor_copy(self.now[half][:, :],
                                   self.experts[:, phase // 2, bass.ds(RING * i + q, 4)].bitcast(U32))
            ins.then_inc(self.numbers, 1)
            pool.wait_ge(self.numbers, 2 * i + (r // 4 + 1))
            pool.sem_inc(self.groups_begun, 1)
            for s in range(4):
                pool.indirect_dma_start(
                    out=self.ring[r % RING + s], out_offset=None,
                    in_=self.c.dram["expert_v" if phase % 2 else "expert_u"],
                    in_offset=bass.IndirectOffsetOnAxis(ap=self.now[half][:, s:s + 1], axis=0),
                ).then_inc(self.row_in[r % RING + s], 16)
            self.row["pool"] += 4

    def begin_stage(self, rows):
        self.end += rows

    def dots(self, dve, n):
        for _ in range(min(n, self.end - self.row["dve"])):
            self.dot(dve, 0)

    def dot(self, dve, i):
        r = self.row["dve"]
        m, q, s = r // (2 * SLOTS), r % SLOTS, r % RING
        row = self.ring[s]
        dve.wait_ge(self.row_in[s], 16 * i + 16 * (r // RING + 1))
        dve.scalar_tensor_tensor(out=row, in0=row, scalar=1.0, in1=self.c.row(m, H2), op0=ALU.mult, op1=ALU.mult,
                                 accum_out=self.dots_at[:, m, bass.ds(RING * i + q, 1)]).then_inc(self.row_used, 1)
        self.row["dve"] += 1

    def begin_sums(self, act):
        r = self.row["act"] // (2 * SLOTS) * 2 * SLOTS + SLOTS
        m = r // (2 * SLOTS)
        act.wait_ge(self.row_used, self.of_dve(r))
        act.activation(self.weights[:, m, :], self.dots_at[:, m, :], ACT.Gelu).then_inc(self.c.next("gelu"), 1)
        act.wait_ge(*self.c.count("weights"))

    def weigh(self, dve):
        m, c = self.row["dve"] // (2 * SLOTS), self.c
        dve.wait_ge(*c.count("gelu"))
        dve.tensor_tensor(self.weights[:, m, :], self.weights[:, m, :], self.gates[:, m, :],
                          ALU.mult).then_inc(c.next("weights"), 1)
        dve.wait_ge(*c.count("weights"))

    def adds(self, dve, n):
        for _ in range(min(n, (self.end - self.row["dve"]) // PART_OF_DVE)):
            self.add(dve, 0)

    def add(self, dve, i):
        r = self.row["dve"]
        m, q, s = r // (2 * SLOTS), r % SLOTS, r % RING
        row, y = self.ring[s], self.c.row(m, H2)
        weight = self.weights[:, m, bass.ds(RING * i + q, 1)]
        dve.wait_ge(self.row_in[s], 16 * i + 16 * (r // RING + 1))
        if q == 0:
            ins = dve.tensor_scalar(y, row, weight, None, ALU.mult)
        else:
            dve.wait_ge(self.row_used, self.steps(r)[0] * i + self.of_dve(r))
            ins = dve.scalar_tensor_tensor(out=y, in0=row, scalar=weight, in1=y, op0=ALU.mult, op1=ALU.add)
        ins.then_inc(self.row_used, 1)
        self.row["dve"] += PART_OF_DVE

    def row_of(self, engine):
        r = self.row[engine]
        if r // SLOTS % 2 == 0:
            r = (r // SLOTS + 1) * SLOTS
        self.row[engine] = r + (r % PART_OF_DVE == 0)
        return self.row[engine]

    def diagonals(self, act, n):
        for _ in range(n):
            if self.row_of("act") < self.end:
                self.diagonal(act, 0)

    def diagonal(self, act, i):
        r = self.row_of("act")
        m, q = r // (2 * SLOTS), r % SLOTS
        used = self.of_pe(r - q if q < RING else r - RING + 1)
        if used:
            act.wait_ge(self.row_summed, 6 * i + used)
        act.activation(self.diags[r % RING], self.c.mat("ident"), ACT.Copy,
                       scale=self.weights[:, m, bass.ds(RING * i + q, 1)]).then_inc(self.diag_made, 1)
        self.row["act"] += 1

    def sums(self, pe, n):
        for _ in range(n):
            if self.row_of("pe") < self.end:
                self.sum(pe, 0)

    def sum(self, pe, i):
        r = self.row_of("pe")
        q, s = r % SLOTS, r % RING
        pe.wait_ge(self.row_in[s], 16 * i + 16 * (r // RING + 1))
        pe.wait_ge(self.diag_made, 6 * i + (self.of_pe(r) + 1))
        for half in range(2):
            mm = pe.matmul(self.c.ps[:, 1 + 2 * half, :], self.diags[s], self.ring[s][:, half * HALF:(half + 1) * HALF],
                           start=(q == 1), stop=(q == SLOTS - 1))
        mm.then_inc(self.row_summed, 1)
        self.row["pe"] += 1

    def turns(self, eng, engine, n, step, per_turn):
        with eng.Fori(0, n) as i:
            for _ in range(per_turn):
                step(eng, i)
        self.row[engine] += RING * (n - 1)


def delta_rule(c, m):
    nc, rows_of = c.nc, c.experts
    gate = c.part(m, GATE_A)
    qT, kT, vT = (c.part(m, a) for a in (Q_A, K_A, V_A))
    slot = lambda n: c.area(SCRATCH + D * n, HEADS, P)
    v_t, k_t, g_run, decay, N, a_qk, q_dec, X, Y, PX, N_l, u = (slot(n) for n in range(12))
    S = slot(STATE_A)
    b_diag = N_l
    kb, wT = g_run, decay
    o, v_new, k_dec = u, v_t, k_t
    both = c.area(PARTS * D * m + D * Q_A, 2 * D)
    sq, root = c.area(SCRATCH, 2 * D), c.area(SCRATCH + 2 * D, 2 * D)
    sm = c.small
    beta, z, z_abs, lnp, g = (sm[:, 16 * n:16 * n + 16].rearrange("p (m h) -> p m h", m=TILES)
                              for n in range(5))
    neg_a, a_log, dt_bias = sm[:, 80:88], sm[:, 256:264], sm[:, 264:272]
    e_g = sm[:, 96:128]
    bg, stat = sm[:, 160:168], sm[:, 176:208]
    bt = c.bt[:, :].rearrange("p (m n) -> p m n", m=TILES)
    rows = lambda ch: slice(CHUNK * ch, CHUNK * (ch + 1))
    beside = m == 0

    names = ["k_t", "v_t", "decay", "g_cols", "g_rows", "kk", "beta", "qk"]
    for l in range(LEVELS):
        names += [f"P{l}"] + ([f"X{l}"] if 0 < l < LEVELS - 1 else []) + ([f"Y{l}"] if l else [])
    names += ["u", "w"] + [f"{x}.{n}" for n in range(2) for x in ("ws", "o", "s")]
    un = Units(c, names)

    rows_of.begin_stage(DOTS_BESIDE_DELTA if m else 0)
    with nc.Block() as block:
        @block.sync
        def _(sp):
            if m == 0:
                sp.dma_start(a_log, c.dram["a_log"]).then_inc(c.loaded.sem, 16)
                sp.dma_start(dt_bias, c.dram["dt_bias"]).then_inc(c.loaded.sem, 16)
                for name in ("b_f", "b_i", "b_q", "b_gate"):
                    c.stream(sp, name)

        if m:
            @block.gpsimd
            def _(pool):
                rows_of.fetch(pool, DOTS_BESIDE_DELTA // RING)

        @block.scalar
        def _(act):
            if m == 0:
                act.activation(beta, bt[:, :, 0:8], ACT.Sigmoid).then_inc(c.next("beta"), 1)
                act.wait_ge(*c.count("z_abs"))
                act.activation(lnp, z_abs, ACT.Exp, scale=-1.0).then_inc(c.act_chain.next(), 1)
                act.wait_ge(*c.act_chain.made())
                act.activation(lnp, lnp, ACT.Ln, bias=1.0).then_inc(c.next("ln"), 1)
                act.wait_ge(*c.loaded.count(32))
                act.activation(neg_a, a_log, ACT.Exp).then_inc(c.next("exp_a"), 1)
            act.wait_ge(*c.count("norms"))
            act.activation(root, c.ps[:, 4:8, :].rearrange("p b n -> p (b n)"),
                           ACT.Sqrt, bias=EPS).then_inc(c.next("norm_root"), 1)
            act.wait_ge(*un.full("k_t"))
            act.activation(k_t, un.view("k_t"), ACT.Copy).then_inc(un.freed("k_t"), 1)
            if beside:
                c.read_beside(act, 0)
            act.wait_ge(*un.full("decay"))
            act.activation(decay, un.view("decay"), ACT.Exp).then_inc(un.freed("decay"), 1)
            act.wait_ge(*un.full("g_cols"))
            act.activation(q_dec, un.view("g_cols"), ACT.Exp).then_inc(un.freed("g_cols"), 1)
            act.wait_ge(*un.full("g_rows"))
            act.activation(e_g, un.view("g_rows", 2)[:, 0, 0:32], ACT.Exp).then_inc(un.freed("g_rows"), 1)
            if beside:
                c.read_beside(act, 1)
            for l in range(LEVELS):
                act.wait_ge(*un.full(f"P{l}"))
                act.activation(PX, un.view(f"P{l}"), ACT.Copy).then_inc(un.freed(f"P{l}"), 1)
                if beside:
                    c.read_beside(act, 2 + 2 * l)
                    c.read_beside(act, 3 + 2 * l)
            act.wait_ge(*un.full("u"))
            act.activation(u, un.view("u"), ACT.Copy).then_inc(un.freed("u"), 1)
            act.wait_ge(*un.full("w"))
            act.activation(wT, un.view("w"), ACT.Copy).then_inc(un.freed("w"), 1)
            for ch in range(2):
                r = rows(ch)
                if beside:
                    c.read_beside(act, 14 + ch)
                act.wait_ge(*un.full(f"o.{ch}"))
                act.wait_ge(*un.read_out(f"ws.{ch}"))
                act.activation(o[r], un.view(f"o.{ch}")[r], ACT.Copy).then_inc(un.freed(f"o.{ch}"), 1)
            for ch in range(2):
                act.wait_ge(*un.read_out(f"o.{ch}"))
            norm_gate_act(c, act, o, stat, PX, 1)

        @block.vector
        def _(dve):
            def step(ins):
                ins.then_inc(c.dve_chain.next(), 1)
                dve.wait_ge(*c.dve_chain.made())

            def dots(n):
                if m:
                    rows_of.dots(dve, n)

            if m == 0:
                dve.wait_ge(*c.loaded.count(32))
                step(dve.tensor_tensor(z, bt[:, :, 8:16], spread(dt_bias, TILES), ALU.add))
                dve.scalar_tensor_tensor(out=z_abs, in0=z, scalar=-1.0, in1=z,
                                         op0=ALU.mult, op1=ALU.max).then_inc(c.next("z_abs"), 1)
            dve.tensor_tensor(sq, both, both, ALU.mult).then_inc(c.next("squares"), 1)
            if m == 0:
                dve.wait_ge(*c.count("ln"))
                step(dve.scalar_tensor_tensor(out=g, in0=z, scalar=0.0, in1=lnp, op0=ALU.max, op1=ALU.add))
                dve.wait_ge(*c.count("exp_a"))
                step(dve.scalar_tensor_tensor(out=g, in0=g, scalar=-1.0, in1=spread(neg_a, TILES),
                                              op0=ALU.mult, op1=ALU.mult))
                step(dve.memset(S, 0.0))
            dots(5)
            dve.wait_ge(*c.count("norm_root"))
            step(dve.reciprocal(root, root))
            for n, (t, scale) in enumerate(((qT, DH ** -0.5), (kT, 1.0))):
                dve.scalar_tensor_tensor(out=t, in0=t, scalar=scale, in1=root.rearrange(
                    "p (n h t) -> p n h t", n=2, h=HEADS)[:, n], op0=ALU.mult, op1=ALU.mult)\
                   .then_inc(c.next("unit_rows"), 1)
            dve.wait_ge(*c.count("unit_rows", 2))
            dve.tensor_tensor(g_run, spread(c.mat("upto"), HEADS), along(g[:, m, :], P),
                              ALU.mult).then_inc(c.next("g_run"), 1)
            dots(2)
            dve.wait_ge(*un.full("v_t"))
            if m == 0:
                dve.wait_ge(*c.count("beta"))
            dve.tensor_tensor(v_t, un.view("v_t"), along(beta[:, m, :], DH), ALU.mult).then_inc(un.freed("v_t"), 1)
            dve.tensor_tensor(b_diag, spread(c.mat("ident"), HEADS), along(beta[:, m, :], P),
                              ALU.mult).then_inc(c.next("b_diag"), 1)
            dots(2)
            dve.wait_ge(*un.read_out("decay"))
            step(dve.tensor_tensor(decay, decay, spread(c.mat("upto"), HEADS), ALU.mult))
            dve.wait_ge(*un.read_out("g_cols"))
            dve.tensor_tensor(q_dec, q_dec, qT, ALU.mult).then_inc(c.next("q_dec"), 1)
            dots(1)
            dve.wait_ge(*un.full("kk"))
            dve.tensor_tensor(N, un.view("kk"), decay, ALU.mult).then_inc(un.freed("kk"), 1)
            dve.wait_ge(*un.read_out("kk"))
            dve.wait_ge(*un.full("beta"))
            dve.tensor_tensor(N, N, un.view("beta"), ALU.mult).then_inc(un.freed("beta"), 1)
            dots(1)
            dve.wait_ge(*un.full("qk"))
            dve.tensor_tensor(a_qk, un.view("qk"), decay, ALU.mult).then_inc(un.freed("qk"), 1)
            dve.wait_ge(*un.read_out("beta"))
            for l in range(LEVELS):
                if l:
                    dve.wait_ge(*un.full(f"P{l - 1}"))
                dve.tensor_tensor(N_l, N, spread(c.mat(f"level{l}"), HEADS), ALU.mult).then_inc(c.next("N_l"), 1)
                if l == 0:
                    dve.wait_ge(*c.count("N_l", 1))
                    dve.tensor_tensor(Y, spread(c.mat("ident"), HEADS), N_l, ALU.subtract).then_inc(c.next("Y0"), 1)
                    dots(2)
                    dve.wait_ge(*un.read_out("P0"))
                    dve.tensor_tensor(X, spread(c.mat("ident"), HEADS), PX, ALU.subtract).then_inc(c.next("X0"), 1)
                    dve.wait_ge(*c.count("X0", 1))
                    continue
                dots(5)
                if l < LEVELS - 1:
                    dve.wait_ge(*un.full(f"X{l}"))
                    dve.tensor_tensor(X, X, un.view(f"X{l}"), ALU.subtract).then_inc(un.freed(f"X{l}"), 1)
                dots(1)
                dve.wait_ge(*un.full(f"Y{l}"))
                dve.tensor_tensor(Y, Y, un.view(f"Y{l}"), ALU.subtract).then_inc(un.freed(f"Y{l}"), 1)
                if l < LEVELS - 1:
                    dve.wait_ge(*un.read_out(f"X{l}"))
                dve.wait_ge(*un.read_out(f"Y{l}"))
            dve.wait_ge(*un.read_out("g_rows"))
            dve.wait_ge(*un.read_out("k_t"))
            step(dve.tensor_tensor(bg, beta[:, m, :], e_g[:, 0:8], ALU.mult))
            dve.tensor_tensor(kb, k_t, along(bg, DH), ALU.mult).then_inc(c.next("kb"), 1)
            dve.wait_ge(*c.count("kb"))
            dve.tensor_tensor(k_dec, k_t, along(e_g[:, 8:16], DH), ALU.mult).then_inc(c.next("k_dec"), 1)
            dots(4)
            dve.wait_ge(*un.read_out("u"))
            for ch in range(2):
                r = rows(ch)
                dots(2)
                dve.wait_ge(*un.full(f"ws.{ch}"))
                dve.tensor_tensor(v_new[r], u[r], un.view(f"ws.{ch}")[r], ALU.subtract).then_inc(un.freed(f"ws.{ch}"), 1)
                dots(2)
                dve.wait_ge(*un.full(f"o.{ch}"))
                step(dve.tensor_tensor(S, S, along(e_g[:, 16 + 8 * ch:24 + 8 * ch], DH), ALU.mult))
                dve.wait_ge(*un.full(f"s.{ch}"))
                dve.tensor_tensor(S, S, un.view(f"s.{ch}"), ALU.add).then_inc(un.freed(f"s.{ch}"), 1)
                dve.wait_ge(*un.read_out(f"s.{ch}"))
            dots(2)
            norm_gate_dve(c, dve, o, gate, 0, stat, PX, 1)
            dots(SLOTS)

        @block.tensor
        def _(pe):
            ones, ident, after = c.mat("ones"), c.mat("ident"), c.mat("after")
            pe.wait_ge(*c.count("squares"))
            for b in range(4):
                mm = pe.matmul(c.ps[:, 4 + b, :], ones, sq[:, b * HALF:(b + 1) * HALF],
                               start=True, stop=True)
            mm.then_inc(c.next("norms"), 1)
            if beside:
                c.product_beside(pe, 0)
            pe.wait_ge(*c.count("unit_rows", 2))

            def heads(name, lhs, rhs):
                out = un.view(name)
                pe.wait_ge(*un.emptied(name))
                for h in range(HEADS):
                    mm = pe.matmul(out[:, h, :], lhs(h), rhs(h), start=True, stop=True)
                mm.then_inc(un.filled(), 1)

            def wide(name, lhs, rhs):
                out = un.view(name, 2)
                pe.wait_ge(*un.emptied(name))
                for b in range(2):
                    mm = pe.matmul(out[:, b, :], lhs, rhs[:, 4 * b:4 * b + 4, :].rearrange("p h n -> p (h n)"),
                                   start=True, stop=True)
                mm.then_inc(un.filled(), 1)

            for name, src in (("k_t", kT), ("v_t", vT)):
                pe.wait_ge(*un.emptied(name))
                for h in range(HEADS):
                    mm = pe.transpose(un.view(name)[:, h, :], src[:, h, :], ident)
                mm.then_inc(un.filled(), 1)
            pe.wait_ge(*c.count("g_run"))
            wide("decay", after, g_run)
            wide("g_cols", ones, g_run)
            pe.wait_ge(*un.emptied("g_rows"))
            for n, mat in enumerate(("upto", "after", "chunk0", "chunk1")):
                mm = pe.matmul(un.view("g_rows", 2)[:, 0, 8 * n:8 * n + 8], c.mat(mat),
                               g[:, m, :], start=True, stop=True)
            mm.then_inc(un.filled(), 1)
            if beside:
                c.product_beside(pe, 1)
            heads("kk", lambda h: kT[:, h, :], lambda h: kT[:, h, :])
            pe.wait_ge(*c.count("b_diag"))
            wide("beta", ones, b_diag)
            heads("qk", lambda h: kT[:, h, :], lambda h: qT[:, h, :])
            for l in range(LEVELS):
                pe.wait_ge(*c.count("N_l", l + 1))
                if l == 1:
                    pe.wait_ge(*c.count("X0"))
                heads(f"P{l}", lambda h: N_l[:, h, :], lambda h: X[:, h, :] if l else ident)
                if beside:
                    c.product_beside(pe, 2 + 2 * l)
                if l:
                    pe.wait_ge(*un.read_out(f"P{l}"))
                    if l < LEVELS - 1:
                        heads(f"X{l}", lambda h: Y[:, h, :], lambda h: PX[:, h, :])
                    heads(f"Y{l}", lambda h: PX[:, h, :], lambda h: Y[:, h, :])
                if beside:
                    c.product_beside(pe, 3 + 2 * l)
            pe.wait_ge(*un.read_out(f"Y{LEVELS - 1}"))
            heads("u", lambda h: Y[:, h, :], lambda h: v_t[:, h, :])
            pe.wait_ge(*c.count("kb"))
            heads("w", lambda h: kb[:, h, :], lambda h: Y[:, h, :])
            if beside:
                c.product_beside(pe, 14)
            pe.wait_ge(*un.read_out("w"))
            pe.wait_ge(*c.count("k_dec"))
            for ch in range(2):
                r = rows(ch)
                heads(f"ws.{ch}", lambda h: wT[:, h, :], lambda h: S[:, h, :])
                if beside and ch:
                    c.product_beside(pe, 15)
                pe.wait_ge(*un.read_out(f"ws.{ch}"))
                pe.wait_ge(*un.emptied(f"o.{ch}"))
                for h in range(HEADS):
                    out = un.view(f"o.{ch}")[:, h, :]
                    pe.matmul(out, q_dec[:, h, :], S[:, h, :], start=True, stop=False)
                    mm = pe.matmul(out, a_qk[r, h, :], v_new[r, h, :], start=False, stop=True)
                mm.then_inc(un.filled(), 1)
                heads(f"s.{ch}", lambda h: k_dec[r, h, :], lambda h: v_new[r, h, :])
                pe.wait_ge(*un.read_out(f"s.{ch}"))
    un.close()
    if m == 0:
        c.loaded.base += 32
    c.end_stage()


def hgrn(c, m):
    nc, rows_of = c.nc, c.experts
    gate, f, v, qT = (c.part(m, a) for a in (GATE_B, F_B, I_B, Q_B))
    slot = lambda n: c.area(SCRATCH + D * n, HEADS, P)
    k_t, kT, span, both, a_qk, e_b, q_dec, k_dec, o, log_f, lb, lb1 = (slot(n) for n in range(12))
    junk = span
    S = slot(STATE_B)
    flat = lambda t: t.rearrange("p h n -> p (h n)")
    stat = c.small[:, 176:208]
    rows = lambda ch: slice(CHUNK * ch, CHUNK * (ch + 1))
    beside = m == 0
    names = ["k_t", "same"] + [f"{x}{l}" for l in range(LEVELS) for x in ("span", "a")]
    names += ["e_b", "to_end"] + [f"{x}.{n}" for n in range(2) for x in ("o", "s")]
    un = Units(c, names)

    rows_of.begin_stage(DOTS_BESIDE_HGRN if m else 0)
    with nc.Block() as block:
        @block.sync
        def _(sp):
            if m == 0:
                load_row(c, sp, flat(lb), "b_low0")
                load_row(c, sp, flat(lb1), "b_low1")
                for name in ("g_a", "g_b"):
                    c.stream(sp, name)

        if m:
            @block.gpsimd
            def _(pool):
                rows_of.fetch(pool, DOTS_BESIDE_HGRN // RING)

        @block.scalar
        def _(act):
            if m == 0:
                act.wait_ge(*c.count("low_diff"))
                act.activation(lb, lb, ACT.Sigmoid).then_inc(c.next("low"), 1)
                act.wait_ge(*c.count("f", TILES))
            act.activation(log_f, f, ACT.Ln).then_inc(c.next("log_f"), 1)
            act.wait_ge(*un.full("k_t"))
            act.activation(kT, un.view("k_t"), ACT.Copy).then_inc(un.freed("k_t"), 1)
            for l in range(LEVELS):
                act.wait_ge(*un.full(f"span{l}"))
                if l:
                    act.wait_ge(*c.count("both", 2 * l))
                act.activation(span, un.view(f"span{l}"), ACT.Exp).then_inc(un.freed(f"span{l}"), 1)
                if beside:
                    c.read_beside(act, BESIDE_DELTA + l)
            act.wait_ge(*un.full("e_b"))
            act.activation(e_b, un.view("e_b"), ACT.Exp).then_inc(un.freed("e_b"), 1)
            act.wait_ge(*un.full("to_end"))
            act.activation(k_dec, un.view("to_end"), ACT.Exp).then_inc(un.freed("to_end"), 1)
            for ch in range(2):
                r = rows(ch)
                if beside:
                    c.read_beside(act, BESIDE_DELTA + LEVELS + ch)
                act.wait_ge(*un.full(f"o.{ch}"))
                act.activation(o[r], un.view(f"o.{ch}")[r], ACT.Copy).then_inc(un.freed(f"o.{ch}"), 1)
            for ch in range(2):
                act.wait_ge(*un.read_out(f"o.{ch}"))
            norm_gate_act(c, act, o, stat, junk, 1)

        @block.vector
        def _(dve):
            def step(ins):
                ins.then_inc(c.dve_chain.next(), 1)
                dve.wait_ge(*c.dve_chain.made())

            def dots(n):
                if m:
                    rows_of.dots(dve, n)

            if m == 0:
                dve.wait_ge(*c.loaded.count(32))
                dve.tensor_tensor(lb, lb, lb1, ALU.subtract).then_inc(c.next("low_diff"), 1)
                step(dve.memset(S, 0.0))
                dve.wait_ge(*c.count("low"))
                step(dve.tensor_scalar(lb1, lb, -1.0, 1.0, ALU.mult, ALU.add))
                for tile in range(TILES):
                    step(dve.tensor_tensor(c.part(tile, F_B), c.part(tile, F_B), lb1, ALU.mult))
                    dve.tensor_tensor(c.part(tile, F_B), c.part(tile, F_B), lb, ALU.add).then_inc(c.next("f"), 1)
                dve.wait_ge(*c.count("f", TILES))
            dve.tensor_scalar(k_t, f, -1.0, 1.0, ALU.mult, ALU.add).then_inc(c.next("k_t"), 1)
            dots(3)
            dve.wait_ge(*un.full("same"))
            dve.tensor_tensor(a_qk, un.view("same"), spread(c.mat("ident"), HEADS), ALU.mult).then_inc(un.freed("same"), 1)
            for l in range(LEVELS):
                halves = lambda t: t.rearrange("p h (b s t) -> p h b s t", s=2, t=1 << l)
                dots(2)
                dve.wait_ge(*un.read_out(f"span{l}"))
                if l:
                    dve.wait_ge(*un.full(f"a{l - 1}"))
                for side, x in ((1, qT), (0, kT)):
                    dve.tensor_tensor(halves(both)[:, :, :, side, :], halves(x)[:, :, :, side, :],
                                      halves(span)[:, :, :, side, :], ALU.mult).then_inc(c.next("both"), 1)
                dots(2)
                dve.wait_ge(*un.full(f"a{l}"))
                if l == 0:
                    dve.wait_ge(*un.read_out("same"))
                else:
                    dve.wait_ge(*un.read_out(f"a{l - 1}"))
                dve.copy_predicated(out=a_qk, mask=spread(c.masks[:, l, :], HEADS),
                                    data=un.view(f"a{l}")).then_inc(un.freed(f"a{l}"), 1)
            dots(2)
            dve.wait_ge(*un.read_out("e_b"))
            dve.tensor_tensor(q_dec, qT, e_b, ALU.mult).then_inc(c.next("q_dec_b"), 1)
            dve.wait_ge(*un.read_out("to_end"))
            dve.wait_ge(*c.count("k_t"))
            dve.tensor_tensor(k_dec, k_dec, k_t, ALU.mult).then_inc(c.next("k_dec_b"), 1)
            for ch in range(2):
                last = CHUNK * (ch + 1) - 1
                dots(3)
                dve.wait_ge(*un.full(f"o.{ch}"))
                step(dve.tensor_tensor(S, S, e_b[:, :, last:last + 1].broadcast_to([P, HEADS, DH]), ALU.mult))
                dve.wait_ge(*un.full(f"s.{ch}"))
                dve.tensor_tensor(S, S, un.view(f"s.{ch}"), ALU.add).then_inc(un.freed(f"s.{ch}"), 1)
                dve.wait_ge(*un.read_out(f"s.{ch}"))
            dots(2)
            norm_gate_dve(c, dve, o, gate, 1, stat, junk, 1)
            dots(SLOTS)

        @block.tensor
        def _(pe):
            def heads(name, lhs, rhs):
                out = un.view(name)
                pe.wait_ge(*un.emptied(name))
                for h in range(HEADS):
                    mm = pe.matmul(out[:, h, :], lhs(h), rhs(h), start=True, stop=True)
                mm.then_inc(un.filled(), 1)

            pe.wait_ge(*c.count("k_t"))
            pe.wait_ge(*un.emptied("k_t"))
            for h in range(HEADS):
                mm = pe.transpose(un.view("k_t")[:, h, :], k_t[:, h, :], c.mat("ident"))
            mm.then_inc(un.filled(), 1)
            pe.wait_ge(*un.read_out("k_t"))
            heads("same", lambda h: kT[:, h, :], lambda h: qT[:, h, :])
            pe.wait_ge(*c.count("log_f"))
            for l in range(LEVELS):
                heads(f"span{l}", lambda h: log_f[:, h, :], lambda h: c.mat(f"span{l}"))
                if beside:
                    c.product_beside(pe, BESIDE_DELTA + l)
                pe.wait_ge(*c.count("both", 2 * (l + 1)))
                heads(f"a{l}", lambda h: both[:, h, :], lambda h: both[:, h, :])
            heads("e_b", lambda h: log_f[:, h, :], lambda h: c.mat("upto"))
            pe.wait_ge(*un.emptied("to_end"))
            for b in range(2):
                mm = pe.matmul(un.view("to_end", 2)[:, b, :], c.mat("after"),
                               flat(log_f)[:, b * HALF:(b + 1) * HALF], start=True, stop=True)
            mm.then_inc(un.filled(), 1)
            for ch in range(2):
                r = rows(ch)
                if beside:
                    c.product_beside(pe, BESIDE_DELTA + LEVELS + ch)
                if ch == 0:
                    pe.wait_ge(*c.count("q_dec_b"))
                    pe.wait_ge(*c.count("k_dec_b"))
                pe.wait_ge(*un.emptied(f"o.{ch}"))
                for h in range(HEADS):
                    out = un.view(f"o.{ch}")[:, h, :]
                    pe.matmul(out, q_dec[:, h, :], S[:, h, :], start=True, stop=False)
                    mm = pe.matmul(out, a_qk[r, h, :], v[r, h, :], start=False, stop=True)
                mm.then_inc(un.filled(), 1)
                heads(f"s.{ch}", lambda h: k_dec[r, h, :], lambda h: v[r, h, :])
                pe.wait_ge(*un.read_out(f"s.{ch}"))
    un.close()
    if m == 0:
        c.loaded.base += 32
    c.end_stage()


def branches(c, m):
    nc, rows_of = c.nc, c.experts
    o_a, o_b, g_a, g_b = (c.row(m, a) for a in (GATE_A, GATE_B, MIX_A, MIX_B))
    aT, bT, mixT = (c.area(SCRATCH + D * n, KC, P) for n in range(3))
    uses = list(c.bank_uses)
    names = [f"{x}.{m}" for x in ("branch_a", "branch_b", "w_out")]
    first = FIRST[names[0]]
    rows_of.begin_stage(ROWS_BESIDE_BRANCHES if m else 0)
    with nc.Block() as block:
        @block.sync
        def _(sp):
            for name in names:
                c.stream(sp, name)

        if m:
            @block.gpsimd
            def _(pool):
                rows_of.fetch(pool, ROWS_BESIDE_BRANCHES // RING)

        @block.tensor
        def _(pe):
            turn_tile(c, pe, o_a)
            wait_turned_tile_read(c, pe)
            turn_tile(c, pe, o_b)
            c.products_of_tile(pe, names[0], aT, channel_major=False)
            if m:
                rows_of.sums(pe, 3)
            wait_turned_tile_read(c, pe)
            c.products_of_tile(pe, names[1], bT, channel_major=False)
            if m:
                rows_of.sums(pe, 6)
            pe.wait_ge(*c.count("mix"))
            turn_tile(c, pe, g_a)
            if m:
                rows_of.sums(pe, 3)
            wait_turned_tile_read(c, pe)
            c.products_of_tile(pe, names[2], mixT, channel_major=False)
            if m:
                rows_of.sums(pe, SLOTS)

        @block.scalar
        def _(act):
            if m:
                rows_of.begin_sums(act)
            for n, out in enumerate((aT, bT, mixT)):
                read_turned_tile(c, act, out, n)
                if m:
                    rows_of.diagonals(act, SLOTS if n == 2 else 6)

        @block.vector
        def _(dve):
            if m:
                rows_of.weigh(dve)
            for n, gate in enumerate((g_a, g_b)):
                for q in range(2):
                    dve.wait_ge(c.panel_done.sem, first + 2 * n + q + 1)
                    bank = 2 * ((first + q) % 2)
                    at = gate[:, q * HALF:(q + 1) * HALF]
                    dve.tensor_tensor(at, at, c.ps[:, bank, :], ALU.mult).then_inc(c.bank_read[bank].sem, 1)
                if m:
                    rows_of.adds(dve, 2)
            for b in (0, 2):
                dve.wait_ge(c.bank_read[b].sem, uses[b] + 4)
            dve.tensor_tensor(g_a, g_a, g_b, ALU.add).then_inc(c.next("mix"), 1)
            for q in range(2):
                dve.wait_ge(c.panel_done.sem, first + 4 + q + 1)
                bank = 2 * ((first + q) % 2)
                at = c.x[:, m, q * HALF:(q + 1) * HALF]
                dve.tensor_tensor(at, at, c.ps[:, bank, :], ALU.add).then_inc(c.bank_read[bank].sem, 1)
            if m:
                rows_of.adds(dve, SLOTS)
    c.turned.base += 6
    c.end_stage()


def norm_of_tile(c, m):
    nc = c.nc
    g, junk = (c.area(SCRATCH + D * n, D) for n in range(2))
    out, x = c.row(m, H2), c.x[:, m, :]
    sm = c.small[:, 300:304]
    with nc.Block() as block:
        @block.sync
        def _(sp):
            load_row(c, sp, g, "norm2")

        @block.scalar
        def _(act):
            act.activation(junk, x, ACT.Square, accum_out=sm[:, 0:1]).then_inc(c.next("square"), 1)
            act.wait_ge(*c.count("mean"))
            act.activation(sm[:, 2:3], sm[:, 1:2], ACT.Sqrt).then_inc(c.next("root"), 1)
            read_turned_tile(c, act, c.xT[:, :, m * P:(m + 1) * P], 0)

        @block.vector
        def _(dve):
            dve.wait_ge(*c.count("square"))
            dve.tensor_scalar(sm[:, 1:2], sm[:, 0:1], 1.0 / D, EPS, ALU.mult, ALU.add).then_inc(c.next("mean"), 1)
            dve.wait_ge(*c.count("root"))
            dve.reciprocal(sm[:, 3:4], sm[:, 2:3]).then_inc(c.dve_chain.next(), 1)
            dve.wait_ge(*c.dve_chain.made())
            dve.wait_ge(*c.loaded.count(16))
            dve.scalar_tensor_tensor(out=out, in0=x, scalar=sm[:, 3:4], in1=g,
                                     op0=ALU.mult, op1=ALU.mult).then_inc(c.next("normed"), 1)

        @block.tensor
        def _(pe):
            pe.wait_ge(*c.count("normed"))
            turn_tile(c, pe, out)
    c.loaded.base += 16
    c.turned.base += 2
    c.end_stage()


def choose_experts(c, m):
    nc, rows_of = c.nc, c.experts
    slot = lambda n, *shape: c.area(SCRATCH + D * n, *shape)
    qT, keys = slot(0, 2 * P_HEADS, P), slot(2, 2 * P_HEADS, N_KEYS)
    scores, left = slot(4, 2 * P_HEADS, N_KEYS), slot(6, 2 * P_HEADS, N_KEYS)
    cand, cand_left = slot(8, P_HEADS, TOPK * TOPK), slot(4, P_HEADS, TOPK * TOPK)
    hot = slot(6, P_HEADS, TOPK, TOPK)
    tops = SCRATCH + D * 10
    top, best = c.area(tops, 2 * P_HEADS, TOPK), c.area(tops + 512, P_HEADS, TOPK)
    top_at = c.area(tops + 256, 2 * P_HEADS, TOPK)
    best_at = c.area(tops + 640, P_HEADS, TOPK)
    half_at = [c.area(tops + 768 + 128 * n, P_HEADS, TOPK) for n in range(2)]
    named = [c.area(tops + 1024 + 128 * n, P_HEADS, TOPK) for n in range(2)]
    top_key = c.area(tops + 1280, 2 * P_HEADS, TOPK)
    iota, total = c.area(tops + 1536, TOPK), c.area(tops + 1552, P_HEADS)
    experts = c.area(KEPT, TILES, SLOTS)[:, m]
    gates = c.area(KEPT + 256, TILES, P_HEADS, TOPK)[:, m]
    pq = f"w_pq.{m}"
    rows_of.begin_stage(ROWS_BESIDE_CHOICE if m else 0)
    with nc.Block() as block:
        @block.sync
        def _(sp):
            sp.dma_start(keys, c.dram["sub_keys"]).then_inc(c.loaded.sem, 16)
            sp.dma_start(iota, c.dram["iota"]).then_inc(c.loaded.sem, 16)
            c.stream(sp, pq)

        if m:
            @block.gpsimd
            def _(pool):
                rows_of.fetch(pool, ROWS_BESIDE_CHOICE // RING)

        @block.tensor
        def _(pe):
            c.products_of_tile(pe, pq, c.xT[:, :, m * P:(m + 1) * P], channel_major=True)
            pe.wait_ge(*c.loaded.count(32))
            for b in (0, 2):
                pe.wait_ge(c.bank_read[b].sem, c.bank_uses[b])
            for n in range(2 * P_HEADS):
                out = c.ps[:, 4 + n // 4, (n % 4) * P:(n % 4 + 1) * P]
                mm = pe.matmul(out, qT[:, n, :], keys[:, n, :], start=True, stop=True)
            mm.then_inc(c.next("scores"), 1)
            if m:
                rows_of.sums(pe, SLOTS)

        @block.scalar
        def _(act):
            for q in range(COUNT[pq]):
                act.wait_ge(c.panel_done.sem, FIRST[pq] + q + 1)
                bank = 2 * ((FIRST[pq] + q) % 2)
                act.activation(qT[:, 4 * q:4 * q + 4, :], c.ps[:, bank, :].rearrange("p (k t) -> p k t", k=4),
                               ACT.Copy).then_inc(c.bank_read[bank].sem, 1)
            act.wait_ge(*c.count("scores"))
            act.activation(scores.rearrange("p n k -> p (n k)"), c.ps[:, 4:8, :].rearrange("p b n -> p (b n)"),
                           ACT.Copy).then_inc(c.next("scores_read"), 1)
            if m:
                rows_of.diagonals(act, SLOTS)
            act.wait_ge(*c.count("best_less_max"))
            act.activation(gates, gates, ACT.Exp).then_inc(c.next("gate_exp"), 1)

        @block.vector
        def _(dve):
            chain = c.dve_chain

            def step(ins):
                ins.then_inc(c.dve_chain.next(), 1)
                dve.wait_ge(*c.dve_chain.made())

            def adds(n):
                if m:
                    rows_of.adds(dve, n)

            def top16(values, left, top, at, groups):
                at = at.bitcast(U32)
                for g in range(groups):
                    dve.max(top[:, g, 0:8], values[:, g, :]).then_inc(chain.next(), 1)
                adds(1)
                dve.wait_ge(*chain.made())
                for g in range(groups):
                    dve.max_index(at[:, g, 0:8], top[:, g, 0:8], values[:, g, :]).then_inc(chain.next(), 1)
                    dve.match_replace(left[:, g, :], top[:, g, 0:8], values[:, g, :], LOWEST).then_inc(chain.next(), 1)
                    if g % 8 == 7:
                        adds(1)
                dve.wait_ge(*chain.made())
                for g in range(groups):
                    dve.max(top[:, g, 8:16], left[:, g, :]).then_inc(chain.next(), 1)
                adds(1)
                dve.wait_ge(*chain.made())
                for g in range(groups):
                    dve.max_index(at[:, g, 8:16], top[:, g, 8:16], left[:, g, :]).then_inc(chain.next(), 1)
                adds(1)
                dve.wait_ge(*chain.made())

            adds(6)
            dve.wait_ge(*c.loaded.count(32))
            dve.wait_ge(*c.count("scores_read"))
            top16(scores, left, top, top_at, 2 * P_HEADS)
            step(dve.tensor_copy(top_key, top_at.bitcast(U32)))
            pairs_of = top.rearrange("p (h s) k -> p h s k", s=2)
            shape = [P, P_HEADS, TOPK, TOPK]
            first = pairs_of[:, :, 0, :].unsqueeze(3).broadcast_to(shape)
            second = pairs_of[:, :, 1, :].unsqueeze(2).broadcast_to(shape)
            step(dve.tensor_tensor(cand.rearrange("p h (a b) -> p h a b", a=TOPK), first, second, ALU.add))
            top16(cand, cand_left, best, best_at, P_HEADS)
            dve.tensor_tensor(gates, best, best[:, :, 0:1].broadcast_to([P, P_HEADS, TOPK]),
                              ALU.subtract).then_inc(c.next("best_less_max"), 1)
            where = best_at.bitcast(U32)
            a, b = (x.bitcast(U32) for x in named)
            step(dve.tensor_scalar(a, where, 4, None, ALU.logical_shift_right))
            step(dve.tensor_scalar(b, where, TOPK - 1, None, ALU.bitwise_and))
            keys_of = top_key.rearrange("p (h s) k -> p h s k", s=2)
            for n, x in enumerate((a, b)):
                step(dve.tensor_copy(half_at[n], x))
            for n in range(2):
                spot = half_at[n].unsqueeze(3).broadcast_to(shape)
                lists = keys_of[:, :, n, :].unsqueeze(2).broadcast_to(shape)
                step(dve.tensor_tensor(hot, spot, iota.unsqueeze(1).unsqueeze(1).broadcast_to(shape),
                                       ALU.is_equal))
                adds(1)
                step(dve.tensor_tensor(hot, hot, lists, ALU.mult))
                step(dve.tensor_reduce(named[n], hot, AX_X, ALU.add))
                adds(1)
            step(dve.scalar_tensor_tensor(out=named[0], in0=named[0], scalar=float(N_KEYS), in1=named[1],
                                          op0=ALU.mult, op1=ALU.add))
            step(dve.tensor_copy(experts.bitcast(U32), named[0].rearrange("p h k -> p (h k)")))
            adds(SLOTS)
            dve.wait_ge(*c.count("gate_exp"))
            step(dve.tensor_reduce(total, gates, AX_X, ALU.add))
            step(dve.reciprocal(total, total))
            step(dve.tensor_tensor(gates, gates, along(total, TOPK), ALU.mult))
    c.loaded.base += 32
    c.end_stage()


def sum_experts(c):
    nc, rows_of = c.nc, c.experts
    left = (SLOTS - ROWS_BESIDE_BRANCHES - ROWS_BESIDE_CHOICE) // RING
    turns = SLOTS // RING
    by_dve = RING // PART_OF_DVE
    by_pe = RING - by_dve
    rows_of.begin_stage(2 * SLOTS + left * RING)
    with nc.Block() as block:
        @block.gpsimd
        def _(pool):
            for n in (left, turns, turns):
                rows_of.fetch(pool, n)

        @block.scalar
        def _(act):
            rows_of.turns(act, "act", left, rows_of.diagonal, by_pe)
            rows_of.begin_sums(act)
            rows_of.diagonals(act, by_pe)
            rows_of.turns(act, "act", turns - 1, rows_of.diagonal, by_pe)

        @block.tensor
        def _(pe):
            for m in range(TILES):
                if m:
                    pe.wait_ge(*c.count("sum_read", 2))
                    rows_of.sums(pe, by_pe)
                    rows_of.turns(pe, "pe", turns - 2, rows_of.sum, by_pe)
                else:
                    rows_of.turns(pe, "pe", left - 1, rows_of.sum, by_pe)
                rows_of.sums(pe, by_pe)

        @block.vector
        def _(dve):
            for m in range(TILES):
                if m:
                    rows_of.turns(dve, "dve", turns, rows_of.dot, RING)
                    rows_of.weigh(dve)
                    rows_of.adds(dve, by_dve)
                    rows_of.turns(dve, "dve", turns - 1, rows_of.add, by_dve)
                else:
                    rows_of.turns(dve, "dve", left, rows_of.add, by_dve)
                r = rows_of.row["dve"]
                dve.wait_ge(rows_of.row_used, rows_of.of_dve(r))
                dve.wait_ge(rows_of.row_summed, rows_of.of_pe(r))
                dve.tensor_tensor(c.x[:, m, :], c.x[:, m, :], c.row(m, H2), ALU.add).then_inc(c.dve_chain.next(), 1)
                dve.wait_ge(*c.dve_chain.made())
                for half in range(2):
                    x = c.x[:, m, half * HALF:(half + 1) * HALF]
                    dve.tensor_tensor(x, x, c.ps[:, 1 + 2 * half, :], ALU.add).then_inc(c.next("sum_read"), 1)
    c.end_stage()



def pooling(c):
    nc = c.nc
    mats = c.area(0, TILES * len(WINDOWS), T)
    w = c.area(8 * T, 2 * len(WINDOWS), 2 * P)
    scale, pooled = c.area(8 * T + 16 * P, D), c.area(6 * D, KC, T)
    mixed = c.area(8 * D, TILES, D)
    with nc.Block() as block:
        @block.sync
        def _(sp):
            sp.dma_start(mats, c.dram["pool_m"].rearrange("p m g t -> p (m g) t")).then_inc(c.loaded.sem, 16)
            sp.dma_start(w, c.dram["pool_w"].rearrange("p g k n -> p (g k) n")).then_inc(c.loaded.sem, 16)
            load_row(c, sp, scale, "pool_scale")

        @block.tensor
        def _(pe):
            pe.wait_ge(*c.loaded.count(48))
            for n in range(KC):
                for m in range(TILES):
                    mm = pe.matmul(c.ps[:, n // 2, (n % 2) * T:(n % 2 + 1) * T], c.x[:, m, n * P:(n + 1) * P],
                                   mats[:, m * len(WINDOWS) + n // 2, :], start=(m == 0), stop=(m == TILES - 1))
                if n % 2:
                    mm.then_inc(c.next("pooled"), 1)
            for m in range(TILES):
                for g in range(len(WINDOWS)):
                    pe.wait_ge(*c.count("pooled_read", g + 1))
                    for k in range(2):
                        mm = pe.matmul(c.ps[:, 4 + 2 * m + g // 2, (g % 2) * T:(g % 2 + 1) * T],
                                       pooled[:, 2 * g + k, m * P:(m + 1) * P], w[:, 2 * g + k, :],
                                       start=(k == 0), stop=(k == 1))
                mm.then_inc(c.next("mixed"), 1)

        @block.scalar
        def _(act):
            for g in range(len(WINDOWS)):
                act.wait_ge(*c.count("pooled", g + 1))
                act.activation(pooled[:, 2 * g:2 * g + 2, :].rearrange("p k t -> p (k t)"),
                                      c.ps[:, g, :], ACT.Copy).then_inc(c.next("pooled_read"), 1)

        @block.vector
        def _(dve):
            dve.wait_ge(*c.loaded.count(48))
            for m in range(TILES):
                dve.wait_ge(*c.count("mixed", m + 1))
                out = c.ps[:, 4 + 2 * m:6 + 2 * m, :].rearrange("p b n -> p (b n)")
                dve.tensor_tensor(mixed[:, m, :], out, scale, ALU.mult).then_inc(c.dve_chain.next(), 1)
                dve.wait_ge(*c.dve_chain.made())
                dve.scalar_tensor_tensor(out=c.x[:, m, :], in0=c.x[:, m, :], scalar=ALPHA, in1=mixed[:, m, :],
                                         op0=ALU.mult, op1=ALU.add).then_inc(c.dve_chain.next(), 1)
                dve.wait_ge(*c.dve_chain.made())
    c.loaded.base += 48
    c.end_stage()


def feed_forward(c, i):
    nc = c.nc
    up, down = f"ff{i}", f"down{i}"
    hidden = c.area(0, FF_T, T)
    silu = c.area(FF_T * T, 2, HALF)
    uses, first = list(c.bank_uses), FIRST[up]
    with nc.Block() as block:
        @block.sync
        def _(sp):
            c.stream(sp, up)
            c.stream(sp, down)

        @block.tensor
        def _(pe):
            c.products(pe, up, c.xT, channel_major=True)
            for n in range(FF_T):
                if n % 4 == 0:
                    slot = c.wait_panel(pe, down, n // 8, n // 4 % 2)
                if n % 2 == 0:
                    q = n // 2
                    b = 2 * ((first + q) % 2) + 1
                    pe.wait_ge(c.bank_read[b].sem, uses[b] + q // 2 + 1)
                w = c.panels[:, slot, :].rearrange("p (k n) -> p k n", k=4)
                for m in range(TILES):
                    for half in range(2):
                        mm = pe.matmul(c.ps[:, 4 + 2 * m + half, :], hidden[:, n, m * P:(m + 1) * P],
                                       w[:, n % 4, half * HALF:(half + 1) * HALF],
                                       start=(n == 0), stop=(n == FF_T - 1))
                if n % 4 == 3 or n == FF_T - 1:
                    mm.then_inc(c.panel_done.sem, 1)

        @block.scalar
        def _(act):
            def read(i, par, j, bank):
                act.wait_ge(c.bank_read[bank + 1].sem, i + uses[bank + 1])
                return act.activation(silu[:, bank // 2, :], c.ps[:, bank, :], ACT.Silu)
            c.evacuate(act, up, read, halves=(0,))

        @block.vector
        def _(dve):
            def read(i, par, j, bank):
                dve.wait_ge(c.bank_read[bank - 1].sem, i + (uses[bank - 1] + 1))
                out = hidden[:, bass.ds(4 * i + 2 * par, 2), :].rearrange("p k t -> p (k t)")
                return dve.tensor_tensor(out, silu[:, bank // 2, :], c.ps[:, bank, :], ALU.mult)
            c.evacuate(dve, up, read, halves=(1,))
            dve.wait_ge(c.panel_done.sem, FIRST[down] + COUNT[down])
            for m in range(TILES):
                out = c.ps[:, 4 + 2 * m:6 + 2 * m, :].rearrange("p b n -> p (b n)")
                dve.scalar_tensor_tensor(out=c.x[:, m, :], in0=c.x[:, m, :], scalar=ALPHA,
                                                         in1=out, op0=ALU.mult, op1=ALU.add).then_inc(c.dve_chain.next(), 1)
    c.end_stage()


def attention(c):
    nc = c.nc
    qkT = c.area(0, 2 * HEADS, T)
    v = c.area(4 * D, TILES, HEADS, DH)
    bias = c.area(6 * D, HEADS, T)
    s = c.area(8 * D, 2 * HEADS, T)
    aT = c.area(12 * D, HEADS * TILES, P)
    o = c.area(14 * D, TILES, HEADS, DH)
    junk = c.area(16 * D, HEADS, DH)
    lam_p, unseen = c.area(17 * D, 4, HEAD_DIM), c.area(17 * D + 256, P)
    lam_prod = c.area(17 * D + 384, 2, HEAD_DIM)
    sm = c.small
    top, total, lam, stat = sm[:, 0:16], sm[:, 16:32], sm[:, 32:36], sm[:, 64:96]
    names = [f"s0.{n}" for n in range(2)] + ["a0.0", "o0"] + [f"s1.{n}" for n in range(4)] + ["a1.0", "a1.1", "o1"]
    un = Units(c, names)
    flat = lambda t: t.rearrange("p h n -> p (h n)")
    with nc.Block() as block:
        @block.sync
        def _(sp):
            sp.dma_start(bias, c.dram["rel_bias"]).then_inc(c.loaded.sem, 16)
            sp.dma_start(unseen, c.dram["not_seen"]).then_inc(c.loaded.sem, 16)
            sp.dma_start(lam_p, c.dram["lam_p"]).then_inc(c.loaded.sem, 16)
            for name in ("qk", "v", "w_o"):
                c.stream(sp, name)

        @block.tensor
        def _(pe):
            c.products(pe, "qk", c.xT, channel_major=True)
            c.products(pe, "v", c.xT, channel_major=False)
            for b in range(4):
                pe.wait_ge(c.bank_read[b].sem, c.bank_uses[b])
            for m in range(TILES):
                keys = P * (m + 1)
                per = 8 // (m + 1)
                for n in range(2 * HEADS // per):
                    pe.wait_ge(*un.emptied(f"s{m}.{n}"))
                    out = un.view(f"s{m}.{n}", per).rearrange("p (s k) n -> p s k n", s=2)
                    for k in range(per):
                        h, half = divmod(n * per + k, 2)
                        r = slice(HEAD_DIM * half, HEAD_DIM * (half + 1))
                        mm = pe.matmul(out[:, half, k // 2, :], qkT[r, h, m * P:(m + 1) * P], qkT[r, HEADS + h, 0:keys],
                                       start=True, stop=True)
                    mm.then_inc(un.filled(), 1)
                pe.wait_ge(*c.count("a", m + 1))
                for kt in range(m + 1):
                    pe.wait_ge(*un.emptied(f"a{m}.{kt}"))
                    for h in range(HEADS):
                        at = s[:, 2 * h, kt * P:(kt + 1) * P]
                        mm = pe.transpose(un.view(f"a{m}.{kt}")[:, h, :], at, c.mat("ident"))
                    mm.then_inc(un.filled(), 1)
                for kt in range(m + 1):
                    pe.wait_ge(*un.read_out(f"a{m}.{kt}"))
                pe.wait_ge(*un.emptied(f"o{m}"))
                for h in range(HEADS):
                    for kt in range(m + 1):
                        mm = pe.matmul(un.view(f"o{m}")[:, h, :], aT[:, kt * HEADS + h, :], v[:, kt, h, :],
                                       start=(kt == 0), stop=(kt == m))
                mm.then_inc(un.filled(), 1)
            pe.wait_ge(*c.count("o_normed", TILES))
            turn(c, pe, o.rearrange("p m h n -> p m (h n)"))
            wait_turned_read(c, pe)
            c.products(pe, "w_o", c.xT, channel_major=False)

        @block.scalar
        def _(act):
            def read_qk(i, par, j, bank):
                return act.activation(qkT[:, bass.ds(8 * i + 4 * par + 2 * j, 2), :],
                                      c.ps[:, bank, :].rearrange("p (k t) -> p k t", k=2), ACT.Copy)
            c.evacuate(act, "qk", read_qk)

            def read_v(i, par, j, bank):
                q = 2 * i + par
                return act.activation(flat(v[:, j, 4 * q:4 * q + 4, :]), c.ps[:, bank, :], ACT.Copy)
            c.evacuate(act, "v", read_v)
            act.wait_ge(*c.count("lam_sums"))
            act.activation(lam[:, 2:4], lam[:, 0:2], ACT.Exp).then_inc(c.next("lam_exp"), 1)
            for m in range(TILES):
                keys = P * (m + 1)
                act.wait_ge(*c.count("s_less_top", m + 1))
                act.activation(s[:, :, 0:keys], s[:, :, 0:keys], ACT.Exp).then_inc(c.next("p"), 1)
                for kt in range(m + 1):
                    act.wait_ge(*un.full(f"a{m}.{kt}"))
                    act.activation(aT[:, kt * HEADS:(kt + 1) * HEADS, :], un.view(f"a{m}.{kt}"), ACT.Copy).then_inc(un.freed(f"a{m}.{kt}"), 1)
                act.wait_ge(*un.full(f"o{m}"))
                act.activation(o[:, m], un.view(f"o{m}"), ACT.Copy).then_inc(un.freed(f"o{m}"), 1)
                act.wait_ge(*un.read_out(f"o{m}"))
                norm_gate_act(c, act, o[:, m], stat, junk, m + 1)
            read_turned(c, act, c.xT, 0)

        @block.vector
        def _(dve):
            def step(ins):
                ins.then_inc(c.dve_chain.next(), 1)
                dve.wait_ge(*c.dve_chain.made())

            dve.wait_ge(*c.loaded.count(48))
            step(dve.tensor_tensor(bias[:, :, P:T], bias[:, :, P:T], spread(unseen, HEADS), ALU.add))
            both = lam_p.rearrange("p (a b) n -> p a b n", b=2)
            step(dve.tensor_tensor(lam_prod, both[:, :, 0, :], both[:, :, 1, :], ALU.mult))
            dve.tensor_reduce(lam[:, 0:2], lam_prod, AX_X, ALU.add).then_inc(c.next("lam_sums"), 1)
            dve.wait_ge(*c.count("lam_exp"))
            step(dve.tensor_tensor(lam[:, 0:1], lam[:, 3:4], lam[:, 2:3], ALU.subtract))
            step(dve.tensor_scalar(lam[:, 0:1], lam[:, 0:1], -LAMBDA_INIT, None, ALU.add))
            for m in range(TILES):
                keys = P * (m + 1)
                per = 8 // (m + 1)
                for n in range(2 * HEADS // per):
                    dve.wait_ge(*un.full(f"s{m}.{n}"))
                    if m and n == 0:
                        dve.wait_ge(*un.full("a0.0"))
                    out = un.view(f"s{m}.{n}", per).rearrange("p (s k) n -> p s k n", s=2)
                    for k in range(per // 2):
                        h = n * per // 2 + k
                        ins = dve.scalar_tensor_tensor(
                            out=s[:, 2 * h:2 * h + 2, 0:keys], in0=out[:, :, k, :], scalar=HEAD_DIM ** -0.5,
                            in1=spread(bias[:, h, T - keys:T], 2), op0=ALU.mult, op1=ALU.add)
                    ins.then_inc(un.freed(f"s{m}.{n}"), 1)
                for n in range(2 * HEADS // per)[-2:]:
                    dve.wait_ge(*un.read_out(f"s{m}.{n}"))
                now = s[:, :, 0:keys]
                step(dve.tensor_reduce(top, now, AX_X, ALU.max))
                dve.tensor_tensor(now, now, along(top, keys), ALU.subtract).then_inc(c.next("s_less_top"), 1)
                dve.wait_ge(*c.count("p", m + 1))
                step(dve.tensor_reduce(total, now, AX_X, ALU.add))
                step(dve.reciprocal(total, total))
                second = total.rearrange("p (h s) -> p h s", s=2)[:, :, 1]
                step(dve.tensor_scalar(second, second, lam[:, 0:1], None, ALU.mult))
                step(dve.tensor_tensor(now, now, along(total, keys), ALU.mult))
                by_head = now.rearrange("p (h s) k -> p h s k", s=2)
                dve.tensor_tensor(by_head[:, :, 0, :], by_head[:, :, 0, :], by_head[:, :, 1, :], ALU.add).then_inc(c.next("a"), 1)
                norm_gate_dve(c, dve, o[:, m], None, 2, stat, junk, m + 1, eps=LN_EPS)
                dve.tensor_scalar(o[:, m], o[:, m], 1.0 - LAMBDA_INIT, None, ALU.mult).then_inc(c.next("o_normed"), 1)

            def add(i, par, j, bank):
                q = 2 * i + par
                at = c.x[:, j, q * HALF:(q + 1) * HALF]
                return dve.scalar_tensor_tensor(out=at, in0=at, scalar=ALPHA, in1=c.ps[:, bank, :],
                                                op0=ALU.mult, op1=ALU.add)
            c.evacuate(dve, "w_o", add)
    un.close()
    c.turned.base += 4
    c.loaded.base += 48
    c.end_stage()



def build(nc, dram, out):
    with ExitStack() as ctx:
        c = Core(nc, ctx, dram)
        c.experts = Experts(c, ctx)
        norm(c, "rms_beside", None, first=True)
        project(c)
        for m in range(TILES):
            delta_rule(c, m)
            hgrn(c, m)
            branches(c, m)
            norm_of_tile(c, m)
            choose_experts(c, m)
        sum_experts(c)
        norm(c, "rms", "final_norm", turned=False)
        pooling(c)
        norm(c, "layer", "ln_mix_g0", "ln_mix_b0", eps=LN_EPS)
        feed_forward(c, 0)
        norm(c, "layer", "ln_ffn_g0", "ln_ffn_b0", eps=LN_EPS)
        attention(c)
        norm(c, "layer", "ln_mix_g1", "ln_mix_b1", eps=LN_EPS)
        feed_forward(c, 1)
        norm(c, "layer", "ln_ffn_g1", "ln_ffn_b1", eps=LN_EPS, store=out, turned=False)


def panel_columns(w):
    k, n = w.shape
    return w.reshape(k // P, P, n // HALF, HALF).transpose(2, 1, 0, 3).reshape(n // HALF, P, PANEL)


def laid_out(inputs):
    a = {n: np.asarray(v) for n, v in inputs.items()}
    w_in = a["w_in"][0]
    at = np.cumsum([0, D, D, D, HEADS, HEADS, D, D, D, D, D, D, D])
    q, k, v, beta, alpha, a_gate, b_f, b_i, b_q, b_gate, g_a, g_b = (slice(x, y) for x, y in zip(at[:-1], at[1:]))
    wall = [panel_columns(w_in[:, s]) for s in (q, k, v, a_gate, b_f, b_i, b_q, b_gate, g_a, g_b)]
    wall += [panel_columns(a[n][0]) for n in ("w_branch_a", "w_branch_b", "w_out", "w_pq")]

    def feed_forward(i):
        gate, up, down = (a[n][i] for n in ("w_gate_2", "w_up_2", "w_down_2"))
        both = np.stack([gate.reshape(D, FF_PANELS, 256), up.reshape(D, FF_PANELS, 256)], 2)
        padded = np.zeros((DOWN_PANELS * 4 * P, D), np.float32)
        padded[:D_FF] = down
        return [panel_columns(both.reshape(D, FF_PANELS * HALF)),
                padded.reshape(DOWN_PANELS, 4, P, D).transpose(0, 2, 1, 3).reshape(DOWN_PANELS, P, PANEL)]

    wall += feed_forward(0)
    wall += [panel_columns(a["w_qkv_2"][0]), panel_columns(a["w_o_2"][0])]
    wall += feed_forward(1)
    wall = np.concatenate(wall, 0)
    assert wall.shape[0] == WALL_PANELS
    on_all = lambda v: np.broadcast_to(v, (P,) + v.shape)
    rows = [a["b_lower_bound"][0], a["b_lower_bound"][1], a["norm2"][0], a["final_norm"], a["pool_scale_2"][0]]
    for i in range(2):
        rows += [a["ln_mix_g_2"][i], a["ln_mix_b_2"][i], a["ln_ffn_g_2"][i], a["ln_ffn_b_2"][i]]
    mats = constant_matrices()
    q_, k_ = np.meshgrid(np.arange(P), np.arange(T), indexing="ij")
    rel = P + q_ - k_
    table = a["rel_table_2"][rel_bucket(np.maximum(rel, 0))]
    return {
        "x": a["x"][0].reshape(TILES, P, D),
        "wall": wall,
        "mats": mats,
        "masks": (mats[:, MAT["level0"]:] > 0).astype(np.int32),
        "norm1": on_all(a["norm1"][0]),
        "onorms": np.stack([on_all(a["a_onorm"][0]), on_all(a["b_onorm"][0]), on_all(a["subln_g_2"][0])], 1),
        "w_bt": w_in[:, 3 * D:3 * D + 16].reshape(KC, P, 16).transpose(1, 0, 2),
        "w_conv": a["conv_a"][0].T.reshape(3 * HEADS, P, CONV_W).transpose(1, 0, 2),
        "a_log": on_all(a["a_log"][0]),
        "dt_bias": on_all(a["dt_bias"][0]),
        "rows": np.stack([on_all(r) for r in rows]),
        "sub_keys": a["sub_keys"][0].transpose(3, 1, 0, 2).reshape(P, 2 * P_HEADS, N_KEYS),
        "expert_u": a["expert_u"][0],
        "expert_v": a["expert_v"][0],
        "pool_m": pool_matrices(),
        "pool_w": a["pool_w_2"][0].reshape(4, 2, P, 256).transpose(2, 0, 1, 3),
        "rel_bias": table.transpose(0, 2, 1),
        "not_seen": np.where(rel[:, P:] < 0, MASKED, 0.0).astype(np.float32),
        "lam_p": on_all(a["lam_p_2"][0]),
        "iota": on_all(np.arange(TOPK, dtype=np.float32)),
    }


def kernel(**inputs):
    import concourse.bacc as bacc
    from concourse.bass_utils import run_bass_kernel_spmd

    nc = bacc.Bacc("TRN2", target_bir_lowering=False, num_devices=1)
    arrays = {n: np.ascontiguousarray(v) for n, v in laid_out(inputs).items()}
    dram = {n: nc.dram_tensor("in_" + n, v.shape, mybir.dt.from_np(v.dtype), kind="ExternalInput").ap()
            for n, v in arrays.items()}
    out = nc.dram_tensor("out", (TILES, P, D), F32, kind="ExternalOutput").ap()
    build(nc, dram, out)
    result = run_bass_kernel_spmd(nc, [{"in_" + n: v for n, v in arrays.items()}], core_ids=[0])
    return result.results[0]["out"].reshape(1, T, D)
```

```python
from contextlib import ExitStack

import numpy as np

import concourse.bass as bass
from concourse import mybir

F32 = mybir.dt.float32
I32 = mybir.dt.int32
U32 = mybir.dt.uint32
ALU = mybir.AluOpType
ACT = mybir.ActivationFunctionType
AX_X = mybir.AxisListType.X

P = 128
D = 1024
T = 256
TILES = T // P
KC = D // P
CHUNK = 64
HEADS = 8
DH = 128
EPS = 1e-6
CONV_W = 4
N_KEYS = 128
TOPK = 16
P_HEADS = 8
SLOTS = P_HEADS * TOPK
D_FF = 2816
FF_T = D_FF // P
LN_EPS = 1e-5
ALPHA = 4.0 ** 0.25
WINDOWS = (2, 4, 8, 16)
HEAD_DIM = 64
LAMBDA_INIT = 0.8 - 0.6 * float(np.exp(-0.3))
MASKED = -1e30
LOWEST = -3.0e38
MAIN = 35 * D
LEVELS = 6

PANEL = 4096
HALF = 512
FF_PANELS = FF_T // 2
DOWN_PANELS = -(-FF_T // 4)

WEIGHTS = [("conv", 6), ("a_gate", 2), ("b_f", 2), ("b_i", 2), ("b_q", 2), ("b_gate", 2), ("g_a", 2),
           ("g_b", 2), ("branch_a", 2), ("branch_b", 2), ("w_out", 2), ("w_pq", 4),
           ("ff0", FF_PANELS), ("down0", DOWN_PANELS), ("qk", 4), ("v", 2), ("w_o", 2),
           ("ff1", FF_PANELS), ("down1", DOWN_PANELS)]
BY_TILE = ("branch_a", "branch_b", "w_out", "w_pq")
_at = [x for x, _ in WEIGHTS].index(BY_TILE[0])
_one = WEIGHTS[_at:_at + len(BY_TILE)]
PLAN = (WEIGHTS[:_at] + [(f"{x}.{m}", n) for m in range(TILES) for x, n in _one]
        + WEIGHTS[_at + len(BY_TILE):])


def first_of(plan):
    first, total = {}, 0
    for name, n in plan:
        first[name] = total
        total += n
    return first, total


FIRST, N_PANELS = first_of(PLAN)
IN_WALL, WALL_PANELS = first_of(WEIGHTS)
COUNT = dict(PLAN)
WALL_AT = [IN_WALL[x.split(".")[0]] + q for x, n in PLAN for q in range(n)]
HALF_AT = {}
for _name, _n in PLAN:
    HALF_AT[_name] = sum(n for x, n in PLAN if FIRST[x] < FIRST[_name]
                         and not x.startswith("down") and "." not in x)
BESIDE = [(x, q, j) for x in ("b_f", "b_i", "b_q", "b_gate", "g_a", "g_b") for q in range(2) for j in range(2)]
BESIDE_DELTA = 16

MATS = (["ident", "upto", "after", "ones", "chunk0", "chunk1"]
        + [f"span{l}" for l in range(LEVELS)] + [f"level{l}" for l in range(LEVELS)])
MAT = {n: i for i, n in enumerate(MATS)}
ROWS = ["b_low0", "b_low1", "norm2", "final_norm", "pool_scale", "ln_mix_g0", "ln_mix_b0",
        "ln_ffn_g0", "ln_ffn_b0", "ln_mix_g1", "ln_mix_b1", "ln_ffn_g1", "ln_ffn_b1"]
ROW = {n: i for i, n in enumerate(ROWS)}


def constant_matrices():
    p, i = np.meshgrid(np.arange(P), np.arange(P), indexing="ij")
    same = p // CHUNK == i // CHUNK
    out = [p == i, same & (p <= i), same & (p > i), np.ones((P, P)), p < CHUNK, p >= CHUNK]
    spans, levels = [], []
    for l in range(LEVELS):
        s = 1 << l
        mid = i // (2 * s) * 2 * s + s
        right = i >= mid
        spans.append(np.where(right, (p >= mid) & (p <= i), (p > i) & (p < mid)))
        levels.append((p // (2 * s) == i // (2 * s)) & right & (p < mid))
    return np.stack([np.asarray(m, np.float32) for m in out + spans + levels], 1)


def pool_matrices():
    s, t = np.meshgrid(np.arange(T), np.arange(T), indexing="ij")
    groups = [((s <= t) & (s > t - w)) / np.minimum(t + 1, w) - (s == t) for w in WINDOWS]
    m = np.stack(groups, 1).astype(np.float32)
    return np.ascontiguousarray(m.reshape(TILES, P, len(WINDOWS), T).transpose(1, 0, 2, 3))


def rel_bucket(n):
    large = 16 + (np.log(np.maximum(n, 1) / 16) / np.log(8.0) * 16).astype(np.int64)
    return np.where(n < 16, n, np.minimum(large, 31))


PARTS = 10
GATE_A, Q_A, K_A, V_A, F_B, I_B, Q_B, GATE_B, MIX_A, MIX_B = range(PARTS)
SCRATCH = TILES * PARTS * D
STATE_A, STATE_B, KEPT_IN = 12, 13, 14
KEPT = SCRATCH + D * KEPT_IN
NORM_G, NORM_B = SCRATCH + 10 * D, SCRATCH + 11 * D
LOW_0, LOW_1 = KEPT, SCRATCH + D * STATE_B
POOL_AT = SCRATCH
RING = 8
H2, DIAGS = MIX_A, MIX_B


class Signal:

    def __init__(self, ctx, nc, name):
        self.sem = ctx.enter_context(nc.semaphore(name))
        self.base = 0

    def count(self, n):
        return self.sem, self.base + n


class Chain:

    def __init__(self, ctx, nc, name):
        self.sem = ctx.enter_context(nc.semaphore(name))
        self.n, self.turn = 0, 0

    def next(self):
        self.n += 1
        return self.sem

    def made(self, behind=0):
        return self.sem, self.turn + (self.n - behind)

    def begin(self, i, per_turn):
        self.start, self.per = self.n, per_turn
        self.turn = i * per_turn

    def end(self, turns):
        assert self.n - self.start == self.per, (self.n - self.start, self.per)
        self.turn = 0
        self.n = self.start + self.per * turns


def pairs(eng, n, body):
    if n // 2 > 1:
        with eng.Fori(0, n // 2) as i:
            body(i, 0)
            body(i, 1)
    else:
        for i in range(n // 2):
            body(i, 0)
            body(i, 1)
    if n % 2:
        body(n // 2, 0)


def spread(ap, n):
    return ap.unsqueeze(1).broadcast_to([ap.shape[0], n, ap.shape[1]])


def along(ap, n):
    return ap.unsqueeze(2).broadcast_to([ap.shape[0], ap.shape[1], n])


class Core:

    def __init__(self, nc, ctx, dram):
        self.nc, self.dram = nc, dram
        self.sb = lambda name, shape, dt=F32: ctx.enter_context(nc.sbuf_tensor(name, shape, dt))
        self.panels = self.sb("panels", [P, 2, PANEL])
        self.mats = self.sb("mats", [P, len(MATS), P])
        self.masks = self.sb("masks", [P, LEVELS, P], I32)
        self.x = self.sb("x", [P, TILES, D])
        self.xT = self.sb("xT", [P, KC, T])
        self.main = self.sb("main", [P, MAIN])
        self.small = self.sb("small", [P, 768])
        self.onorm = self.sb("onorm", [P, 3, DH])
        self.ps = ctx.enter_context(nc.psum_tensor("ps", [P, 8, HALF], F32))
        sig = lambda name: Signal(ctx, nc, name)
        self.panel_loaded = [sig("panel_loaded0"), sig("panel_loaded1")]
        self.half_done = sig("half_done")
        self.panel_done = sig("panel_done")
        self.bank_read = [sig(f"bank_read{b}") for b in range(4)]
        self.bank_uses = [1] * 4
        self.pair_full = [sig("pair_full0"), sig("pair_full1")]
        self.pair_read = [sig("pair_read0"), sig("pair_read1")]
        for p in self.pair_read:
            p.base = 1
        self.turned = sig("turned")
        self.loaded = sig("loaded")
        self.stored = sig("stored")
        self.x_loaded = sig("x_loaded")
        self.pool_loaded = sig("pool_loaded")
        self.ahead_loaded = sig("ahead_loaded")
        self.row_sums = self.sb("row_sums", [P, TILES, 2])
        self.named, self.raised = {}, {}
        self.act_chain = Chain(ctx, nc, "act_chain")
        self.dve_chain = Chain(ctx, nc, "dve_chain")
        self.w_bt = self.sb("w_bt", [P, KC, 16])
        self.w_conv = self.sb("w_conv", [P, 3 * HEADS, CONV_W])
        self.bt = self.sb("bt", [P, 32])
        self.ctx = ctx

    def next(self, name):
        if name not in self.named:
            self.named[name] = Signal(self.ctx, self.nc, name)
        self.raised[name] = self.raised.get(name, 0) + 1
        return self.named[name].sem

    def count(self, name, n=1):
        if name not in self.named:
            self.named[name] = Signal(self.ctx, self.nc, name)
        return self.named[name].count(n)

    def end_stage(self):
        for name, n in self.raised.items():
            self.named[name].base += n
        self.raised = {}

    def load_ahead(self, sp, dst, src):
        sp.dma_start(dst, src).then_inc(self.ahead_loaded.sem, 16)
        self.ahead_loaded.base += 16

    def load_norm_rows(self, sp, name):
        for at, row in ((NORM_G, f"ln_{name[:-1]}_g{name[-1]}"), (NORM_B, f"ln_{name[:-1]}_b{name[-1]}")):
            self.load_ahead(sp, self.area(at, D), self.dram["rows"][ROW[row]])

    def mat(self, name):
        return self.mats[:, MAT[name], :]

    def area(self, at, *shape):
        n = int(np.prod(shape))
        v = self.main[:, at:at + n]
        if len(shape) == 2:
            return v.rearrange("p (a b) -> p a b", a=shape[0])
        if len(shape) == 3:
            return v.rearrange("p (a b c) -> p a b c", a=shape[0], b=shape[1])
        return v

    def part(self, m, n):
        return self.area(PARTS * D * m + D * n, HEADS, P)

    def row(self, m, n):
        return self.area(PARTS * D * m + D * n, D)

    def stream(self, sp, name):
        first, n = FIRST[name] + 2, min(COUNT[name], N_PANELS - FIRST[name] - 2)
        wall = self.dram["wall"]
        at = WALL_AT[first:first + max(n, 0)]
        if n // 2 > 1 and at == list(range(at[0], at[0] + n)):
            pair = wall[at[0]:at[0] + n // 2 * 2].rearrange("(g s) p n -> g s p n", s=2)
            with sp.Fori(0, n // 2) as i:
                for par in range(2):
                    slot = (first + par) % 2
                    sp.wait_ge(self.panel_done.sem, 2 * i + (first + par - 1))
                    sp.dma_start(self.panels[:, slot, :], pair[i, par])\
                      .then_inc(self.panel_loaded[slot].sem, 16)
            loaded = n // 2 * 2
        else:
            loaded = 0
        for q in range(loaded, n):
            slot = (first + q) % 2
            sp.wait_ge(self.panel_done.sem, first + q - 1)
            sp.dma_start(self.panels[:, slot, :], wall[at[q]]).then_inc(self.panel_loaded[slot].sem, 16)

    def wait_panel(self, pe, name, i, par):
        first = FIRST[name]
        slot = (first + par) % 2
        pe.wait_ge(self.panel_loaded[slot].sem, 16 * i + 16 * ((first + par) // 2 + 1))
        return slot

    def products(self, pe, name, actT, channel_major):
        first = FIRST[name]
        base = list(self.bank_uses)

        def body(i, par):
            slot = self.wait_panel(pe, name, i, par)
            w = self.panels[:, slot, :].rearrange("p (k n) -> p k n", k=KC)
            for j in range(2):
                bank = 2 * slot + j
                pe.wait_ge(self.bank_read[bank].sem, i + base[bank])
                if channel_major:
                    for t in range(2):
                        for k in range(KC):
                            c = (2 * j + t) * P
                            mm = pe.matmul(self.ps[:, bank, t * T:(t + 1) * T], w[:, k, c:c + P],
                                           actT[:, k, :], start=(k == 0), stop=(k == KC - 1))
                else:
                    for k in range(KC):
                        mm = pe.matmul(self.ps[:, bank, :], actT[:, k, j * P:(j + 1) * P],
                                       w[:, k, :], start=(k == 0), stop=(k == KC - 1))
                mm.then_inc((self.half_done if j == 0 else self.panel_done).sem, 1)

        pairs(pe, COUNT[name], body)
        self._used(name)

    def _used(self, name):
        first = FIRST[name]
        for q in range(COUNT[name]):
            for j in range(2):
                self.bank_uses[2 * ((first + q) % 2) + j] += 1

    def product_beside(self, pe, n):
        name, q, j = BESIDE[n]
        slot = self.wait_panel(pe, name, q // 2, q % 2)
        w = self.panels[:, slot, :].rearrange("p (k n) -> p k n", k=KC)
        bank = 2 * slot + j
        pe.wait_ge(self.bank_read[bank].sem, self.bank_uses[bank])
        self.bank_uses[bank] += 1
        if name == "b_q":
            for t in range(2):
                for k in range(KC):
                    at = (2 * j + t) * P
                    mm = pe.matmul(self.ps[:, bank, t * T:(t + 1) * T], w[:, k, at:at + P],
                                   self.xT[:, k, :], start=(k == 0), stop=(k == KC - 1))
        else:
            for k in range(KC):
                mm = pe.matmul(self.ps[:, bank, :], self.xT[:, k, j * P:(j + 1) * P],
                               w[:, k, :], start=(k == 0), stop=(k == KC - 1))
        mm.then_inc((self.half_done if j == 0 else self.panel_done).sem, 1)

    def read_beside(self, act, n):
        name, q, j = BESIDE[n]
        bank = 2 * ((FIRST[name] + q) % 2) + j
        done = self.half_done if j == 0 else self.panel_done
        act.wait_ge(done.sem, (HALF_AT[name] if j == 0 else FIRST[name]) + q + 1)
        if name == "b_q":
            for m in range(TILES):
                src = self.ps[:, bank, :].rearrange("p (k m t) -> p k m t", k=2, m=TILES)[:, :, m, :]
                ins = act.activation(self.part(m, Q_B)[:, 4 * q + 2 * j:4 * q + 2 * j + 2, :], src, ACT.Silu)
        else:
            at, func = {"b_f": (F_B, ACT.Sigmoid), "b_i": (I_B, ACT.Copy), "b_gate": (GATE_B, ACT.Sigmoid),
                        "g_a": (MIX_A, ACT.Sigmoid), "g_b": (MIX_B, ACT.Sigmoid)}[name]
            ins = act.activation(self.row(j, at)[:, q * HALF:(q + 1) * HALF], self.ps[:, bank, :], func)
        ins.then_inc(self.bank_read[bank].sem, 1)

    def products_of_tile(self, pe, name, actT, channel_major, after=None):
        for q in range(COUNT[name]):
            slot = self.wait_panel(pe, name, q // 2, q % 2)
            w = self.panels[:, slot, :].rearrange("p (k n) -> p k n", k=KC)
            bank = 2 * slot
            pe.wait_ge(self.bank_read[bank].sem, self.bank_uses[bank])
            self.bank_uses[bank] += 1
            if channel_major:
                for t in range(4):
                    for k in range(KC):
                        mm = pe.matmul(self.ps[:, bank, t * P:(t + 1) * P], w[:, k, t * P:(t + 1) * P],
                                       actT[:, k, :], start=(k == 0), stop=(k == KC - 1))
            else:
                for k in range(KC):
                    mm = pe.matmul(self.ps[:, bank, :], actT[:, k, :], w[:, k, :],
                                   start=(k == 0), stop=(k == KC - 1))
            mm.then_inc(self.panel_done.sem, 1)
            if after:
                after()

    def evacuate(self, eng, name, read, halves=(0, 1)):
        first = FIRST[name]

        def body(i, par):
            slot = (first + par) % 2
            for j in halves:
                done = self.half_done if j == 0 else self.panel_done
                base = HALF_AT[name] if j == 0 else first
                eng.wait_ge(done.sem, 2 * i + (base + par + 1))
                read(i, par, j, 2 * slot + j).then_inc(self.bank_read[2 * slot + j].sem, 1)

        pairs(eng, COUNT[name], body)



def turn(c, pe, src):
    for n in range(4):
        pe.wait_ge(c.bank_read[n].sem, c.bank_uses[n])
        c.bank_uses[n] += 1
        for k in range(2):
            for m in range(TILES):
                at = (2 * n + k) * P
                mm = pe.transpose(c.ps[:, n, k * T + m * P:k * T + (m + 1) * P],
                                  src[:, m, at:at + P], c.mat("ident"))
        mm.then_inc(c.turned.sem, 1)


def turn_tile(c, pe, src):
    for n in (0, 2):
        pe.wait_ge(c.bank_read[n].sem, c.bank_uses[n])
        c.bank_uses[n] += 1
        for k in range(4):
            at = (2 * n + k) * P
            mm = pe.transpose(c.ps[:, n, k * P:(k + 1) * P], src[:, at:at + P], c.mat("ident"))
        mm.then_inc(c.turned.sem, 1)


def read_turned_tile(c, act, dst, nth):
    for n in (0, 2):
        act.wait_ge(*c.turned.count(2 * nth + n // 2 + 1))
        act.activation(dst[:, 2 * n:2 * n + 4, :], c.ps[:, n, :].rearrange("p (k t) -> p k t", k=4),
                       ACT.Copy).then_inc(c.bank_read[n].sem, 1)


def wait_turned_tile_read(c, pe):
    for n in (0, 2):
        pe.wait_ge(c.bank_read[n].sem, c.bank_uses[n])


def read_turned(c, eng, dst, nth):
    for n in range(4):
        eng.wait_ge(*c.turned.count(4 * nth + n + 1))
        out = dst[:, 2 * n:2 * n + 2, :].rearrange("p k t -> p (k t)")
        eng.activation(out, c.ps[:, n, :], ACT.Copy).then_inc(c.bank_read[n].sem, 1)


def wait_turned_read(c, pe):
    for n in range(4):
        pe.wait_ge(c.bank_read[n].sem, c.bank_uses[n])


def layer_norm(c, parts, store=None):
    nc = c.nc
    centred, squared = c.area(8 * D, TILES, D), c.area(10 * D, TILES, D)
    g, b = c.area(NORM_G, D), c.area(NORM_B, D)
    stat = c.small[:, 0:16]
    neg_mean, squares, variance, root, scale = (stat[:, 2 * n:2 * n + 2] for n in range(5))
    with nc.Block() as block:
        @block.sync
        def _(sp):
            if store is not None:
                for m in range(TILES):
                    sp.wait_ge(*c.count("normed", m + 1))
                    sp.dma_start(store[m], c.x[:, m, :]).then_inc(c.stored.sem, 16)
                sp.wait_ge(*c.stored.count(16 * TILES))

        @block.scalar
        def _(act):
            act.wait_ge(*c.count("neg_mean"))
            for m in range(TILES):
                act.activation(squared[:, m, :], c.x[:, m, :], ACT.Square, bias=neg_mean[:, m:m + 1],
                               accum_out=squares[:, m:m + 1]).then_inc(c.next("square"), 1)
            act.wait_ge(*c.count("variance"))
            act.activation(root, variance, ACT.Sqrt).then_inc(c.next("root"), 1)
            if store is None:
                read_turned(c, act, c.xT, 0)

        @block.vector
        def _(dve):
            sums = c.row_sums[:, :, 0]
            if parts == 2:
                dve.tensor_tensor(sums, sums, c.row_sums[:, :, 1], ALU.add).then_inc(c.dve_chain.next(), 1)
                dve.wait_ge(*c.dve_chain.made())
            dve.tensor_scalar(neg_mean, sums, -1.0 / D, None, ALU.mult).then_inc(c.next("neg_mean"), 1)
            dve.wait_ge(*c.count("neg_mean"))
            dve.wait_ge(*c.ahead_loaded.count(0))
            for m in range(TILES):
                dve.scalar_tensor_tensor(out=centred[:, m, :], in0=c.x[:, m, :], scalar=neg_mean[:, m:m + 1],
                                         in1=g, op0=ALU.add, op1=ALU.mult).then_inc(c.dve_chain.next(), 1)
            dve.wait_ge(*c.count("square", TILES))
            dve.tensor_scalar(variance, squares, 1.0 / D, LN_EPS, ALU.mult, ALU.add).then_inc(c.next("variance"), 1)
            dve.wait_ge(*c.count("root"))
            dve.reciprocal(scale, root).then_inc(c.dve_chain.next(), 1)
            dve.wait_ge(*c.dve_chain.made())
            for m in range(TILES):
                dve.scalar_tensor_tensor(out=c.x[:, m, :], in0=centred[:, m, :], scalar=scale[:, m:m + 1],
                                         in1=b, op0=ALU.mult, op1=ALU.add).then_inc(c.next("normed"), 1)

        @block.tensor
        def _(pe):
            if store is None:
                for m in range(TILES):
                    pe.wait_ge(*c.count("normed", m + 1))
                turn(c, pe, c.x)
    if store is not None:
        c.stored.base += 16 * TILES
    else:
        c.turned.base += 4
    c.end_stage()


def rms_norm(c, first=False):
    nc = c.nc
    g, squared = c.area(NORM_G, D), c.area(10 * D, TILES, D)
    out = c.area(6 * D, TILES, D) if first else c.x
    row_in = c.ahead_loaded.base
    stat = c.small[:, 0:16]
    squares, variance, root, scale = (stat[:, 2 * n:2 * n + 2] for n in range(4))
    loads = 16 * 4 if first else 0
    with nc.Block() as block:
        @block.sync
        def _(sp):
            if first:
                for m in range(TILES):
                    sp.dma_start(c.x[:, m, :], c.dram["x"][m]).then_inc(c.x_loaded.sem, 16)
                sp.dma_start(g, c.dram["norm1"]).then_inc(c.loaded.sem, 16)
                sp.dma_start(c.mat("ident"), c.dram["mats"][:, MAT["ident"], :]).then_inc(c.loaded.sem, 16)
                sp.dma_start(c.w_conv[:, :, :], c.dram["w_conv"]).then_inc(c.loaded.sem, 16)
                sp.dma_start(c.w_bt[:, :, :], c.dram["w_bt"]).then_inc(c.loaded.sem, 16)
                for n in range(2):
                    sp.dma_start(c.panels[:, n, :], c.dram["wall"][n]).then_inc(c.panel_loaded[n].sem, 16)
            else:
                for dst, src in ((c.area(POOL_AT, TILES * len(WINDOWS), T),
                                  c.dram["pool_m"].rearrange("p m g t -> p (m g) t")),
                                 (c.area(POOL_AT + 8 * T, 2 * len(WINDOWS), 2 * P),
                                  c.dram["pool_w"].rearrange("p g k n -> p (g k) n")),
                                 (c.area(POOL_AT + 8 * T + 16 * P, D), c.dram["rows"][ROW["pool_scale"]])):
                    sp.dma_start(dst, src).then_inc(c.pool_loaded.sem, 16)

        @block.scalar
        def _(act):
            if first:
                for n in range(4):
                    act.sem_inc(c.bank_read[n].sem, 1)
                for n in range(2):
                    act.sem_inc(c.pair_read[n].sem, 1)
                act.wait_ge(*c.x_loaded.count(16 * TILES))
            for m in range(TILES):
                act.activation(squared[:, m, :], c.x[:, m, :], ACT.Square,
                               accum_out=squares[:, m:m + 1]).then_inc(c.next("square"), 1)
            act.wait_ge(*c.count("variance"))
            act.activation(root, variance, ACT.Sqrt).then_inc(c.next("root"), 1)
            if first:
                read_turned(c, act, c.xT, 0)

        @block.vector
        def _(dve):
            dve.wait_ge(*c.count("square", TILES))
            dve.tensor_scalar(variance, squares, 1.0 / D, EPS, ALU.mult, ALU.add).then_inc(c.next("variance"), 1)
            dve.wait_ge(*c.count("root"))
            dve.reciprocal(scale, root).then_inc(c.dve_chain.next(), 1)
            dve.wait_ge(*c.dve_chain.made())
            if first:
                dve.wait_ge(*c.loaded.count(loads))
            else:
                dve.wait_ge(c.ahead_loaded.sem, row_in)
            for m in range(TILES):
                dve.scalar_tensor_tensor(out=out[:, m, :], in0=c.x[:, m, :], scalar=scale[:, m:m + 1],
                                         in1=g, op0=ALU.mult, op1=ALU.mult).then_inc(c.next("normed"), 1)

        @block.tensor
        def _(pe):
            if first:
                pe.wait_ge(*c.loaded.count(loads))
                for m in range(TILES):
                    pe.wait_ge(*c.count("normed", m + 1))
                turn(c, pe, out)
    c.loaded.base += loads
    if first:
        c.turned.base += 4
    c.end_stage()



def project(c):
    nc = c.nc
    raw = c.area(SCRATCH, 3 * HEADS, T + 4)
    main = c.main[:, 0:SCRATCH].rearrange("p (m n t) -> p m n t", m=TILES, t=P)
    pair = c.ps[:, 4, 0:32]
    read_base = list(c.bank_uses)
    with nc.Block() as block:
        @block.sync
        def _(sp):
            c.stream(sp, "conv")
            sp.dma_start(c.mats[:, 1:, :], c.dram["mats"][:, 1:, :]).then_inc(c.loaded.sem, 16)
            sp.dma_start(c.masks[:, :, :], c.dram["masks"]).then_inc(c.loaded.sem, 16)
            sp.dma_start(c.onorm[:, :, :], c.dram["onorms"]).then_inc(c.loaded.sem, 16)
            c.stream(sp, "a_gate")

        @block.tensor
        def _(pe):
            c.products(pe, "conv", c.xT, channel_major=True)
            for m in range(TILES):
                for k in range(KC):
                    mm = pe.matmul(pair[:, 16 * m:16 * m + 16], c.xT[:, k, m * P:(m + 1) * P],
                                   c.w_bt[:, k, :], start=(k == 0), stop=(k == KC - 1))
            mm.then_inc(c.next("bt_done"), 1)
            c.products(pe, "a_gate", c.xT, channel_major=False)

        @block.scalar
        def _(act):
            act.wait_ge(*c.count("zeros"))

            def read_conv(i, par, j, bank):
                return act.activation(raw[:, bass.ds(8 * i + 4 * par + 2 * j, 2), 3:3 + T],
                                      c.ps[:, bank, :].rearrange("p (k t) -> p k t", k=2), ACT.Copy)
            c.evacuate(act, "conv", read_conv)
            act.wait_ge(*c.count("bt_done"))
            act.activation(c.bt[:, :], pair, ACT.Copy).then_inc(c.next("bt"), 1)
            act.wait_ge(*c.count("conv"))
            for m in range(TILES):
                v = c.area(PARTS * D * m + D * Q_A, 3 * D)
                act.activation(v, v, ACT.Silu).then_inc(c.act_chain.next(), 1)

            def read_gate(i, par, j, bank):
                q = 2 * i + par
                return act.activation(c.row(j, GATE_A)[:, q * HALF:(q + 1) * HALF], c.ps[:, bank, :], ACT.Silu)
            c.evacuate(act, "a_gate", read_gate)

        @block.vector
        def _(dve):
            dve.memset(raw[:, :, 0:3], 0.0).then_inc(c.next("zeros"), 1)

            def conv(i, par):
                slot = (FIRST["conv"] + par) % 2
                for j in range(2):
                    bank = 2 * slot + j
                    dve.wait_ge(c.bank_read[bank].sem, i + (read_base[bank] + 1))
                    at = 8 * i + 4 * par + 2 * j
                    for tap in range(CONV_W):
                        for t in range(2):
                            w = c.w_conv[:, bass.ds(at + t, 1), tap:tap + 1].rearrange("p a b -> p (a b)")
                            out = main[:, :, bass.ds(at + (HEADS * Q_A + t), 1), :].rearrange("p m a t -> p m (a t)")
                            src = raw[:, bass.ds(at + t, 1), tap:tap + T].rearrange("p a (m t) -> p (a m) t", m=TILES)
                            if tap == 0:
                                ins = dve.tensor_scalar(out, src, w, None, ALU.mult)
                            else:
                                dve.wait_ge(*c.dve_chain.made(behind=1))
                                ins = dve.scalar_tensor_tensor(out=out, in0=src, scalar=w, in1=out,
                                                               op0=ALU.mult, op1=ALU.add)
                            ins.then_inc(c.dve_chain.next(), 1)

            with dve.Fori(0, COUNT["conv"] // 2) as i:
                c.dve_chain.begin(i, 4 * 2 * CONV_W)
                for par in range(2):
                    conv(i, par)
            c.dve_chain.end(COUNT["conv"] // 2)
            dve.wait_ge(*c.dve_chain.made())
            dve.memset(c.small[:, 700:701], 0.0).then_inc(c.next("conv"), 1)
            dve.wait_ge(*c.loaded.count(48))
    c.loaded.base += 48
    c.end_stage()


class Units:

    def __init__(self, c, names):
        self.c, self.names = c, list(names)
        self.at = {x: i for i, x in enumerate(self.names)}
        assert len(self.at) == len(self.names)
        self.n = 0

    def bank(self, name):
        return 4 + 2 * (self.at[name] % 2)

    def view(self, name, groups=HEADS):
        b = self.bank(name)
        return self.c.ps[:, b:b + 2, :].rearrange("p b (g n) -> p (b g) n", g=groups // 2)

    def emptied(self, name):
        assert self.names[self.n] == name, (name, self.names[self.n])
        u = self.at[name]
        return self.c.pair_read[u % 2].count(u // 2)

    def filled(self):
        u, self.n = self.n, self.n + 1
        return self.c.pair_full[u % 2].sem

    def full(self, name):
        u = self.at[name]
        return self.c.pair_full[u % 2].count(u // 2 + 1)

    def freed(self, name):
        return self.c.pair_read[self.at[name] % 2].sem

    def read_out(self, name):
        u = self.at[name]
        return self.c.pair_read[u % 2].count(u // 2 + 1)

    def close(self):
        n = len(self.names)
        assert self.n == n, (self.n, n)
        for p in range(2):
            self.c.pair_full[p].base += (n + 1 - p) // 2
            self.c.pair_read[p].base += (n + 1 - p) // 2


def norm_gate_act(c, act, o, stat, squared, turn_no):
    act.activation(squared, o, ACT.Square).then_inc(c.next("o_squares"), 1)
    act.wait_ge(*c.count("o_mean", turn_no))
    act.activation(stat[:, 16:24], stat[:, 8:16], ACT.Sqrt).then_inc(c.next("o_root"), 1)


def norm_gate_dve(c, dve, o, gate, which, stat, squared, turn_no, eps=EPS):
    def step(ins):
        ins.then_inc(c.dve_chain.next(), 1)
        dve.wait_ge(*c.dve_chain.made())

    dve.wait_ge(*c.count("o_squares", turn_no))
    step(dve.tensor_reduce(stat[:, 0:8], squared, AX_X, ALU.add))
    dve.tensor_scalar(stat[:, 8:16], stat[:, 0:8], 1.0 / DH, eps, ALU.mult, ALU.add).then_inc(c.next("o_mean"), 1)
    step(dve.tensor_tensor(o, o, spread(c.onorm[:, which, :], HEADS), ALU.mult))
    dve.wait_ge(*c.count("o_root", turn_no))
    step(dve.reciprocal(stat[:, 24:32], stat[:, 16:24]))
    step(dve.tensor_tensor(o, o, along(stat[:, 24:32], DH), ALU.mult))
    if gate is not None:
        step(dve.tensor_tensor(gate, gate, o, ALU.mult))


ROWS_BESIDE_DELTA = 80
ROWS_BESIDE_HGRN = 48
ROWS_BESIDE_BRANCHES = 24
ROWS_BESIDE_CHOICE = 64
PART_OF_DVE = 4
PHASES = []
for _m, _count in ((0, SLOTS), (1, SLOTS)):
    for _q in range(0, SLOTS, _count):
        for _table in ("expert_u", "expert_v"):
            PHASES.append((_table, _m, _q, _count, sum(p[3] for p in PHASES)))


class Experts:

    def __init__(self, c, ctx):
        nc = c.nc
        self.c = c
        self.ring = [c.row(0, n) for n in range(RING)]
        self.diags = [c.row(0, DIAGS)[:, P * n:P * (n + 1)] for n in range(RING)]
        self.experts, self.gates, self.dots_at, self.weights = (
            c.area(KEPT + 256 * n, TILES, SLOTS) for n in range(4))
        self.now = [c.sb(f"numbers_now{n}", [P, 4], U32) for n in range(2)]
        sem = lambda name: ctx.enter_context(nc.semaphore(name))
        self.row_used, self.row_summed, self.diag_made = sem("row_used"), sem("row_summed"), sem("diag_made")
        self.numbers, self.groups_begun = sem("numbers"), sem("groups_begun")
        self.gelu_made, self.weights_made = sem("gelu_made"), sem("weights_made")
        self.row_in = [sem(f"row_in{n}") for n in range(RING)]
        self.end = 0
        self.row = {"pool": 0, "dve": 0, "pe": 0, "act": 0}

    def phase(self, r):
        return next(n for n, p in enumerate(PHASES) if p[4] <= r < p[4] + p[3])

    def at(self, r):
        table, m, q, _, start = PHASES[self.phase(r)]
        return table == "expert_v", m, q + r - start, r - start

    def of_dve(self, r):
        before = 0
        for table, _, _, count, start in PHASES:
            n = min(max(r - start, 0), count)
            before += n if table == "expert_u" else -(-n // PART_OF_DVE)
        return before

    def of_pe(self, r):
        return r - self.of_dve(r)

    def steps(self, r):
        return (RING // PART_OF_DVE, RING - RING // PART_OF_DVE) if self.at(r)[0] else (RING, 0)

    def sums_before(self, r):
        return sum(p[0] == "expert_v" for p in PHASES[:self.phase(r)])

    def begin_stage(self, rows):
        self.end += rows

    def fetch(self, pool, turns):
        end = self.row["pool"] + RING * turns
        while self.row["pool"] < end:
            r = self.row["pool"]
            place, count = self.at(r)[3], PHASES[self.phase(r)][3]
            n = min(end - r, count - place) // RING
            if place < RING or n == 1:
                self.fetch_turn(pool, 0)
            else:
                with pool.Fori(0, n) as i:
                    self.fetch_turn(pool, i)
                self.row["pool"] += RING * (n - 1)

    def fetch_turn(self, pool, i):
        for half in range(2):
            r = self.row["pool"]
            summed, m, q, _ = self.at(r)
            dve_rows, pe_rows = self.steps(r)
            if r >= RING:
                pool.wait_ge(self.row_used, dve_rows * i + self.of_dve(r - 4))
                if self.of_pe(r - 4):
                    pool.wait_ge(self.row_summed, pe_rows * i + self.of_pe(r - 4))
            ins = pool.tensor_copy(self.now[half][:, :],
                                   self.experts[:, m, bass.ds(RING * i + q, 4)].bitcast(U32))
            ins.then_inc(self.numbers, 1)
            pool.wait_ge(self.numbers, 2 * i + (r // 4 + 1))
            pool.sem_inc(self.groups_begun, 1)
            for s in range(4):
                pool.indirect_dma_start(
                    out=self.ring[r % RING + s], out_offset=None,
                    in_=self.c.dram["expert_v" if summed else "expert_u"],
                    in_offset=bass.IndirectOffsetOnAxis(ap=self.now[half][:, s:s + 1], axis=0),
                ).then_inc(self.row_in[r % RING + s], 16)
            self.row["pool"] += 4

    def dve_steps(self, dve, n):
        for _ in range(n):
            if self.row["dve"] < self.end:
                self.dve_step(dve, 0)

    def dve_step(self, dve, i):
        r = self.row["dve"]
        summed, m, q, place = self.at(r)
        s, by = r % RING, bass.ds(RING * i + q, 1)
        row = self.ring[s]
        if summed and place == 0:
            dve.wait_ge(self.gelu_made, self.sums_before(r) + 1)
            cols = slice(q, q + PHASES[self.phase(r)][3])
            dve.tensor_tensor(self.weights[:, m, cols], self.weights[:, m, cols], self.gates[:, m, cols],
                              ALU.mult).then_inc(self.weights_made, 1)
            dve.wait_ge(self.weights_made, self.sums_before(r) + 1)
        dve.wait_ge(self.row_in[s], 16 * i + 16 * (r // RING + 1))
        if not summed:
            dve.scalar_tensor_tensor(out=row, in0=row, scalar=1.0, in1=self.c.row(m, H2), op0=ALU.mult,
                                     op1=ALU.mult, accum_out=self.dots_at[:, m, by]).then_inc(self.row_used, 1)
            self.row["dve"] += 1
            return
        y, row = self.y(m), row.rearrange("p (a b) -> p a b", b=P)
        if q == 0:
            ins = dve.tensor_scalar(y, row, self.weights[:, m, by], None, ALU.mult)
        else:
            dve.wait_ge(self.row_used, self.steps(r)[0] * i + self.of_dve(r))
            ins = dve.scalar_tensor_tensor(out=y, in0=row, scalar=self.weights[:, m, by], in1=y,
                                           op0=ALU.mult, op1=ALU.add)
        ins.then_inc(self.row_used, 1)
        self.row["dve"] += PART_OF_DVE

    def y(self, m):
        return self.c.xT[:, :, m * P:(m + 1) * P]

    def row_of(self, engine):
        r = self.row[engine]
        if engine != "dve" and r < PHASES[-1][3] + PHASES[-1][4]:
            if not self.at(r)[0]:
                start, count = PHASES[self.phase(r)][4], PHASES[self.phase(r)][3]
                r = start + count
            r += r % PART_OF_DVE == 0
        self.row[engine] = r
        return r

    def diagonals(self, act, n):
        for _ in range(n):
            if self.row_of("act") < self.end:
                self.diagonal(act, 0)

    def diagonal(self, act, i):
        r = self.row_of("act")
        _, m, q, place = self.at(r)
        if place == 1:
            act.wait_ge(self.row_used, self.of_dve(r - 1))
            cols = slice(q - 1, q - 1 + PHASES[self.phase(r)][3])
            act.activation(self.weights[:, m, cols], self.dots_at[:, m, cols], ACT.Gelu).then_inc(self.gelu_made, 1)
            act.wait_ge(self.weights_made, self.sums_before(r) + 1)
        used = self.of_pe(r - place if place < RING else r - RING + 1)
        if used:
            act.wait_ge(self.row_summed, 6 * i + used)
        act.activation(self.diags[r % RING], self.c.mat("ident"), ACT.Copy,
                       scale=self.weights[:, m, bass.ds(RING * i + q, 1)]).then_inc(self.diag_made, 1)
        self.row["act"] += 1

    def sums(self, pe, n):
        for _ in range(n):
            if self.row_of("pe") < self.end:
                self.sum(pe, 0)

    def sum(self, pe, i):
        r = self.row_of("pe")
        q, s = self.at(r)[2], r % RING
        pe.wait_ge(self.row_in[s], 16 * i + 16 * (r // RING + 1))
        pe.wait_ge(self.diag_made, 6 * i + (self.of_pe(r) + 1))
        for half in range(2):
            mm = pe.matmul(self.c.ps[:, 1 + 2 * half, :], self.diags[s], self.ring[s][:, half * HALF:(half + 1) * HALF],
                           start=(q == 1), stop=(q == SLOTS - 1))
        mm.then_inc(self.row_summed, 1)
        self.row["pe"] += 1

    def rest(self, eng, engine, step, end):
        first = 0 if engine == "dve" else 1
        while self.row_of(engine) < end:
            r = self.row_of(engine)
            _, _, q, place = self.at(r)
            count = PHASES[self.phase(r)][3]
            turns = min(end - r + first, count - place + first) // RING
            if q - place + count == SLOTS:
                turns -= 1
            if place < RING or r % RING != first or turns < 2:
                step(eng, 0)
                continue
            of_dve, of_pe = self.steps(r)
            with eng.Fori(0, turns) as i:
                for _ in range(of_dve if engine == "dve" else of_pe):
                    step(eng, i)
            self.row[engine] += RING * (turns - 1)


def sum_experts(c):
    nc, rows_of = c.nc, c.experts
    ends = [2 * SLOTS * (m + 1) for m in range(TILES)]
    left = ends[-1] - rows_of.end
    rows_of.begin_stage(left)
    with nc.Block() as block:
        @block.sync
        def _(sp):
            c.load_ahead(sp, c.area(NORM_G, D), c.dram["rows"][ROW["final_norm"]])

        @block.gpsimd
        def _(pool):
            rows_of.fetch(pool, left // RING)

        @block.scalar
        def _(act):
            rows_of.rest(act, "act", rows_of.diagonal, ends[-1])

        @block.tensor
        def _(pe):
            rows_of.rest(pe, "pe", rows_of.sum, ends[0])
            pe.wait_ge(*c.count("sum_read", 2))
            rows_of.rest(pe, "pe", rows_of.sum, ends[1])

        @block.vector
        def _(dve):
            for m in range(TILES):
                rows_of.rest(dve, "dve", rows_of.dve_step, ends[m])
                dve.wait_ge(rows_of.row_used, rows_of.of_dve(ends[m]))
                dve.wait_ge(rows_of.row_summed, rows_of.of_pe(ends[m]))
                x = c.x[:, m, :].rearrange("p (a b) -> p a b", b=P)
                dve.tensor_tensor(x, x, rows_of.y(m), ALU.add).then_inc(c.dve_chain.next(), 1)
                dve.wait_ge(*c.dve_chain.made())
                for half in range(2):
                    x = c.x[:, m, half * HALF:(half + 1) * HALF]
                    dve.tensor_tensor(x, x, c.ps[:, 1 + 2 * half, :], ALU.add).then_inc(c.next("sum_read"), 1)
    c.end_stage()


def delta_rule(c, m):
    nc, rows_of = c.nc, c.experts
    gate = c.part(m, GATE_A)
    qT, kT, vT = (c.part(m, a) for a in (Q_A, K_A, V_A))
    slot = lambda n: c.area(SCRATCH + D * n, HEADS, P)
    v_t, k_t, g_run, decay, N, a_qk, q_dec, X, Y, PX, N_l, u = (slot(n) for n in range(12))
    S = slot(STATE_A)
    b_diag = N_l
    kb, wT = g_run, decay
    o, v_new, k_dec = u, v_t, k_t
    both = c.area(PARTS * D * m + D * Q_A, 2 * D)
    sq, root = c.area(SCRATCH, 2 * D), c.area(SCRATCH + 2 * D, 2 * D)
    sm = c.small
    beta, z, z_abs, lnp, g = (sm[:, 16 * n:16 * n + 16].rearrange("p (m h) -> p m h", m=TILES)
                              for n in range(5))
    neg_a, a_log, dt_bias = sm[:, 80:88], sm[:, 256:264], sm[:, 264:272]
    e_g = sm[:, 96:128]
    bg, stat = sm[:, 160:168], sm[:, 176:208]
    bt = c.bt[:, :].rearrange("p (m n) -> p m n", m=TILES)
    rows = lambda ch: slice(CHUNK * ch, CHUNK * (ch + 1))
    beside = m == 0

    names = ["k_t", "v_t", "decay", "g_cols", "g_rows", "kk", "beta", "qk"]
    for l in range(LEVELS):
        names += [f"P{l}"] + ([f"X{l}"] if 0 < l < LEVELS - 1 else []) + ([f"Y{l}"] if l else [])
    names += ["u", "w"] + [f"{x}.{n}" for n in range(2) for x in ("ws", "o", "s")]
    un = Units(c, names)

    rows_of.begin_stage(ROWS_BESIDE_DELTA if m else 0)
    with nc.Block() as block:
        @block.sync
        def _(sp):
            if m == 0:
                sp.dma_start(a_log, c.dram["a_log"]).then_inc(c.loaded.sem, 16)
                sp.dma_start(dt_bias, c.dram["dt_bias"]).then_inc(c.loaded.sem, 16)
                c.load_ahead(sp, c.area(LOW_0, D), c.dram["rows"][ROW["b_low0"]])
                c.load_ahead(sp, c.area(LOW_1, D), c.dram["rows"][ROW["b_low1"]])
                for name in ("b_f", "b_i", "b_q", "b_gate"):
                    c.stream(sp, name)

        if m:
            @block.gpsimd
            def _(pool):
                rows_of.fetch(pool, ROWS_BESIDE_DELTA // RING)

        @block.scalar
        def _(act):
            act.activation(sq, both, ACT.Square).then_inc(c.next("squares"), 1)
            if m == 0:
                act.activation(beta, bt[:, :, 0:8], ACT.Sigmoid).then_inc(c.next("beta"), 1)
                act.wait_ge(*c.count("z_abs"))
                act.activation(lnp, z_abs, ACT.Exp, scale=-1.0).then_inc(c.act_chain.next(), 1)
                act.wait_ge(*c.act_chain.made())
                act.activation(lnp, lnp, ACT.Ln, bias=1.0).then_inc(c.next("ln"), 1)
                act.wait_ge(*c.loaded.count(32))
                act.activation(neg_a, a_log, ACT.Exp).then_inc(c.next("exp_a"), 1)
            if beside:
                c.read_beside(act, 0)
            act.wait_ge(*c.count("norms"))
            act.activation(root, c.ps[:, 4:8, :].rearrange("p b n -> p (b n)"),
                           ACT.Sqrt, bias=EPS).then_inc(c.next("norm_root"), 1)
            if beside:
                c.read_beside(act, 1)
            act.wait_ge(*un.full("k_t"))
            act.activation(k_t, un.view("k_t"), ACT.Copy).then_inc(un.freed("k_t"), 1)
            act.wait_ge(*un.full("decay"))
            act.activation(decay, un.view("decay"), ACT.Exp).then_inc(un.freed("decay"), 1)
            act.wait_ge(*un.full("g_cols"))
            act.activation(q_dec, un.view("g_cols"), ACT.Exp).then_inc(un.freed("g_cols"), 1)
            act.wait_ge(*un.full("g_rows"))
            act.activation(e_g, un.view("g_rows", 2)[:, 0, 0:32], ACT.Exp).then_inc(un.freed("g_rows"), 1)
            for l in range(LEVELS):
                act.wait_ge(*un.full(f"P{l}"))
                act.activation(PX, un.view(f"P{l}"), ACT.Copy).then_inc(un.freed(f"P{l}"), 1)
                if beside:
                    c.read_beside(act, 2 + 2 * l)
                    c.read_beside(act, 3 + 2 * l)
                elif l in (1, 2, 4, 5):
                    rows_of.diagonals(act, 6)
            act.wait_ge(*un.full("u"))
            act.activation(u, un.view("u"), ACT.Copy).then_inc(un.freed("u"), 1)
            act.wait_ge(*un.full("w"))
            act.activation(wT, un.view("w"), ACT.Copy).then_inc(un.freed("w"), 1)
            for ch in range(2):
                r = rows(ch)
                if beside:
                    c.read_beside(act, 14 + ch)
                act.wait_ge(*un.full(f"o.{ch}"))
                act.wait_ge(*un.read_out(f"ws.{ch}"))
                act.activation(o[r], un.view(f"o.{ch}")[r], ACT.Copy).then_inc(un.freed(f"o.{ch}"), 1)
            for ch in range(2):
                act.wait_ge(*un.read_out(f"o.{ch}"))
            norm_gate_act(c, act, o, stat, PX, 1)

        @block.vector
        def _(dve):
            def step(ins):
                ins.then_inc(c.dve_chain.next(), 1)
                dve.wait_ge(*c.dve_chain.made())

            def dots(n):
                if m:
                    rows_of.dve_steps(dve, n)

            if m == 0:
                dve.wait_ge(*c.loaded.count(32))
                step(dve.tensor_tensor(z, bt[:, :, 8:16], spread(dt_bias, TILES), ALU.add))
                dve.scalar_tensor_tensor(out=z_abs, in0=z, scalar=-1.0, in1=z,
                                         op0=ALU.mult, op1=ALU.max).then_inc(c.next("z_abs"), 1)
            if m == 0:
                dve.wait_ge(*c.count("ln"))
                step(dve.scalar_tensor_tensor(out=g, in0=z, scalar=0.0, in1=lnp, op0=ALU.max, op1=ALU.add))
                dve.wait_ge(*c.count("exp_a"))
                step(dve.scalar_tensor_tensor(out=g, in0=g, scalar=-1.0, in1=spread(neg_a, TILES),
                                              op0=ALU.mult, op1=ALU.mult))
                step(dve.memset(S, 0.0))
            dve.wait_ge(*c.count("norm_root"))
            step(dve.reciprocal(root, root))
            for n, (t, scale) in enumerate(((qT, DH ** -0.5), (kT, 1.0))):
                dve.scalar_tensor_tensor(out=t, in0=t, scalar=scale, in1=root.rearrange(
                    "p (n h t) -> p n h t", n=2, h=HEADS)[:, n], op0=ALU.mult, op1=ALU.mult)\
                   .then_inc(c.next("unit_rows"), 1)
            dve.wait_ge(*c.count("unit_rows", 2))
            dve.tensor_tensor(g_run, spread(c.mat("upto"), HEADS), along(g[:, m, :], P),
                              ALU.mult).then_inc(c.next("g_run"), 1)
            dots(4)
            dve.wait_ge(*un.full("v_t"))
            if m == 0:
                dve.wait_ge(*c.count("beta"))
            dve.tensor_tensor(v_t, un.view("v_t"), along(beta[:, m, :], DH), ALU.mult).then_inc(un.freed("v_t"), 1)
            dve.tensor_tensor(b_diag, spread(c.mat("ident"), HEADS), along(beta[:, m, :], P),
                              ALU.mult).then_inc(c.next("b_diag"), 1)
            dots(2)
            dve.wait_ge(*un.read_out("decay"))
            step(dve.tensor_tensor(decay, decay, spread(c.mat("upto"), HEADS), ALU.mult))
            dve.wait_ge(*un.read_out("g_cols"))
            dve.tensor_tensor(q_dec, q_dec, qT, ALU.mult).then_inc(c.next("q_dec"), 1)
            dots(1)
            dve.wait_ge(*un.full("kk"))
            dve.tensor_tensor(N, un.view("kk"), decay, ALU.mult).then_inc(un.freed("kk"), 1)
            dve.wait_ge(*un.read_out("kk"))
            dve.wait_ge(*un.full("beta"))
            dve.tensor_tensor(N, N, un.view("beta"), ALU.mult).then_inc(un.freed("beta"), 1)
            dots(1)
            dve.wait_ge(*un.full("qk"))
            dve.tensor_tensor(a_qk, un.view("qk"), decay, ALU.mult).then_inc(un.freed("qk"), 1)
            dve.wait_ge(*un.read_out("beta"))
            for l in range(LEVELS):
                if l:
                    dve.wait_ge(*un.full(f"P{l - 1}"))
                dve.tensor_tensor(N_l, N, spread(c.mat(f"level{l}"), HEADS), ALU.mult).then_inc(c.next("N_l"), 1)
                if l == 0:
                    dve.wait_ge(*c.count("N_l", 1))
                    dve.tensor_tensor(Y, spread(c.mat("ident"), HEADS), N_l, ALU.subtract).then_inc(c.next("Y0"), 1)
                    dots(2)
                    dve.wait_ge(*un.read_out("P0"))
                    dve.tensor_tensor(X, spread(c.mat("ident"), HEADS), PX, ALU.subtract).then_inc(c.next("X0"), 1)
                    dve.wait_ge(*c.count("X0", 1))
                    continue
                dots(6)
                if l < LEVELS - 1:
                    dve.wait_ge(*un.full(f"X{l}"))
                    dve.tensor_tensor(X, X, un.view(f"X{l}"), ALU.subtract).then_inc(un.freed(f"X{l}"), 1)
                dots(1)
                dve.wait_ge(*un.full(f"Y{l}"))
                dve.tensor_tensor(Y, Y, un.view(f"Y{l}"), ALU.subtract).then_inc(un.freed(f"Y{l}"), 1)
                if l < LEVELS - 1:
                    dve.wait_ge(*un.read_out(f"X{l}"))
                dve.wait_ge(*un.read_out(f"Y{l}"))
            dve.wait_ge(*un.read_out("g_rows"))
            dve.wait_ge(*un.read_out("k_t"))
            step(dve.tensor_tensor(bg, beta[:, m, :], e_g[:, 0:8], ALU.mult))
            dve.tensor_tensor(kb, k_t, along(bg, DH), ALU.mult).then_inc(c.next("kb"), 1)
            dve.wait_ge(*c.count("kb"))
            dve.tensor_tensor(k_dec, k_t, along(e_g[:, 8:16], DH), ALU.mult).then_inc(c.next("k_dec"), 1)
            dots(4)
            dve.wait_ge(*un.read_out("u"))
            for ch in range(2):
                r = rows(ch)
                dots(2)
                dve.wait_ge(*un.full(f"ws.{ch}"))
                dve.tensor_tensor(v_new[r], u[r], un.view(f"ws.{ch}")[r], ALU.subtract).then_inc(un.freed(f"ws.{ch}"), 1)
                dots(2)
                dve.wait_ge(*un.full(f"o.{ch}"))
                step(dve.tensor_tensor(S, S, along(e_g[:, 16 + 8 * ch:24 + 8 * ch], DH), ALU.mult))
                dve.wait_ge(*un.full(f"s.{ch}"))
                dve.tensor_tensor(S, S, un.view(f"s.{ch}"), ALU.add).then_inc(un.freed(f"s.{ch}"), 1)
                dve.wait_ge(*un.read_out(f"s.{ch}"))
            dots(2)
            norm_gate_dve(c, dve, o, gate, 0, stat, PX, 1)
            dots(SLOTS)

        @block.tensor
        def _(pe):
            ones, ident, after = c.mat("ones"), c.mat("ident"), c.mat("after")
            if beside:
                c.product_beside(pe, 0)
            pe.wait_ge(*c.count("squares"))
            for b in range(4):
                mm = pe.matmul(c.ps[:, 4 + b, :], ones, sq[:, b * HALF:(b + 1) * HALF],
                               start=True, stop=True)
            mm.then_inc(c.next("norms"), 1)
            if beside:
                c.product_beside(pe, 1)
            pe.wait_ge(*c.count("unit_rows", 2))

            def heads(name, lhs, rhs):
                out = un.view(name)
                pe.wait_ge(*un.emptied(name))
                for h in range(HEADS):
                    mm = pe.matmul(out[:, h, :], lhs(h), rhs(h), start=True, stop=True)
                mm.then_inc(un.filled(), 1)

            def wide(name, lhs, rhs):
                out = un.view(name, 2)
                pe.wait_ge(*un.emptied(name))
                for b in range(2):
                    mm = pe.matmul(out[:, b, :], lhs, rhs[:, 4 * b:4 * b + 4, :].rearrange("p h n -> p (h n)"),
                                   start=True, stop=True)
                mm.then_inc(un.filled(), 1)

            for name, src in (("k_t", kT), ("v_t", vT)):
                pe.wait_ge(*un.emptied(name))
                for h in range(HEADS):
                    mm = pe.transpose(un.view(name)[:, h, :], src[:, h, :], ident)
                mm.then_inc(un.filled(), 1)
            pe.wait_ge(*c.count("g_run"))
            wide("decay", after, g_run)
            wide("g_cols", ones, g_run)
            pe.wait_ge(*un.emptied("g_rows"))
            for n, mat in enumerate(("upto", "after", "chunk0", "chunk1")):
                mm = pe.matmul(un.view("g_rows", 2)[:, 0, 8 * n:8 * n + 8], c.mat(mat),
                               g[:, m, :], start=True, stop=True)
            mm.then_inc(un.filled(), 1)
            heads("kk", lambda h: kT[:, h, :], lambda h: kT[:, h, :])
            pe.wait_ge(*c.count("b_diag"))
            wide("beta", ones, b_diag)
            heads("qk", lambda h: kT[:, h, :], lambda h: qT[:, h, :])
            for l in range(LEVELS):
                pe.wait_ge(*c.count("N_l", l + 1))
                if l == 1:
                    pe.wait_ge(*c.count("X0"))
                if l:
                    heads(f"P{l}", lambda h: N_l[:, h, :], lambda h: X[:, h, :])
                else:
                    pe.wait_ge(*un.emptied("P0"))
                    for h in range(HEADS):
                        mm = pe.transpose(un.view("P0")[:, h, :], N_l[:, h, :], ident)
                    mm.then_inc(un.filled(), 1)
                if beside:
                    c.product_beside(pe, 2 + 2 * l)
                elif l in (1, 2, 4, 5):
                    rows_of.sums(pe, 3)
                if l:
                    pe.wait_ge(*un.read_out(f"P{l}"))
                    if l < LEVELS - 1:
                        heads(f"X{l}", lambda h: Y[:, h, :], lambda h: PX[:, h, :])
                    heads(f"Y{l}", lambda h: PX[:, h, :], lambda h: Y[:, h, :])
                if beside:
                    c.product_beside(pe, 3 + 2 * l)
                elif l in (1, 2, 4, 5):
                    rows_of.sums(pe, 3)
            pe.wait_ge(*un.read_out(f"Y{LEVELS - 1}"))
            heads("u", lambda h: Y[:, h, :], lambda h: v_t[:, h, :])
            pe.wait_ge(*c.count("kb"))
            heads("w", lambda h: kb[:, h, :], lambda h: Y[:, h, :])
            if beside:
                c.product_beside(pe, 14)
            pe.wait_ge(*un.read_out("w"))
            pe.wait_ge(*c.count("k_dec"))
            for ch in range(2):
                r = rows(ch)
                heads(f"ws.{ch}", lambda h: wT[:, h, :], lambda h: S[:, h, :])
                if beside and ch:
                    c.product_beside(pe, 15)
                pe.wait_ge(*un.read_out(f"ws.{ch}"))
                pe.wait_ge(*un.emptied(f"o.{ch}"))
                for h in range(HEADS):
                    out = un.view(f"o.{ch}")[:, h, :]
                    pe.matmul(out, q_dec[:, h, :], S[:, h, :], start=True, stop=False)
                    mm = pe.matmul(out, a_qk[r, h, :], v_new[r, h, :], start=False, stop=True)
                mm.then_inc(un.filled(), 1)
                heads(f"s.{ch}", lambda h: k_dec[r, h, :], lambda h: v_new[r, h, :])
                pe.wait_ge(*un.read_out(f"s.{ch}"))
    un.close()
    if m == 0:
        c.loaded.base += 32
    c.end_stage()


def hgrn(c, m):
    nc, rows_of = c.nc, c.experts
    gate, f, v, qT = (c.part(m, a) for a in (GATE_B, F_B, I_B, Q_B))
    slot = lambda n: c.area(SCRATCH + D * n, HEADS, P)
    k_t, kT, span, both, a_qk, e_b, q_dec, k_dec, o, log_f, lb, lb1 = (slot(n) for n in range(12))
    squared = span
    S = slot(STATE_B)
    flat = lambda t: t.rearrange("p h n -> p (h n)")
    stat = c.small[:, 176:208]
    rows = lambda ch: slice(CHUNK * ch, CHUNK * (ch + 1))
    beside = m == 0
    names = ["k_t", "same"] + [f"{x}{l}" for l in range(LEVELS) for x in ("span", "a")]
    names += ["e_b", "to_end"] + [f"{x}.{n}" for n in range(2) for x in ("o", "s")]
    un = Units(c, names)

    rows_of.begin_stage(ROWS_BESIDE_HGRN if m else 0)
    with nc.Block() as block:
        @block.sync
        def _(sp):
            if m == 0:
                for name in ("g_a", "g_b"):
                    c.stream(sp, name)

        if m:
            @block.gpsimd
            def _(pool):
                rows_of.fetch(pool, ROWS_BESIDE_HGRN // RING)

        @block.scalar
        def _(act):
            if m == 0:
                act.wait_ge(*c.count("low_diff"))
                act.activation(lb, lb, ACT.Sigmoid).then_inc(c.next("low"), 1)
                c.read_beside(act, BESIDE_DELTA)
                act.wait_ge(*c.count("f"))
            act.activation(k_t, f, ACT.Copy, scale=-1.0, bias=1.0).then_inc(c.next("k_t"), 1)
            act.activation(log_f, f, ACT.Ln).then_inc(c.next("log_f"), 1)
            act.wait_ge(*un.full("k_t"))
            act.activation(kT, un.view("k_t"), ACT.Copy).then_inc(un.freed("k_t"), 1)
            for l in range(LEVELS):
                act.wait_ge(*un.full(f"span{l}"))
                if l:
                    act.wait_ge(*c.count("both", 2 * l))
                act.activation(span, un.view(f"span{l}"), ACT.Exp).then_inc(un.freed(f"span{l}"), 1)
                if beside:
                    c.read_beside(act, BESIDE_DELTA + l + 1)
                elif l in (3, 4):
                    rows_of.diagonals(act, 6)
            act.wait_ge(*un.full("e_b"))
            act.activation(e_b, un.view("e_b"), ACT.Exp).then_inc(un.freed("e_b"), 1)
            act.wait_ge(*un.full("to_end"))
            act.activation(k_dec, un.view("to_end"), ACT.Exp).then_inc(un.freed("to_end"), 1)
            for ch in range(2):
                r = rows(ch)
                if beside and ch:
                    c.read_beside(act, BESIDE_DELTA + LEVELS + ch)
                act.wait_ge(*un.full(f"o.{ch}"))
                act.activation(o[r], un.view(f"o.{ch}")[r], ACT.Copy).then_inc(un.freed(f"o.{ch}"), 1)
            for ch in range(2):
                act.wait_ge(*un.read_out(f"o.{ch}"))
            norm_gate_act(c, act, o, stat, squared, 1)

        @block.vector
        def _(dve):
            def step(ins):
                ins.then_inc(c.dve_chain.next(), 1)
                dve.wait_ge(*c.dve_chain.made())

            def dots(n):
                if m:
                    rows_of.dve_steps(dve, n)

            def lower_bound(tile):
                step(dve.tensor_tensor(c.part(tile, F_B), c.part(tile, F_B), lb1, ALU.mult))
                dve.tensor_tensor(c.part(tile, F_B), c.part(tile, F_B), lb, ALU.add).then_inc(c.next("f"), 1)

            if m == 0:
                dve.wait_ge(*c.ahead_loaded.count(0))
                dve.tensor_tensor(lb, c.area(LOW_0, HEADS, P), c.area(LOW_1, HEADS, P), ALU.subtract).then_inc(c.next("low_diff"), 1)
                dve.wait_ge(*c.count("low"))
                step(dve.tensor_scalar(lb1, lb, -1.0, 1.0, ALU.mult, ALU.add))
                lower_bound(0)
                dve.wait_ge(*c.count("f"))
            if m == 0:
                lower_bound(1)
                step(dve.memset(S, 0.0))
            dots(3)
            dve.wait_ge(*un.full("same"))
            dve.tensor_tensor(a_qk, un.view("same"), spread(c.mat("ident"), HEADS), ALU.mult).then_inc(un.freed("same"), 1)
            for l in range(LEVELS):
                halves = lambda t: t.rearrange("p h (b s t) -> p h b s t", s=2, t=1 << l)
                dots(2)
                dve.wait_ge(*un.read_out(f"span{l}"))
                if l:
                    dve.wait_ge(*un.full(f"a{l - 1}"))
                for side, x in ((1, qT), (0, kT)):
                    dve.tensor_tensor(halves(both)[:, :, :, side, :], halves(x)[:, :, :, side, :],
                                      halves(span)[:, :, :, side, :], ALU.mult).then_inc(c.next("both"), 1)
                dots(2)
                dve.wait_ge(*un.full(f"a{l}"))
                if l == 0:
                    dve.wait_ge(*un.read_out("same"))
                else:
                    dve.wait_ge(*un.read_out(f"a{l - 1}"))
                dve.copy_predicated(out=a_qk, mask=spread(c.masks[:, l, :], HEADS),
                                    data=un.view(f"a{l}")).then_inc(un.freed(f"a{l}"), 1)
            dots(2)
            dve.wait_ge(*un.read_out("e_b"))
            dve.tensor_tensor(q_dec, qT, e_b, ALU.mult).then_inc(c.next("q_dec_b"), 1)
            dve.wait_ge(*un.read_out("to_end"))
            dve.wait_ge(*c.count("k_t"))
            dve.tensor_tensor(k_dec, k_dec, k_t, ALU.mult).then_inc(c.next("k_dec_b"), 1)
            for ch in range(2):
                last = CHUNK * (ch + 1) - 1
                dots(3)
                dve.wait_ge(*un.full(f"o.{ch}"))
                step(dve.tensor_tensor(S, S, e_b[:, :, last:last + 1].broadcast_to([P, HEADS, DH]), ALU.mult))
                dve.wait_ge(*un.full(f"s.{ch}"))
                dve.tensor_tensor(S, S, un.view(f"s.{ch}"), ALU.add).then_inc(un.freed(f"s.{ch}"), 1)
                dve.wait_ge(*un.read_out(f"s.{ch}"))
            dots(2)
            norm_gate_dve(c, dve, o, gate, 1, stat, squared, 1)
            dots(SLOTS)

        @block.tensor
        def _(pe):
            def heads(name, lhs, rhs):
                out = un.view(name)
                pe.wait_ge(*un.emptied(name))
                for h in range(HEADS):
                    mm = pe.matmul(out[:, h, :], lhs(h), rhs(h), start=True, stop=True)
                mm.then_inc(un.filled(), 1)

            if beside:
                c.product_beside(pe, BESIDE_DELTA)
            pe.wait_ge(*c.count("k_t"))
            pe.wait_ge(*un.emptied("k_t"))
            for h in range(HEADS):
                mm = pe.transpose(un.view("k_t")[:, h, :], k_t[:, h, :], c.mat("ident"))
            mm.then_inc(un.filled(), 1)
            pe.wait_ge(*un.read_out("k_t"))
            heads("same", lambda h: kT[:, h, :], lambda h: qT[:, h, :])
            pe.wait_ge(*c.count("log_f"))
            for l in range(LEVELS):
                heads(f"span{l}", lambda h: log_f[:, h, :], lambda h: c.mat(f"span{l}"))
                if beside:
                    c.product_beside(pe, BESIDE_DELTA + l + 1)
                elif l in (3, 4):
                    rows_of.sums(pe, 3)
                pe.wait_ge(*c.count("both", 2 * (l + 1)))
                heads(f"a{l}", lambda h: both[:, h, :], lambda h: both[:, h, :])
                if l in (3, 4) and not beside:
                    rows_of.sums(pe, 3)
            heads("e_b", lambda h: log_f[:, h, :], lambda h: c.mat("upto"))
            pe.wait_ge(*un.emptied("to_end"))
            for b in range(2):
                mm = pe.matmul(un.view("to_end", 2)[:, b, :], c.mat("after"),
                               flat(log_f)[:, b * HALF:(b + 1) * HALF], start=True, stop=True)
            mm.then_inc(un.filled(), 1)
            for ch in range(2):
                r = rows(ch)
                if beside and ch:
                    c.product_beside(pe, BESIDE_DELTA + LEVELS + ch)
                if ch == 0:
                    pe.wait_ge(*c.count("q_dec_b"))
                    pe.wait_ge(*c.count("k_dec_b"))
                pe.wait_ge(*un.emptied(f"o.{ch}"))
                for h in range(HEADS):
                    out = un.view(f"o.{ch}")[:, h, :]
                    pe.matmul(out, q_dec[:, h, :], S[:, h, :], start=True, stop=False)
                    mm = pe.matmul(out, a_qk[r, h, :], v[r, h, :], start=False, stop=True)
                mm.then_inc(un.filled(), 1)
                heads(f"s.{ch}", lambda h: k_dec[r, h, :], lambda h: v[r, h, :])
                pe.wait_ge(*un.read_out(f"s.{ch}"))
    un.close()
    c.end_stage()


def branches(c, m):
    nc, rows_of = c.nc, c.experts
    o_a, o_b, g_a, g_b = (c.row(m, a) for a in (GATE_A, GATE_B, MIX_A, MIX_B))
    aT, bT, mixT = (c.area(SCRATCH + D * n, KC, P) for n in range(3))
    uses = list(c.bank_uses)
    names = [f"{x}.{m}" for x in ("branch_a", "branch_b", "w_out")]
    first = FIRST[names[0]]
    rows_of.begin_stage(ROWS_BESIDE_BRANCHES if m else 0)
    with nc.Block() as block:
        @block.sync
        def _(sp):
            c.load_ahead(sp, c.area(NORM_G, D), c.dram["rows"][ROW["norm2"]])
            for name in names:
                c.stream(sp, name)

        if m:
            @block.gpsimd
            def _(pool):
                rows_of.fetch(pool, ROWS_BESIDE_BRANCHES // RING)

        @block.tensor
        def _(pe):
            turn_tile(c, pe, o_a)
            if m:
                rows_of.sums(pe, 3)
            wait_turned_tile_read(c, pe)
            turn_tile(c, pe, o_b)
            c.products_of_tile(pe, names[0], aT, channel_major=False)
            if m:
                rows_of.sums(pe, 3)
            wait_turned_tile_read(c, pe)
            c.products_of_tile(pe, names[1], bT, channel_major=False)
            if m:
                rows_of.sums(pe, 3)
            pe.wait_ge(*c.count("mix"))
            turn_tile(c, pe, g_a)
            if m:
                rows_of.sums(pe, 3)
            wait_turned_tile_read(c, pe)
            c.products_of_tile(pe, names[2], mixT, channel_major=False)
            if m:
                rows_of.sums(pe, SLOTS)

        @block.scalar
        def _(act):
            for n, out in enumerate((aT, bT, mixT)):
                if m:
                    rows_of.diagonals(act, 6 if n == 0 else 3)
                read_turned_tile(c, act, out, n)
            if m:
                rows_of.diagonals(act, SLOTS)

        @block.vector
        def _(dve):
            if m:
                rows_of.dve_steps(dve, 2)
            for n, gate in enumerate((g_a, g_b)):
                for q in range(2):
                    dve.wait_ge(c.panel_done.sem, first + 2 * n + q + 1)
                    bank = 2 * ((first + q) % 2)
                    at = gate[:, q * HALF:(q + 1) * HALF]
                    dve.tensor_tensor(at, at, c.ps[:, bank, :], ALU.mult).then_inc(c.bank_read[bank].sem, 1)
                if m:
                    rows_of.dve_steps(dve, 1)
            for b in (0, 2):
                dve.wait_ge(c.bank_read[b].sem, uses[b] + 4)
            dve.tensor_tensor(g_a, g_a, g_b, ALU.add).then_inc(c.next("mix"), 1)
            if m:
                rows_of.dve_steps(dve, 1)
            for q in range(2):
                dve.wait_ge(c.panel_done.sem, first + 4 + q + 1)
                bank = 2 * ((first + q) % 2)
                at = c.x[:, m, q * HALF:(q + 1) * HALF]
                dve.tensor_tensor(at, at, c.ps[:, bank, :], ALU.add).then_inc(c.bank_read[bank].sem, 1)
            if m:
                rows_of.dve_steps(dve, SLOTS)
    c.turned.base += 6
    c.end_stage()


def norm_of_tile(c, m):
    nc = c.nc
    g, squared = c.area(NORM_G, D), c.area(SCRATCH, D)
    out, x = c.row(m, H2), c.x[:, m, :]
    sm = c.small[:, 300:304]
    with nc.Block() as block:
        @block.scalar
        def _(act):
            act.activation(squared, x, ACT.Square, accum_out=sm[:, 0:1]).then_inc(c.next("square"), 1)
            act.wait_ge(*c.count("mean"))
            act.activation(sm[:, 2:3], sm[:, 1:2], ACT.Sqrt).then_inc(c.next("root"), 1)
            read_turned_tile(c, act, c.xT[:, :, m * P:(m + 1) * P], 0)

        @block.vector
        def _(dve):
            dve.wait_ge(*c.count("square"))
            dve.tensor_scalar(sm[:, 1:2], sm[:, 0:1], 1.0 / D, EPS, ALU.mult, ALU.add).then_inc(c.next("mean"), 1)
            dve.wait_ge(*c.count("root"))
            dve.reciprocal(sm[:, 3:4], sm[:, 2:3]).then_inc(c.dve_chain.next(), 1)
            dve.wait_ge(*c.dve_chain.made())
            dve.wait_ge(*c.ahead_loaded.count(0))
            dve.scalar_tensor_tensor(out=out, in0=x, scalar=sm[:, 3:4], in1=g,
                                     op0=ALU.mult, op1=ALU.mult).then_inc(c.next("normed"), 1)

        @block.tensor
        def _(pe):
            pe.wait_ge(*c.count("normed"))
            turn_tile(c, pe, out)
    c.turned.base += 2
    c.end_stage()


def choose_experts(c, m):
    nc, rows_of = c.nc, c.experts
    slot = lambda n, *shape: c.area(SCRATCH + D * n, *shape)
    qT, keys = slot(0, 2 * P_HEADS, P), slot(2, 2 * P_HEADS, N_KEYS)
    scores, left = slot(4, 2 * P_HEADS, N_KEYS), slot(6, 2 * P_HEADS, N_KEYS)
    cand, cand_left = slot(8, P_HEADS, TOPK * TOPK), slot(4, P_HEADS, TOPK * TOPK)
    hot = slot(6, P_HEADS, TOPK, TOPK)
    tops = SCRATCH + D * 10
    top, best = c.area(tops, 2 * P_HEADS, TOPK), c.area(tops + 512, P_HEADS, TOPK)
    top_at = c.area(tops + 256, 2 * P_HEADS, TOPK)
    best_at = c.area(tops + 640, P_HEADS, TOPK)
    half_at = [c.area(tops + 768 + 128 * n, P_HEADS, TOPK) for n in range(2)]
    named = [c.area(tops + 1024 + 128 * n, P_HEADS, TOPK) for n in range(2)]
    top_key = c.area(tops + 1280, 2 * P_HEADS, TOPK)
    iota, total = c.area(tops + 1536, TOPK), c.area(tops + 1552, P_HEADS)
    experts = c.area(KEPT, TILES, SLOTS)[:, m]
    gates = c.area(KEPT + 256, TILES, P_HEADS, TOPK)[:, m]
    pq = f"w_pq.{m}"
    rows_of.begin_stage(ROWS_BESIDE_CHOICE if m else 0)
    with nc.Block() as block:
        @block.sync
        def _(sp):
            sp.dma_start(keys, c.dram["sub_keys"]).then_inc(c.loaded.sem, 16)
            sp.dma_start(iota, c.dram["iota"]).then_inc(c.loaded.sem, 16)
            c.stream(sp, pq)

        if m:
            @block.gpsimd
            def _(pool):
                rows_of.fetch(pool, ROWS_BESIDE_CHOICE // RING)

        @block.tensor
        def _(pe):
            c.products_of_tile(pe, pq, c.xT[:, :, m * P:(m + 1) * P], channel_major=True,
                               after=(lambda: rows_of.sums(pe, 3)) if m else None)
            pe.wait_ge(*c.loaded.count(32))
            for b in (0, 2):
                pe.wait_ge(c.bank_read[b].sem, c.bank_uses[b])
            for n in range(2 * P_HEADS):
                out = c.ps[:, 4 + n // 4, (n % 4) * P:(n % 4 + 1) * P]
                mm = pe.matmul(out, qT[:, n, :], keys[:, n, :], start=True, stop=True)
            mm.then_inc(c.next("scores"), 1)
            if m:
                rows_of.sums(pe, SLOTS)

        @block.scalar
        def _(act):
            for q in range(COUNT[pq]):
                if m:
                    rows_of.diagonals(act, 3)
                act.wait_ge(c.panel_done.sem, FIRST[pq] + q + 1)
                bank = 2 * ((FIRST[pq] + q) % 2)
                act.activation(qT[:, 4 * q:4 * q + 4, :], c.ps[:, bank, :].rearrange("p (k t) -> p k t", k=4),
                               ACT.Copy).then_inc(c.bank_read[bank].sem, 1)
            act.wait_ge(*c.count("scores"))
            act.activation(scores.rearrange("p n k -> p (n k)"), c.ps[:, 4:8, :].rearrange("p b n -> p (b n)"),
                           ACT.Copy).then_inc(c.next("scores_read"), 1)
            if m:
                rows_of.diagonals(act, SLOTS)
            act.wait_ge(*c.count("best_less_max"))
            act.activation(gates, gates, ACT.Exp).then_inc(c.next("gate_exp"), 1)

        @block.vector
        def _(dve):
            chain = c.dve_chain

            def step(ins):
                ins.then_inc(c.dve_chain.next(), 1)
                dve.wait_ge(*c.dve_chain.made())

            def adds(n):
                if m:
                    rows_of.dve_steps(dve, n)

            def top16(values, left, top, at, groups):
                at = at.bitcast(U32)
                for g in range(groups):
                    dve.max(top[:, g, 0:8], values[:, g, :]).then_inc(chain.next(), 1)
                adds(1)
                dve.wait_ge(*chain.made())
                for g in range(groups):
                    dve.max_index(at[:, g, 0:8], top[:, g, 0:8], values[:, g, :]).then_inc(chain.next(), 1)
                    dve.match_replace(left[:, g, :], top[:, g, 0:8], values[:, g, :], LOWEST).then_inc(chain.next(), 1)
                    if g % 8 == 7:
                        adds(1)
                dve.wait_ge(*chain.made())
                for g in range(groups):
                    dve.max(top[:, g, 8:16], left[:, g, :]).then_inc(chain.next(), 1)
                adds(1)
                dve.wait_ge(*chain.made())
                for g in range(groups):
                    dve.max_index(at[:, g, 8:16], top[:, g, 8:16], left[:, g, :]).then_inc(chain.next(), 1)
                adds(1)
                dve.wait_ge(*chain.made())

            adds(3)
            dve.wait_ge(*c.loaded.count(32))
            dve.wait_ge(*c.count("scores_read"))
            top16(scores, left, top, top_at, 2 * P_HEADS)
            step(dve.tensor_copy(top_key, top_at.bitcast(U32)))
            pairs_of = top.rearrange("p (h s) k -> p h s k", s=2)
            shape = [P, P_HEADS, TOPK, TOPK]
            first = pairs_of[:, :, 0, :].unsqueeze(3).broadcast_to(shape)
            second = pairs_of[:, :, 1, :].unsqueeze(2).broadcast_to(shape)
            step(dve.tensor_tensor(cand.rearrange("p h (a b) -> p h a b", a=TOPK), first, second, ALU.add))
            top16(cand, cand_left, best, best_at, P_HEADS)
            dve.tensor_tensor(gates, best, best[:, :, 0:1].broadcast_to([P, P_HEADS, TOPK]),
                              ALU.subtract).then_inc(c.next("best_less_max"), 1)
            where = best_at.bitcast(U32)
            a, b = (x.bitcast(U32) for x in named)
            step(dve.tensor_scalar(a, where, 4, None, ALU.logical_shift_right))
            step(dve.tensor_scalar(b, where, TOPK - 1, None, ALU.bitwise_and))
            keys_of = top_key.rearrange("p (h s) k -> p h s k", s=2)
            for n, x in enumerate((a, b)):
                step(dve.tensor_copy(half_at[n], x))
            for n in range(2):
                spot = half_at[n].unsqueeze(3).broadcast_to(shape)
                lists = keys_of[:, :, n, :].unsqueeze(2).broadcast_to(shape)
                step(dve.tensor_tensor(hot, spot, iota.unsqueeze(1).unsqueeze(1).broadcast_to(shape),
                                       ALU.is_equal))
                adds(1)
                step(dve.tensor_tensor(hot, hot, lists, ALU.mult))
                step(dve.tensor_reduce(named[n], hot, AX_X, ALU.add))
                adds(1)
            step(dve.scalar_tensor_tensor(out=named[0], in0=named[0], scalar=float(N_KEYS), in1=named[1],
                                          op0=ALU.mult, op1=ALU.add))
            step(dve.tensor_copy(experts.bitcast(U32), named[0].rearrange("p h k -> p (h k)")))
            adds(SLOTS)
            dve.wait_ge(*c.count("gate_exp"))
            step(dve.tensor_reduce(total, gates, AX_X, ALU.add))
            step(dve.reciprocal(total, total))
            step(dve.tensor_tensor(gates, gates, along(total, TOPK), ALU.mult))
    c.loaded.base += 32
    c.end_stage()



def pooling(c):
    nc = c.nc
    mats = c.area(POOL_AT, TILES * len(WINDOWS), T)
    w = c.area(POOL_AT + 8 * T, 2 * len(WINDOWS), 2 * P)
    scale, pooled = c.area(POOL_AT + 8 * T + 16 * P, D), c.area(6 * D, KC, T)
    mixed = c.area(8 * D, TILES, D)
    with nc.Block() as block:
        @block.sync
        def _(sp):
            c.load_norm_rows(sp, "mix0")

        @block.tensor
        def _(pe):
            pe.wait_ge(c.pool_loaded.sem, 48)
            for n in range(KC):
                for m in range(TILES):
                    mm = pe.matmul(c.ps[:, n // 2, (n % 2) * T:(n % 2 + 1) * T], c.x[:, m, n * P:(n + 1) * P],
                                   mats[:, m * len(WINDOWS) + n // 2, :], start=(m == 0), stop=(m == TILES - 1))
                if n % 2:
                    mm.then_inc(c.next("pooled"), 1)
            for m in range(TILES):
                for g in range(len(WINDOWS)):
                    pe.wait_ge(*c.count("pooled_read", g + 1))
                    for k in range(2):
                        mm = pe.matmul(c.ps[:, 4 + 2 * m + g // 2, (g % 2) * T:(g % 2 + 1) * T],
                                       pooled[:, 2 * g + k, m * P:(m + 1) * P], w[:, 2 * g + k, :],
                                       start=(k == 0), stop=(k == 1))
                mm.then_inc(c.next("mixed"), 1)

        @block.scalar
        def _(act):
            for g in range(len(WINDOWS)):
                act.wait_ge(*c.count("pooled", g + 1))
                act.activation(pooled[:, 2 * g:2 * g + 2, :].rearrange("p k t -> p (k t)"),
                                      c.ps[:, g, :], ACT.Copy).then_inc(c.next("pooled_read"), 1)

        @block.vector
        def _(dve):
            dve.wait_ge(c.pool_loaded.sem, 48)
            for m in range(TILES):
                dve.wait_ge(*c.count("mixed", m + 1))
                out = c.ps[:, 4 + 2 * m:6 + 2 * m, :].rearrange("p b n -> p (b n)")
                dve.tensor_tensor(mixed[:, m, :], out, scale, ALU.mult).then_inc(c.dve_chain.next(), 1)
                dve.wait_ge(*c.dve_chain.made())
                dve.scalar_tensor_tensor(out=c.x[:, m, :], in0=c.x[:, m, :], scalar=ALPHA, in1=mixed[:, m, :],
                                         op0=ALU.mult, op1=ALU.add, accum_out=c.row_sums[:, m, 0:1]).then_inc(c.dve_chain.next(), 1)
                dve.wait_ge(*c.dve_chain.made())
    c.end_stage()


def feed_forward(c, i):
    nc = c.nc
    up, down = f"ff{i}", f"down{i}"
    hidden = c.area(0, FF_T, T)
    silu = c.area(FF_T * T, 2, HALF)
    uses, first = list(c.bank_uses), FIRST[up]
    with nc.Block() as block:
        @block.sync
        def _(sp):
            c.load_norm_rows(sp, f"ffn{i}")
            c.stream(sp, up)
            c.stream(sp, down)

        @block.tensor
        def _(pe):
            c.products(pe, up, c.xT, channel_major=True)
            for n in range(FF_T):
                if n % 4 == 0:
                    slot = c.wait_panel(pe, down, n // 8, n // 4 % 2)
                if n % 2 == 0:
                    q = n // 2
                    b = 2 * ((first + q) % 2) + 1
                    pe.wait_ge(c.bank_read[b].sem, uses[b] + q // 2 + 1)
                w = c.panels[:, slot, :].rearrange("p (k n) -> p k n", k=4)
                for m in range(TILES):
                    for half in range(2):
                        mm = pe.matmul(c.ps[:, 4 + 2 * m + half, :], hidden[:, n, m * P:(m + 1) * P],
                                       w[:, n % 4, half * HALF:(half + 1) * HALF],
                                       start=(n == 0), stop=(n == FF_T - 1))
                if n % 4 == 3 or n == FF_T - 1:
                    mm.then_inc(c.panel_done.sem, 1)

        @block.scalar
        def _(act):
            def read(i, par, j, bank):
                act.wait_ge(c.bank_read[bank + 1].sem, i + uses[bank + 1])
                return act.activation(silu[:, bank // 2, :], c.ps[:, bank, :], ACT.Silu)
            c.evacuate(act, up, read, halves=(0,))

        @block.vector
        def _(dve):
            def read(i, par, j, bank):
                dve.wait_ge(c.bank_read[bank - 1].sem, i + (uses[bank - 1] + 1))
                out = hidden[:, bass.ds(4 * i + 2 * par, 2), :].rearrange("p k t -> p (k t)")
                return dve.tensor_tensor(out, silu[:, bank // 2, :], c.ps[:, bank, :], ALU.mult)
            c.evacuate(dve, up, read, halves=(1,))
            dve.wait_ge(c.panel_done.sem, FIRST[down] + COUNT[down])
            for m in range(TILES):
                out = c.ps[:, 4 + 2 * m:6 + 2 * m, :].rearrange("p b n -> p (b n)")
                dve.scalar_tensor_tensor(out=c.x[:, m, :], in0=c.x[:, m, :], scalar=ALPHA,
                                         in1=out, op0=ALU.mult, op1=ALU.add,
                                         accum_out=c.row_sums[:, m, 0:1]).then_inc(c.dve_chain.next(), 1)
    c.end_stage()


def attention(c):
    nc = c.nc
    qkT = c.area(0, 2 * HEADS, T)
    v = c.area(4 * D, TILES, HEADS, DH)
    bias = c.area(6 * D, HEADS, T)
    s = [c.area(8 * D, 2 * HEADS, P), c.area(18 * D, 2 * HEADS, T)]
    aT = c.area(12 * D, HEADS * TILES, P)
    o = c.area(14 * D, TILES, HEADS, DH)
    squared = c.area(16 * D, HEADS, DH)
    lam_p, unseen = c.area(17 * D, 4, HEAD_DIM), c.area(17 * D + 256, P)
    lam_prod = c.area(17 * D + 384, 2, HEAD_DIM)
    sm = c.small
    lam, stat = sm[:, 32:36], sm[:, 64:96]
    top, total = ([sm[:, at + 16 * m:at + 16 * m + 16] for m in range(TILES)] for at in (0, 96))
    names = [f"s0.{n}" for n in range(2)] + [f"s1.{n}" for n in range(4)] + ["a0.0", "o0", "a1.0", "a1.1", "o1"]
    un = Units(c, names)
    flat = lambda t: t.rearrange("p h n -> p (h n)")
    with nc.Block() as block:
        @block.sync
        def _(sp):
            sp.dma_start(bias, c.dram["rel_bias"]).then_inc(c.loaded.sem, 16)
            sp.dma_start(unseen, c.dram["not_seen"]).then_inc(c.loaded.sem, 16)
            sp.dma_start(lam_p, c.dram["lam_p"]).then_inc(c.loaded.sem, 16)
            c.load_norm_rows(sp, "mix1")
            for name in ("qk", "v", "w_o"):
                c.stream(sp, name)

        @block.tensor
        def _(pe):
            c.products(pe, "qk", c.xT, channel_major=True)
            for b in range(4):
                pe.wait_ge(c.bank_read[b].sem, c.bank_uses[b])
            for m in range(TILES):
                keys = P * (m + 1)
                per = 8 // (m + 1)
                for n in range(2 * HEADS // per):
                    pe.wait_ge(*un.emptied(f"s{m}.{n}"))
                    out = un.view(f"s{m}.{n}", per).rearrange("p (s k) n -> p s k n", s=2)
                    for k in range(per):
                        h, half = divmod(n * per + k, 2)
                        r = slice(HEAD_DIM * half, HEAD_DIM * (half + 1))
                        mm = pe.matmul(out[:, half, k // 2, :], qkT[r, h, m * P:(m + 1) * P], qkT[r, HEADS + h, 0:keys],
                                       start=True, stop=True)
                    mm.then_inc(un.filled(), 1)
            c.products(pe, "v", c.xT, channel_major=False)
            for b in range(4):
                pe.wait_ge(c.bank_read[b].sem, c.bank_uses[b])
            for m in range(TILES):
                pe.wait_ge(*c.count("a", m + 1))
                for kt in range(m + 1):
                    pe.wait_ge(*un.emptied(f"a{m}.{kt}"))
                    for h in range(HEADS):
                        at = s[m][:, 2 * h, kt * P:(kt + 1) * P]
                        mm = pe.transpose(un.view(f"a{m}.{kt}")[:, h, :], at, c.mat("ident"))
                    mm.then_inc(un.filled(), 1)
                for kt in range(m + 1):
                    pe.wait_ge(*un.read_out(f"a{m}.{kt}"))
                pe.wait_ge(*un.emptied(f"o{m}"))
                for h in range(HEADS):
                    for kt in range(m + 1):
                        mm = pe.matmul(un.view(f"o{m}")[:, h, :], aT[:, kt * HEADS + h, :], v[:, kt, h, :],
                                       start=(kt == 0), stop=(kt == m))
                mm.then_inc(un.filled(), 1)
            pe.wait_ge(*c.count("o_normed", TILES))
            turn(c, pe, o.rearrange("p m h n -> p m (h n)"))
            wait_turned_read(c, pe)
            c.products(pe, "w_o", c.xT, channel_major=False)

        @block.scalar
        def _(act):
            def read_qk(i, par, j, bank):
                return act.activation(qkT[:, bass.ds(8 * i + 4 * par + 2 * j, 2), :],
                                      c.ps[:, bank, :].rearrange("p (k t) -> p k t", k=2), ACT.Copy)
            c.evacuate(act, "qk", read_qk)

            act.wait_ge(*c.count("lam_sums"))
            act.activation(lam[:, 2:4], lam[:, 0:2], ACT.Exp).then_inc(c.next("lam_exp"), 1)
            for m in range(TILES):
                act.wait_ge(*c.count("s_less_top", m + 1))
                act.activation(s[m], s[m], ACT.Exp).then_inc(c.next("p"), 1)
                for j in range(2):
                    done, at = (c.half_done, HALF_AT["v"]) if j == 0 else (c.panel_done, FIRST["v"])
                    act.wait_ge(done.sem, at + m + 1)
                    bank = 2 * ((FIRST["v"] + m) % 2) + j
                    act.activation(flat(v[:, j, 4 * m:4 * m + 4, :]), c.ps[:, bank, :], ACT.Copy)\
                       .then_inc(c.bank_read[bank].sem, 1)
            for m in range(TILES):
                for kt in range(m + 1):
                    act.wait_ge(*un.full(f"a{m}.{kt}"))
                    act.activation(aT[:, kt * HEADS:(kt + 1) * HEADS, :], un.view(f"a{m}.{kt}"), ACT.Copy)\
                       .then_inc(un.freed(f"a{m}.{kt}"), 1)
                act.wait_ge(*un.full(f"o{m}"))
                act.activation(o[:, m], un.view(f"o{m}"), ACT.Copy).then_inc(un.freed(f"o{m}"), 1)
            for m in range(TILES):
                act.wait_ge(*un.read_out(f"o{m}"))
                norm_gate_act(c, act, o[:, m], stat, squared, m + 1)
            read_turned(c, act, c.xT, 0)

        @block.vector
        def _(dve):
            def step(ins):
                ins.then_inc(c.dve_chain.next(), 1)
                dve.wait_ge(*c.dve_chain.made())

            dve.wait_ge(*c.loaded.count(48))
            step(dve.tensor_tensor(bias[:, :, P:T], bias[:, :, P:T], spread(unseen, HEADS), ALU.add))
            both = lam_p.rearrange("p (a b) n -> p a b n", b=2)
            step(dve.tensor_tensor(lam_prod, both[:, :, 0, :], both[:, :, 1, :], ALU.mult))
            dve.tensor_reduce(lam[:, 0:2], lam_prod, AX_X, ALU.add).then_inc(c.next("lam_sums"), 1)
            dve.wait_ge(*c.count("lam_exp"))
            step(dve.tensor_tensor(lam[:, 0:1], lam[:, 3:4], lam[:, 2:3], ALU.subtract))
            step(dve.tensor_scalar(lam[:, 0:1], lam[:, 0:1], -LAMBDA_INIT, None, ALU.add))
            for m in range(TILES):
                keys = P * (m + 1)
                per = 8 // (m + 1)
                for n in range(2 * HEADS // per):
                    dve.wait_ge(*un.full(f"s{m}.{n}"))
                    out = un.view(f"s{m}.{n}", per).rearrange("p (s k) n -> p s k n", s=2)
                    for k in range(per // 2):
                        h = n * per // 2 + k
                        ins = dve.scalar_tensor_tensor(
                            out=s[m][:, 2 * h:2 * h + 2, :], in0=out[:, :, k, :], scalar=HEAD_DIM ** -0.5,
                            in1=spread(bias[:, h, T - keys:T], 2), op0=ALU.mult, op1=ALU.add)
                    ins.then_inc(un.freed(f"s{m}.{n}"), 1)
                for n in range(2 * HEADS // per)[-2:]:
                    dve.wait_ge(*un.read_out(f"s{m}.{n}"))
                step(dve.tensor_reduce(top[m], s[m], AX_X, ALU.max))
                dve.tensor_tensor(s[m], s[m], along(top[m], keys), ALU.subtract).then_inc(c.next("s_less_top"), 1)
            for m in range(TILES):
                dve.wait_ge(*c.count("p", m + 1))
                step(dve.tensor_reduce(total[m], s[m], AX_X, ALU.add))
                step(dve.reciprocal(total[m], total[m]))
                second = total[m].rearrange("p (h s) -> p h s", s=2)[:, :, 1]
                step(dve.tensor_scalar(second, second, lam[:, 0:1], None, ALU.mult))
                step(dve.tensor_tensor(s[m], s[m], along(total[m], P * (m + 1)), ALU.mult))
                by_head = s[m].rearrange("p (h s) k -> p h s k", s=2)
                dve.tensor_tensor(by_head[:, :, 0, :], by_head[:, :, 0, :], by_head[:, :, 1, :],
                                  ALU.add).then_inc(c.next("a"), 1)
            for m in range(TILES):
                norm_gate_dve(c, dve, o[:, m], None, 2, stat, squared, m + 1, eps=LN_EPS)
                dve.tensor_scalar(o[:, m], o[:, m], 1.0 - LAMBDA_INIT, None, ALU.mult).then_inc(c.next("o_normed"), 1)

            def add(i, par, j, bank):
                q = 2 * i + par
                at = c.x[:, j, q * HALF:(q + 1) * HALF]
                return dve.scalar_tensor_tensor(out=at, in0=at, scalar=ALPHA, in1=c.ps[:, bank, :], op0=ALU.mult,
                                                op1=ALU.add, accum_out=c.row_sums[:, j, q:q + 1])
            c.evacuate(dve, "w_o", add)
    un.close()
    c.turned.base += 4
    c.loaded.base += 48
    c.end_stage()



def build(nc, dram, out):
    with ExitStack() as ctx:
        c = Core(nc, ctx, dram)
        c.experts = Experts(c, ctx)
        rms_norm(c, first=True)
        project(c)
        for m in range(TILES):
            delta_rule(c, m)
            hgrn(c, m)
            branches(c, m)
            norm_of_tile(c, m)
            choose_experts(c, m)
        sum_experts(c)
        rms_norm(c)
        pooling(c)
        layer_norm(c, parts=1)
        feed_forward(c, 0)
        layer_norm(c, parts=1)
        attention(c)
        layer_norm(c, parts=2)
        feed_forward(c, 1)
        layer_norm(c, parts=1, store=out)


def panel_columns(w):
    k, n = w.shape
    return w.reshape(k // P, P, n // HALF, HALF).transpose(2, 1, 0, 3).reshape(n // HALF, P, PANEL)


def laid_out(inputs):
    a = {n: np.asarray(v) for n, v in inputs.items()}
    w_in = a["w_in"][0]
    at = np.cumsum([0, D, D, D, HEADS, HEADS, D, D, D, D, D, D, D])
    q, k, v, beta, alpha, a_gate, b_f, b_i, b_q, b_gate, g_a, g_b = (slice(x, y) for x, y in zip(at[:-1], at[1:]))
    wall = [panel_columns(w_in[:, s]) for s in (q, k, v, a_gate, b_f, b_i, b_q, b_gate, g_a, g_b)]
    wall += [panel_columns(a[n][0]) for n in ("w_branch_a", "w_branch_b", "w_out", "w_pq")]

    def feed_forward(i):
        gate, up, down = (a[n][i] for n in ("w_gate_2", "w_up_2", "w_down_2"))
        both = np.stack([gate.reshape(D, FF_PANELS, 256), up.reshape(D, FF_PANELS, 256)], 2)
        padded = np.zeros((DOWN_PANELS * 4 * P, D), np.float32)
        padded[:D_FF] = down
        return [panel_columns(both.reshape(D, FF_PANELS * HALF)),
                padded.reshape(DOWN_PANELS, 4, P, D).transpose(0, 2, 1, 3).reshape(DOWN_PANELS, P, PANEL)]

    wall += feed_forward(0)
    wall += [panel_columns(a["w_qkv_2"][0]), panel_columns(a["w_o_2"][0])]
    wall += feed_forward(1)
    wall = np.concatenate(wall, 0)
    assert wall.shape[0] == WALL_PANELS
    on_all = lambda v: np.broadcast_to(v, (P,) + v.shape)
    rows = [a["b_lower_bound"][0], a["b_lower_bound"][1], a["norm2"][0], a["final_norm"], a["pool_scale_2"][0]]
    for i in range(2):
        rows += [a["ln_mix_g_2"][i], a["ln_mix_b_2"][i], a["ln_ffn_g_2"][i], a["ln_ffn_b_2"][i]]
    mats = constant_matrices()
    q_, k_ = np.meshgrid(np.arange(P), np.arange(T), indexing="ij")
    rel = P + q_ - k_
    table = a["rel_table_2"][rel_bucket(np.maximum(rel, 0))]
    return {
        "x": a["x"][0].reshape(TILES, P, D),
        "wall": wall,
        "mats": mats,
        "masks": (mats[:, MAT["level0"]:] > 0).astype(np.int32),
        "norm1": on_all(a["norm1"][0]),
        "onorms": np.stack([on_all(a["a_onorm"][0]), on_all(a["b_onorm"][0]), on_all(a["subln_g_2"][0])], 1),
        "w_bt": w_in[:, 3 * D:3 * D + 16].reshape(KC, P, 16).transpose(1, 0, 2),
        "w_conv": a["conv_a"][0].T.reshape(3 * HEADS, P, CONV_W).transpose(1, 0, 2),
        "a_log": on_all(a["a_log"][0]),
        "dt_bias": on_all(a["dt_bias"][0]),
        "rows": np.stack([on_all(r) for r in rows]),
        "sub_keys": a["sub_keys"][0].transpose(3, 1, 0, 2).reshape(P, 2 * P_HEADS, N_KEYS),
        "expert_u": a["expert_u"][0],
        "expert_v": a["expert_v"][0],
        "pool_m": pool_matrices(),
        "pool_w": a["pool_w_2"][0].reshape(4, 2, P, 256).transpose(2, 0, 1, 3),
        "rel_bias": table.transpose(0, 2, 1),
        "not_seen": np.where(rel[:, P:] < 0, MASKED, 0.0).astype(np.float32),
        "lam_p": on_all(a["lam_p_2"][0]),
        "iota": on_all(np.arange(TOPK, dtype=np.float32)),
    }


def kernel(**inputs):
    import concourse.bacc as bacc
    from concourse.bass_utils import run_bass_kernel_spmd

    nc = bacc.Bacc("TRN2", target_bir_lowering=False, num_devices=1)
    arrays = {n: np.ascontiguousarray(v) for n, v in laid_out(inputs).items()}
    dram = {n: nc.dram_tensor("in_" + n, v.shape, mybir.dt.from_np(v.dtype), kind="ExternalInput").ap()
            for n, v in arrays.items()}
    out = nc.dram_tensor("out", (TILES, P, D), F32, kind="ExternalOutput").ap()
    build(nc, dram, out)
    result = run_bass_kernel_spmd(nc, [{"in_" + n: v for n, v in arrays.items()}], core_ids=[0])
    return result.results[0]["out"].reshape(1, T, D)
```
